# Optimizing a Trainium2 kernel written in Bass

```python
import math
import jax, jax.numpy as jnp
from jax import lax
import numpy as np
import jax
import jax.numpy as jnp

D_MODEL = 1024
BATCH = 1
SEQ = 256
DEPTH = 2

CHUNK = 64
Q_BLOCK = 128
N_GROUPS = 4
GROUP_WIDTH = D_MODEL // N_GROUPS
D_MIX = N_GROUPS * GROUP_WIDTH
HEAD_DIM = 64
N_HEADS_G = GROUP_WIDTH // HEAD_DIM
DIFF_D = HEAD_DIM // 2
Q_LORA = 256
KV_LORA = 128
QK_NOPE = 64
QK_ROPE = 32
V_HEAD = HEAD_DIM
ROPE_THETA = 10000.0
IDX_HEADS = 8
IDX_DIM = 32
TOPK_MAX = 256
BAND_CHUNKS = 8
REL_CLIP = 128
D_FF = 2816
N_EXPERTS = 8
TOP_K = 2
D_FF_EXPERT = 3584
N_DENSE = (DEPTH + 1) // 2
N_MOE = DEPTH // 2
EPS = 1e-6

IN_LAYOUT = (
    ('a_q', N_HEADS_G * 2 * DIFF_D), ('a_k', N_HEADS_G * 2 * DIFF_D), ('a_v', N_HEADS_G * 2 * DIFF_D),
    ('b_qd', Q_LORA), ('b_kvd', KV_LORA), ('b_kr', QK_ROPE),
    ('c_q', GROUP_WIDTH), ('c_k', GROUP_WIDTH), ('c_v', GROUP_WIDTH),
    ('c_qi', IDX_HEADS * IDX_DIM), ('c_ki', IDX_DIM), ('c_wi', IDX_HEADS),
    ('d_q', GROUP_WIDTH), ('d_k', GROUP_WIDTH), ('d_v', GROUP_WIDTH),
)
D_IN = int(sum(w for _, w in IN_LAYOUT))
IN_SPLITS = tuple(int(v) for v in np.cumsum([w for _, w in IN_LAYOUT])[:-1])


def rmsnorm(x, g):
    xf = x.astype(jnp.float32)
    y = xf * lax.rsqrt(jnp.mean(xf * xf, axis=-1, keepdims=True) + EPS)
    return (y * g.astype(jnp.float32)).astype(x.dtype)

def adaln(x, g, shift, scale):
    return rmsnorm(x, g) * (1 + scale[:, None, :]) + shift[:, None, :]

def alibi_slopes(n):
    return 2.0 ** (-8.0 * jnp.arange(1, n + 1, dtype=jnp.float32) / n)

def rope_tables(s):
    inv = ROPE_THETA ** (-jnp.arange(0, QK_ROPE, 2, dtype=jnp.float32) / QK_ROPE)
    ang = jnp.arange(s, dtype=jnp.float32)[:, None] * inv[None, :]
    return jnp.cos(ang), jnp.sin(ang)

def apply_rope(x, cos, sin):
    x1, x2 = jnp.split(x, 2, axis=-1)
    cs = cos[None, :, None, :].astype(x.dtype)
    sn = sin[None, :, None, :].astype(x.dtype)
    return jnp.concatenate([x1 * cs - x2 * sn, x1 * sn + x2 * cs], axis=-1)

def to_blocks(a):
    b, s = a.shape[:2]
    return jnp.moveaxis(a.reshape(b, s // Q_BLOCK, Q_BLOCK, *a.shape[2:]), 1, 0)

def from_blocks(a):
    nb, b, qb = a.shape[:3]
    return jnp.moveaxis(a, 0, 1).reshape(b, nb * qb, *a.shape[3:])

def sweep_query_blocks(fn, *qs):
    nb = qs[0].shape[1] // Q_BLOCK
    out = lax.map(lambda a: fn(*a), (jnp.arange(nb), *[to_blocks(q) for q in qs]))
    return from_blocks(out)

def chunk_mask(blk, s_len):
    t = blk * Q_BLOCK + jnp.arange(Q_BLOCK)
    s = jnp.arange(s_len)
    return t, s, (s[None, :] // CHUNK) <= (t[:, None] // CHUNK)

def diff_attention(q, k, v, lam_vecs, norm_g, layer_idx):
    b, s_len, h = q.shape[:3]
    lam_init = 0.8 - 0.6 * math.exp(-0.3 * layer_idx)
    lv = lam_vecs.astype(jnp.float32)
    lam = jnp.exp(jnp.sum(lv[0] * lv[1])) - jnp.exp(jnp.sum(lv[2] * lv[3])) + lam_init
    slopes = alibi_slopes(h)
    scale = DIFF_D ** -0.5

    def block(blk, qb):
        t, s, mask = chunk_mask(blk, s_len)
        bias = -slopes[:, None, None] * jnp.abs(t[:, None] - s[None, :]).astype(jnp.float32)
        bias = jnp.where(mask[None], bias, -jnp.inf)
        logits = jnp.einsum('bqhcd,bshcd->bchqs', qb, k).astype(jnp.float32) * scale + bias[None, None]
        p = jax.nn.softmax(logits, axis=-1)
        p = p[:, 0] - lam * p[:, 1]
        return jnp.einsum('bhqs,bshe->bqhe', p.astype(v.dtype), v)

    o = sweep_query_blocks(block, q)
    o = rmsnorm(o, norm_g) * (1.0 - lam_init)
    return o.reshape(b, s_len, h * 2 * DIFF_D)

def latent_attention(qd, kvd, kr, q_norm_g, kv_norm_g, w_uq, w_ukv, cos, sin):
    b, s_len = qd.shape[:2]
    h = N_HEADS_G
    q = (rmsnorm(qd, q_norm_g) @ w_uq).reshape(b, s_len, h, QK_NOPE + QK_ROPE)
    q = jnp.concatenate([q[..., :QK_NOPE], apply_rope(q[..., QK_NOPE:], cos, sin)], axis=-1)
    kv = (rmsnorm(kvd, kv_norm_g) @ w_ukv).reshape(b, s_len, h, QK_NOPE + V_HEAD)
    k_nope, v = kv[..., :QK_NOPE], kv[..., QK_NOPE:]
    k_rope = apply_rope(kr[:, :, None, :], cos, sin)
    k = jnp.concatenate([k_nope, jnp.broadcast_to(k_rope, (b, s_len, h, QK_ROPE))], axis=-1)
    scale = (QK_NOPE + QK_ROPE) ** -0.5

    def block(blk, qb):
        _, _, mask = chunk_mask(blk, s_len)
        logits = jnp.einsum('bqhd,bshd->bhqs', qb, k).astype(jnp.float32) * scale
        logits = jnp.where(mask[None, None], logits, -jnp.inf)
        p = jax.nn.softmax(logits, axis=-1)
        return jnp.einsum('bhqs,bshd->bqhd', p.astype(v.dtype), v)

    return sweep_query_blocks(block, q).reshape(b, s_len, h * V_HEAD)

def indexed_sparse_attention(q, k, v, q_idx, k_idx, w_idx):
    b, s_len, h, dh = q.shape
    n_sel = min(TOPK_MAX, s_len // 4)
    slopes = alibi_slopes(h)
    scale = dh ** -0.5
    w = w_idx.astype(jnp.float32) * (IDX_HEADS ** -0.5 * IDX_DIM ** -0.5)

    def block(blk, qb, qib, wb):
        t, _, mask = chunk_mask(blk, s_len)
        score = jax.nn.relu(jnp.einsum('bqhd,bsd->bqhs', qib, k_idx).astype(jnp.float32))
        score = jnp.einsum('bqhs,bqh->bqs', score, wb)
        score = jnp.where(mask[None], score, -jnp.inf)
        top_val, top_idx = lax.top_k(score, n_sel)
        valid = jnp.isfinite(top_val)
        k_sel = jax.vmap(lambda kk, ii: kk[ii])(k, top_idx)
        v_sel = jax.vmap(lambda vv, ii: vv[ii])(v, top_idx)
        logits = jnp.einsum('bqhd,bqnhd->bhqn', qb, k_sel).astype(jnp.float32) * scale
        dist = jnp.abs(t[None, :, None] - top_idx).astype(jnp.float32)
        logits = logits - slopes[None, :, None, None] * dist[:, None]
        logits = jnp.where(valid[:, None], logits, -jnp.inf)
        p = jax.nn.softmax(logits, axis=-1)
        return jnp.einsum('bhqn,bqnhd->bqhd', p.astype(v.dtype), v_sel)

    return sweep_query_blocks(block, q, q_idx, w).reshape(b, s_len, h * dh)

def chunk_band_attention(q, k, v, rel_bias):
    b, s_len, h, dh = q.shape
    nc = s_len // CHUNK
    band = (BAND_CHUNKS + 1) * CHUNK
    qc = q.reshape(b, nc, CHUNK, h, dh)
    pad = ((0, 0), (BAND_CHUNKS * CHUNK, 0), (0, 0), (0, 0))
    kp = jnp.pad(k, pad).reshape(b, nc + BAND_CHUNKS, CHUNK, h, dh)
    vp = jnp.pad(v, pad).reshape(b, nc + BAND_CHUNKS, CHUNK, h, dh)
    k_band = jnp.concatenate([kp[:, j:j + nc] for j in range(BAND_CHUNKS + 1)], axis=2)
    v_band = jnp.concatenate([vp[:, j:j + nc] for j in range(BAND_CHUNKS + 1)], axis=2)
    i = jnp.arange(CHUNK)
    j = jnp.arange(band)
    rel = BAND_CHUNKS * CHUNK + i[:, None] - j[None, :]
    bias = rel_bias[:, jnp.clip(rel, -REL_CLIP, REL_CLIP) + REL_CLIP].astype(jnp.float32)
    key_chunk = jnp.arange(nc)[:, None] - BAND_CHUNKS + (j // CHUNK)[None, :]
    valid = key_chunk >= 0
    logits = jnp.einsum('bnqhd,bnkhd->bnhqk', qc, k_band).astype(jnp.float32) * (dh ** -0.5)
    logits = logits + bias[None, None]
    logits = jnp.where(valid[None, :, None, None, :], logits, -jnp.inf)
    p = jax.nn.softmax(logits, axis=-1)
    o = jnp.einsum('bnhqk,bnkhd->bnqhd', p.astype(v.dtype), v_band)
    return o.reshape(b, s_len, h * dh)

def swiglu(h, w1, w3, w2):
    return (jax.nn.silu(h @ w1) * (h @ w3)) @ w2

def moe_swiglu(h, router, w1, w3, w2):
    b, s_len, d = h.shape
    ht = h.reshape(-1, d)
    logits = (ht @ router).astype(jnp.float32)
    top_val, top_idx = lax.top_k(logits, TOP_K)
    gates = jax.nn.softmax(top_val, axis=-1)
    combine = jnp.sum(jax.nn.one_hot(top_idx, N_EXPERTS, dtype=jnp.float32) * gates[..., None], axis=1)
    out = jnp.zeros_like(ht)
    for e in range(N_EXPERTS):
        out = out + combine[:, e:e + 1].astype(ht.dtype) * swiglu(ht, w1[e], w3[e], w2[e])
    return out.reshape(b, s_len, d)

def first_inputs(seed: int = 0) -> dict:
    key = jax.random.key(seed)
    ks = jax.random.split(key, 24)
    h = N_HEADS_G

    def nrm(k, shape, fan_in, s=1.0):
        return jax.random.normal(k, shape, jnp.float32) * (s * fan_in ** -0.5)

    def gain(k, shape):
        return 1.0 + 0.1 * jax.random.normal(k, shape, jnp.float32)

    return {
        'x': jax.random.normal(ks[0], (BATCH, SEQ, D_MODEL), jnp.float32),
        'c': jax.random.normal(ks[1], (BATCH, D_MODEL), jnp.float32),
        'ada_w': nrm(ks[2], (DEPTH, D_MODEL, 6 * D_MODEL), D_MODEL, 0.5),
        'ada_b': 0.02 * jax.random.normal(ks[3], (DEPTH, 6 * D_MODEL), jnp.float32),
        'mix_norm_g': gain(ks[4], (DEPTH, D_MODEL)),
        'ffn_norm_g': gain(ks[5], (DEPTH, D_MODEL)),
        'w_in': nrm(ks[6], (DEPTH, D_MODEL, D_IN), D_MODEL),
        'w_out': nrm(ks[7], (DEPTH, D_MIX, D_MODEL), D_MIX),
        'diff_lambda': 0.1 * jax.random.normal(ks[8], (DEPTH, 4, DIFF_D), jnp.float32),
        'diff_norm_g': gain(ks[9], (DEPTH, 2 * DIFF_D)),
        'mla_q_norm_g': gain(ks[10], (DEPTH, Q_LORA)),
        'mla_kv_norm_g': gain(ks[11], (DEPTH, KV_LORA)),
        'mla_w_uq': nrm(ks[12], (DEPTH, Q_LORA, h * (QK_NOPE + QK_ROPE)), Q_LORA),
        'mla_w_ukv': nrm(ks[13], (DEPTH, KV_LORA, h * (QK_NOPE + V_HEAD)), KV_LORA),
        'band_rel_bias': 0.2 * jax.random.normal(ks[14], (DEPTH, h, 2 * REL_CLIP + 1), jnp.float32),
        'ffn_w1': nrm(ks[15], (N_DENSE, D_MODEL, D_FF), D_MODEL),
        'ffn_w3': nrm(ks[16], (N_DENSE, D_MODEL, D_FF), D_MODEL),
        'ffn_w2': nrm(ks[17], (N_DENSE, D_FF, D_MODEL), D_FF),
        'moe_router': nrm(ks[18], (N_MOE, D_MODEL, N_EXPERTS), D_MODEL),
        'moe_w1': nrm(ks[19], (N_MOE, N_EXPERTS, D_MODEL, D_FF_EXPERT), D_MODEL),
        'moe_w3': nrm(ks[20], (N_MOE, N_EXPERTS, D_MODEL, D_FF_EXPERT), D_MODEL),
        'moe_w2': nrm(ks[21], (N_MOE, N_EXPERTS, D_FF_EXPERT, D_MODEL), D_FF_EXPERT),
        'final_norm_g': gain(ks[22], (D_MODEL,)),
    }

def first_block(x, c, ada_w, ada_b, mix_norm_g, ffn_norm_g, w_in, w_out, diff_lambda, diff_norm_g,
              mla_q_norm_g, mla_kv_norm_g, mla_w_uq, mla_w_ukv, band_rel_bias,
              ffn_w1, ffn_w3, ffn_w2, moe_router, moe_w1, moe_w3, moe_w2, final_norm_g):
    b, s_len, _ = x.shape
    h = N_HEADS_G
    cos, sin = rope_tables(s_len)
    for l in range(DEPTH):
        mod = jax.nn.silu(c) @ ada_w[l] + ada_b[l]
        sh_m, sc_m, g_m, sh_f, sc_f, g_f = jnp.split(mod, 6, axis=-1)
        hn = adaln(x, mix_norm_g[l], sh_m, sc_m)
        (a_q, a_k, a_v, b_qd, b_kvd, b_kr, c_q, c_k, c_v,
         c_qi, c_ki, c_wi, d_q, d_k, d_v) = jnp.split(hn @ w_in[l], IN_SPLITS, axis=-1)
        o_a = diff_attention(a_q.reshape(b, s_len, h, 2, DIFF_D), a_k.reshape(b, s_len, h, 2, DIFF_D),
                             a_v.reshape(b, s_len, h, 2 * DIFF_D), diff_lambda[l], diff_norm_g[l], l)
        o_b = latent_attention(b_qd, b_kvd, b_kr, mla_q_norm_g[l], mla_kv_norm_g[l],
                               mla_w_uq[l], mla_w_ukv[l], cos, sin)
        o_c = indexed_sparse_attention(c_q.reshape(b, s_len, h, HEAD_DIM), c_k.reshape(b, s_len, h, HEAD_DIM),
                                       c_v.reshape(b, s_len, h, HEAD_DIM),
                                       c_qi.reshape(b, s_len, IDX_HEADS, IDX_DIM), c_ki, c_wi)
        o_d = chunk_band_attention(d_q.reshape(b, s_len, h, HEAD_DIM), d_k.reshape(b, s_len, h, HEAD_DIM),
                                   d_v.reshape(b, s_len, h, HEAD_DIM), band_rel_bias[l])
        y = jnp.concatenate([o_a, o_b, o_c, o_d], axis=-1) @ w_out[l]
        x = x + g_m[:, None, :] * y
        hn = adaln(x, ffn_norm_g[l], sh_f, sc_f)
        if l % 2 == 0:
            f = swiglu(hn, ffn_w1[l // 2], ffn_w3[l // 2], ffn_w2[l // 2])
        else:
            f = moe_swiglu(hn, moe_router[l // 2], moe_w1[l // 2], moe_w3[l // 2], moe_w2[l // 2])
        x = x + g_f[:, None, :] * f
    return rmsnorm(x, final_norm_g)


DEPTH_2 = 1

N_HEADS_NA = 8
N_HEADS_DIL = 8
N_HEADS = N_HEADS_NA + N_HEADS_DIL
D_NA = N_HEADS_NA * HEAD_DIM
D_DIL = N_HEADS_DIL * HEAD_DIM
D_MIX_2 = D_NA + D_DIL
GRID_W = 64
NA_KH = 8
NA_KW = 16
NA_COL_BLOCK = 16
NA_COL_SPAN = 32
DIL_PATTERNS = ((128, 1), (512, 4), (2048, 16))
DIL_QBLOCK = 128
T5_BUCKETS = 32
T5_MAX_DIST = 1024
NORM_EPS = 1e-6
MASK_VALUE = -1e30


def rmsnorm_2(x, g):
    xf = x.astype(jnp.float32)
    y = xf * lax.rsqrt(jnp.mean(xf * xf, axis=-1, keepdims=True) + NORM_EPS)
    return (y * g.astype(jnp.float32)).astype(x.dtype)

def swiglu_2(x, w_gate, w_up, w_down):
    return (jax.nn.silu(x @ w_gate) * (x @ w_up)) @ w_down

def t5_bucket(rel):
    nb = T5_BUCKETS // 2
    max_exact = nb // 2
    n = jnp.abs(rel)
    large = max_exact + (jnp.log(jnp.maximum(n, 1).astype(jnp.float32) / max_exact)
                         / math.log(T5_MAX_DIST / max_exact) * (nb - max_exact)).astype(jnp.int32)
    large = jnp.minimum(large, nb - 1)
    return jnp.where(rel > 0, nb, 0) + jnp.where(n < max_exact, n, large)

def neighbourhood_attention(q, k, v, rel_bias):
    B, H, S, Dh = q.shape
    rows = S // GRID_W
    kh = min(NA_KH, rows)
    ncb = GRID_W // NA_COL_BLOCK
    n_keys = kh * NA_COL_SPAN
    r = jnp.arange(rows)
    key_rows = jnp.clip(r - kh // 2, 0, rows - kh)[:, None] + jnp.arange(kh)[None, :]
    cb = jnp.arange(ncb)
    key_cols = (jnp.clip(cb * NA_COL_BLOCK - NA_KW // 2, 0, GRID_W - NA_COL_SPAN)[:, None]
                + jnp.arange(NA_COL_SPAN)[None, :])
    key_idx = (key_rows[:, None, :, None] * GRID_W
               + key_cols[None, :, None, :]).reshape(rows, ncb, n_keys)
    kr = jnp.repeat(key_rows, NA_COL_SPAN, axis=1)
    kc = jnp.tile(key_cols, (1, kh))
    q_col = cb[:, None] * NA_COL_BLOCK + jnp.arange(NA_COL_BLOCK)[None, :]
    q_col_start = jnp.clip(q_col - NA_KW // 2, 0, GRID_W - NA_KW)
    col_valid = ((kc[:, None, :] >= q_col_start[:, :, None])
                 & (kc[:, None, :] < q_col_start[:, :, None] + NA_KW))
    dc_idx = jnp.clip(kc[:, None, :] - q_col[:, :, None] + NA_KW - 1, 0, 2 * NA_KW - 2)
    dr_idx = kr - r[:, None] + NA_KH - 1
    scale = HEAD_DIM ** -0.5
    q_rows = jnp.moveaxis(q.reshape(B, H, rows, ncb, NA_COL_BLOCK, Dh), 2, 0)

    def row_block(args):
        q_r, idx_r, dr_r = args
        k_r = k[:, :, idx_r]
        v_r = v[:, :, idx_r]
        s = jnp.einsum('bhnqe,bhnke->bhnqk', q_r, k_r,
                       preferred_element_type=jnp.float32) * scale
        bias = rel_bias[:, dr_r[None, None, :], dc_idx].astype(jnp.float32)
        s = jnp.where(col_valid, s + bias, MASK_VALUE)
        p = jax.nn.softmax(s, axis=-1)
        return jnp.einsum('bhnqk,bhnke->bhnqe', p.astype(v.dtype), v_r)

    out = lax.map(row_block, (q_rows, key_idx, dr_idx))
    return jnp.moveaxis(out, 0, 2).reshape(B, H, S, Dh)

def dilated_window_attention(q, k, v, t5_bias, window, dilation):
    B, H, S, Dh = q.shape
    radius = window // (2 * dilation)
    L = S // dilation
    qb = min(DIL_QBLOCK, L)
    nb = -(-L // qb)
    Lp = nb * qb
    kb_len = qb + 2 * radius

    def to_sub(t):
        return t.reshape(B, H, L, dilation, Dh).transpose(0, 1, 3, 2, 4)

    qs = jnp.pad(to_sub(q), ((0, 0), (0, 0), (0, 0), (0, Lp - L), (0, 0))).reshape(B, H, dilation, nb, qb, Dh)
    pad_k = ((0, 0), (0, 0), (0, 0), (radius, radius + Lp - L), (0, 0))
    ks = jnp.pad(to_sub(k), pad_k)
    vs = jnp.pad(to_sub(v), pad_k)
    k_idx = jnp.arange(nb)[:, None] * qb + jnp.arange(kb_len)[None, :]
    k_blk = ks[:, :, :, k_idx]
    v_blk = vs[:, :, :, k_idx]
    q_pos = jnp.arange(nb)[:, None] * qb + jnp.arange(qb)[None, :]
    k_pos = k_idx - radius
    off = k_pos[:, None, :] - q_pos[:, :, None]
    valid = (jnp.abs(off) <= radius) & (k_pos[:, None, :] >= 0) & (k_pos[:, None, :] < L)
    bias = t5_bias[:, t5_bucket(off * dilation)].astype(jnp.float32)
    s = jnp.einsum('bhdnqe,bhdnke->bhdnqk', qs, k_blk,
                   preferred_element_type=jnp.float32) * HEAD_DIM ** -0.5
    s = jnp.where(valid, s + bias[:, None], MASK_VALUE)
    m = jnp.max(s, axis=-1, keepdims=True)
    p = jnp.exp(s - m)
    den = jnp.sum(p, axis=-1)
    o = jnp.einsum('bhdnqk,bhdnke->bhdnqe', p.astype(v.dtype), v_blk,
                   preferred_element_type=jnp.float32) / den[..., None]
    lse = m[..., 0] + jnp.log(den)
    o = o.reshape(B, H, dilation, Lp, Dh)[:, :, :, :L].transpose(0, 1, 3, 2, 4).reshape(B, H, S, Dh)
    lse = lse.reshape(B, H, dilation, Lp)[..., :L].transpose(0, 1, 3, 2).reshape(B, H, S)
    return o, lse

def dilated_mixture_attention(q, k, v, t5_bias):
    results = [dilated_window_attention(q, k, v, t5_bias, w, d) for w, d in DIL_PATTERNS]
    outs = jnp.stack([res[0] for res in results])
    lses = jnp.stack([res[1] for res in results])
    wts = jax.nn.softmax(lses, axis=0)
    return jnp.sum(wts[..., None] * outs, axis=0).astype(q.dtype)

def second_inputs(seed: int = 0) -> dict:
    key = jax.random.key(seed)
    ks = jax.random.split(key, 20)

    def nrm(k, shape, scale):
        return jax.random.normal(k, shape, jnp.float32) * scale

    def gain(k, shape):
        return 1.0 + 0.05 * jax.random.normal(k, shape, jnp.float32)

    return {
        'x': nrm(ks[0], (BATCH, SEQ, D_MODEL), 1.0),
        'ffn1_pre_g': gain(ks[1], (DEPTH_2, D_MODEL)),
        'ffn1_w_gate': nrm(ks[2], (DEPTH_2, D_MODEL, D_FF), D_MODEL ** -0.5),
        'ffn1_w_up': nrm(ks[3], (DEPTH_2, D_MODEL, D_FF), D_MODEL ** -0.5),
        'ffn1_w_down': nrm(ks[4], (DEPTH_2, D_FF, D_MODEL), D_FF ** -0.5),
        'ffn1_post_g': gain(ks[5], (DEPTH_2, D_MODEL)),
        'mix_pre_g': gain(ks[6], (DEPTH_2, D_MODEL)),
        'w_qkv': nrm(ks[7], (DEPTH_2, D_MODEL, 3 * D_MIX_2), D_MODEL ** -0.5),
        'na_rel_bias': nrm(ks[8], (DEPTH_2, N_HEADS_NA, 2 * NA_KH - 1, 2 * NA_KW - 1), 0.5),
        't5_rel_bias': nrm(ks[9], (N_HEADS_DIL, T5_BUCKETS), 0.5),
        'na_out_g': gain(ks[10], (DEPTH_2, D_NA)),
        'dil_out_g': gain(ks[11], (DEPTH_2, D_DIL)),
        'w_out': nrm(ks[12], (DEPTH_2, D_MIX_2, D_MODEL), D_MIX_2 ** -0.5),
        'mix_post_g': gain(ks[13], (DEPTH_2, D_MODEL)),
        'ffn2_pre_g': gain(ks[14], (DEPTH_2, D_MODEL)),
        'ffn2_w_gate': nrm(ks[15], (DEPTH_2, D_MODEL, D_FF), D_MODEL ** -0.5),
        'ffn2_w_up': nrm(ks[16], (DEPTH_2, D_MODEL, D_FF), D_MODEL ** -0.5),
        'ffn2_w_down': nrm(ks[17], (DEPTH_2, D_FF, D_MODEL), D_FF ** -0.5),
        'ffn2_post_g': gain(ks[18], (DEPTH_2, D_MODEL)),
    }

def second_block(x, ffn1_pre_g, ffn1_w_gate, ffn1_w_up, ffn1_w_down, ffn1_post_g,
              mix_pre_g, w_qkv, na_rel_bias, t5_rel_bias, na_out_g, dil_out_g, w_out,
              mix_post_g, ffn2_pre_g, ffn2_w_gate, ffn2_w_up, ffn2_w_down, ffn2_post_g):
    B, S, _ = x.shape
    for l in range(DEPTH_2):
        h = swiglu_2(rmsnorm_2(x, ffn1_pre_g[l]), ffn1_w_gate[l], ffn1_w_up[l], ffn1_w_down[l])
        x = x + 0.5 * rmsnorm_2(h, ffn1_post_g[l])
        h = rmsnorm_2(x, mix_pre_g[l])
        qkv = (h @ w_qkv[l]).reshape(B, S, 3, N_HEADS, HEAD_DIM).transpose(2, 0, 3, 1, 4)
        q, k, v = qkv[0], qkv[1], qkv[2]
        o_na = neighbourhood_attention(q[:, :N_HEADS_NA], k[:, :N_HEADS_NA], v[:, :N_HEADS_NA],
                                       na_rel_bias[l])
        o_dil = dilated_mixture_attention(q[:, N_HEADS_NA:], k[:, N_HEADS_NA:], v[:, N_HEADS_NA:],
                                          t5_rel_bias)
        o_na = rmsnorm_2(o_na.transpose(0, 2, 1, 3).reshape(B, S, D_NA), na_out_g[l])
        o_dil = rmsnorm_2(o_dil.transpose(0, 2, 1, 3).reshape(B, S, D_DIL), dil_out_g[l])
        mixed = jnp.concatenate([o_na, o_dil], axis=-1) @ w_out[l]
        x = x + rmsnorm_2(mixed, mix_post_g[l])
        h = swiglu_2(rmsnorm_2(x, ffn2_pre_g[l]), ffn2_w_gate[l], ffn2_w_up[l], ffn2_w_down[l])
        x = x + 0.5 * rmsnorm_2(h, ffn2_post_g[l])
    return x


def setup_inputs(seed=0):
    out = dict(first_inputs(seed))
    for name, value in second_inputs(seed + 1).items():
        if name != "x":
            out[name + "_2"] = value
    return out


def reference(
    x, c, ada_w, ada_b, mix_norm_g, ffn_norm_g, w_in, w_out, diff_lambda, diff_norm_g,
    mla_q_norm_g, mla_kv_norm_g, mla_w_uq, mla_w_ukv, band_rel_bias, ffn_w1, ffn_w3, ffn_w2,
    moe_router, moe_w1, moe_w3, moe_w2, final_norm_g, ffn1_pre_g_2, ffn1_w_gate_2, ffn1_w_up_2,
    ffn1_w_down_2, ffn1_post_g_2, mix_pre_g_2, w_qkv_2, na_rel_bias_2, t5_rel_bias_2,
    na_out_g_2, dil_out_g_2, w_out_2, mix_post_g_2, ffn2_pre_g_2, ffn2_w_gate_2, ffn2_w_up_2,
    ffn2_w_down_2, ffn2_post_g_2,
):
    x = first_block(
        x, c, ada_w, ada_b, mix_norm_g, ffn_norm_g, w_in, w_out, diff_lambda, diff_norm_g,
        mla_q_norm_g, mla_kv_norm_g, mla_w_uq, mla_w_ukv, band_rel_bias, ffn_w1, ffn_w3, ffn_w2,
        moe_router, moe_w1, moe_w3, moe_w2, final_norm_g,
    )
    return second_block(
        x, ffn1_pre_g_2, ffn1_w_gate_2, ffn1_w_up_2, ffn1_w_down_2, ffn1_post_g_2, mix_pre_g_2,
        w_qkv_2, na_rel_bias_2, t5_rel_bias_2, na_out_g_2, dil_out_g_2, w_out_2, mix_post_g_2,
        ffn2_pre_g_2, ffn2_w_gate_2, ffn2_w_up_2, ffn2_w_down_2, ffn2_post_g_2,
    )


_drawn_inputs = setup_inputs


def setup_inputs(seed=0):
    import zlib

    import numpy as np

    out = dict(_drawn_inputs(seed))
    spreads = {}
    factors = {'mla_q_norm_g': 8.0, 'band_rel_bias': 2.978, 'ffn2_post_g_2': 3.524}
    for name, (base, spread) in spreads.items():
        noise = np.random.default_rng([zlib.crc32(name.encode()), seed]).standard_normal(out[name].shape)
        drawn = base * np.exp(spread * noise) if base else spread * noise
        out[name] = jnp.asarray(drawn.astype(out[name].dtype))
    for name, factor in factors.items():
        out[name] = (out[name] * factor).astype(out[name].dtype)
    return out
```

```python
import math
from contextlib import ExitStack

import concourse.bass as bass
import numpy as np
from concourse import mybir

F32 = mybir.dt.float32
BF16 = mybir.dt.bfloat16
I32 = mybir.dt.int32
ALU = mybir.AluOpType
ACT = mybir.ActivationFunctionType
AX_X = mybir.AxisListType.X

P = 128
T = 256
NB = T // P
D = 1024
KT = D // P
CHW = 2048
RING = 6
ADA_RING = 2
LAYERS = 2
D_IN, D_IN_PAD = 3016, 3072
FW = 256
FF_STEPS = 2816 // FW
EX_STEPS = 3584 // FW
EXPERTS = 8
EPS = 1e-6
MASK = -1e30
TAKEN = -3.0e38
N_SEL = 64
HD = 64

A_Q, A_K, A_V, B_QD, B_KVD, B_KR = 0, 256, 512, 768, 1024, 1152
C_Q, C_K, C_V, C_QI, C_KI, C_WI, D_Q, D_K, D_V = 1184, 1440, 1696, 1952, 2208, 2240, 2248, 2504, 2760
B_UQ = B_QD
B_UKV = A_Q
C_WORK = B_QD + P
C_KIREP = B_QD

GEMM_GROUPS = [6, 2, 6, 2, 6, 2]
FF_CHUNKS, EX_CHUNKS = 3 * FF_STEPS, 3 * EX_STEPS
IN0_CHUNK = 0
OUT0_CHUNK = IN0_CHUNK + 12
FFN0_CHUNK = OUT0_CHUNK + 4
IN1_CHUNK = FFN0_CHUNK + FF_CHUNKS
OUT1_CHUNK = IN1_CHUNK + 12
MOE_CHUNK = OUT1_CHUNK + 4
FFN1_CHUNK = MOE_CHUNK + EXPERTS * EX_CHUNKS
QKV_CHUNK = FFN1_CHUNK + FF_CHUNKS
OUT2_CHUNK = QKV_CHUNK + 12
FFN2_CHUNK = OUT2_CHUNK + 4
N_CHUNKS = FFN2_CHUNK + FF_CHUNKS
GEMM_CHUNK = [IN0_CHUNK, OUT0_CHUNK, IN1_CHUNK, OUT1_CHUNK, QKV_CHUNK, OUT2_CHUNK]
FFN_CHUNK = [FFN0_CHUNK, FFN1_CHUNK, FFN2_CHUNK]
assert EX_CHUNKS % RING == 0

ADA_CHUNKS = LAYERS * 6 * 4
ADA_EARLY = 8
ADA_MID = 26

COL = {}
_at = 0
for _name, _n in (("mix_g", 16), ("ffn_g", 16), ("f1_g", 8), ("mp_g", 8), ("f2_g", 8), ("out_g", 8), ("ada_b", 96),
                  ("q_g", 4), ("kv_g", 2), ("c", 8)):
    COL[_name] = _at
    _at += _n
N_COLS = _at

XG_AT, YE_AT, PS_AT, WS_AT, CT_AT = 2048, 3072, 4096, 4352, 4608
Z_WORDS = 6 * D + ADA_RING * CHW
NA_AT, DIL_AT, TRI_AT, IOTA_AT, RW_AT, LNM_AT, RT_AT = 0, 4096, 8192, 8320, 8448, 8512, 9024
FS_WORDS = 1536


def head_slot(h):
    return (h % 2) * 2 + h // 2


class Group:
    def __init__(self, kind, half, layer, gi):
        self.kind, self.half, self.layer, self.gi = kind, half, layer, gi
        self.units, self.fill0, self.n_fills = [], 0, 0


class Unit:
    def __init__(self, kind, b, part, g, su):
        self.kind, self.b, self.part, self.g, self.layer, self.su = kind, b, part, g, g.layer, su
        self.nk = P * (b + 1) if g.layer < LAYERS else T
        self.bi = self.pu = self.idx = self.comb = None
        self.first_of_group = not g.units


def attention_plan():
    groups, units = [], []
    count = {"su": 0, "bi": 0, "pu": 0, "fill": 0, "idx": 0, "comb": 0}

    def take(name):
        count[name] += 1
        return count[name] - 1

    for layer in range(LAYERS + 1):
        kinds = "ABCD" if layer < LAYERS else ["N0", "N1", "L0", "L1"]
        first = len(groups)
        for kind in kinds:
            groups.append(Group(kind[0], int(kind[1]) if len(kind) > 1 else 0, layer, len(groups)))
        for g in groups[first:]:
            g.fill0 = count["fill"]
            g.n_fills = {"A": 2, "B": 10, "C": 4, "D": 2, "N": 2, "L": 2}[g.kind]
            count["fill"] += g.n_fills
        for g in groups[first:]:
            todo = {"A": [("A", b, c) for b in range(NB) for c in range(2)],
                    "C": [("I", b, hg) for b in range(NB) for hg in range(2)] + [("C", b, 0) for b in range(NB)]}
            for kind, b, part in todo.get(g.kind, [(g.kind, b, 0) for b in range(NB)]):
                u = Unit(kind, b, part, g, take("su"))
                if kind == "I":
                    u.idx = take("idx")
                else:
                    u.bi = take("bi")
                    if not (kind == "A" and part == 0):
                        u.pu = take("pu")
                    if kind == "A" and part == 1:
                        u.comb = take("comb")
                g.units.append(u)
                units.append(u)
    return groups, units


GROUPS, UNITS = attention_plan()
N_CONST = 14
NORM_NO = {0: 1, 2: 2, 3: 3, 5: 4, 6: 5, 7: 6, 8: 7, 9: 8}
SQUARES = {0: 2, 2: 4, 3: 6, 5: 8, 6: 10, 7: 12, 8: 16, 9: 18}
X_READY = {2: 1, 3: 2, 5: 3, 6: 5, 7: 6, 9: 7}


def release(u):
    if u.kind == "I":
        return "idx", u.idx + 1
    if u.kind == "A" and u.part == 1:
        return "comb", u.comb + 1
    return "pT", (UNITS[u.su + 1] if u.kind == "A" else u).pu + 1


def units_of(layer):
    return [u for u in UNITS if u.layer == layer]


def pu_end(layer):
    return max(u.pu for u in UNITS if u.layer == layer and u.pu is not None) + 1


def stream_turns(eng, n_steps, per_step, first_chunk, body):
    per_turn = RING // per_step
    turns = n_steps // per_turn
    if turns > 1:
        with eng.Fori(0, turns) as turn:
            for s in range(per_turn):
                body(first_chunk + s * per_step, turn, s)
    else:
        turns = 0
    for s in range(turns * per_turn, n_steps):
        body(first_chunk + s * per_step, 0, s)


def program(nc, d):
    with ExitStack() as ctx:
        def sb(name, shape, dt=F32):
            return ctx.enter_context(nc.sbuf_tensor(name, shape, dt))

        def sem(name):
            return ctx.enter_context(nc.semaphore(name))

        ring = sb("ring", [P, RING, CHW])
        X = sb("X", [P, NB, D])
        XN = sb("XN", [P, NB, D])
        XT = sb("XT", [P, KT, T])
        PROJ = sb("PROJ", [P, NB, D_IN_PAD])
        gate_mix = sb("gate_mix", [P, D])
        gate_ffn = sb("gate_ffn", [P, D])
        row0 = sb("row0", [P, D])
        row1 = sb("row1", [P, D])
        Z = sb("Z", [P, Z_WORDS])
        alibi = sb("alibi", [P, 1536])
        band = sb("band", [P, 1536])
        cmask = sb("cmask", [P, 384])
        FS = sb("FS", [P, FS_WORDS])
        QK = sb("QK", [P, 2, CHW])
        PR = sb("PR", [P, 2, 4, T])
        PT = sb("PT", [P, 4, NB, P])
        UQ = sb("UQ", [P, 2, 384])
        UKV = sb("UKV", [P, 512])
        unit = sb("unit", [P, 2 * P])
        ident, ones = unit[:, 0:P], unit[:, P:2 * P]
        cols = sb("cols", [P, N_COLS])
        cossin = sb("cossin", [P, NB, 2, 16])
        gdiff = sb("gdiff", [P, LAYERS, HD])
        modc = sb("modc", [P, 32])
        xscale = sb("xscale", [P, KT])
        csilu = sb("csilu", [P, KT])
        ss = sb("ss", [P, 8])
        rstd = sb("rstd", [P, 8])
        nmax = sb("nmax", [P, 2, 4])
        den = sb("den", [P, 2, 4])
        rden = sb("rden", [P, 2, 4])
        lamc = sb("lamc", [P, 8])
        w16 = sb("w16", [P, NB, 8])
        top8 = sb("top8", [P, 8])
        minus_half = sb("minus_half", [P, 8])
        flag = sb("flag", [1, 1], I32)
        ps = ctx.enter_context(nc.psum_tensor("ps", [P, 8, 512], F32))

        proj_words = PROJ[:, :, :].rearrange("p b n -> p (b n)")
        YB = proj_words[:, 0:NB * D].rearrange("p (b n) -> p b n", b=NB)
        XG = proj_words[:, XG_AT:XG_AT + D].rearrange("p (k s) -> p k s", k=KT)
        YE = proj_words[:, YE_AT:YE_AT + D]
        PSEL = proj_words[:, PS_AT:PS_AT + T].rearrange("p (b s) -> p b s", b=NB)
        WSEL = proj_words[:, WS_AT:WS_AT + T].rearrange("p (b s) -> p b s", b=NB)
        CT = proj_words[:, CT_AT:CT_AT + T].rearrange("p (b s) -> p b s", b=NB)
        ada_acc = Z[:, 0:6 * D].rearrange("p (m n) -> p m n", m=6)
        ada_ring = Z[:, 6 * D:Z_WORDS].rearrange("p (s n) -> p s n", s=ADA_RING)
        na_bias = Z[:, NA_AT:NA_AT + 4096].rearrange("p (b g h k) -> p b g h k", b=2, g=2, h=4)
        dil_bias = Z[:, DIL_AT:DIL_AT + 4096].rearrange("p (b g h k) -> p b g h k", b=2, g=2, h=4)
        lnm = Z[:, LNM_AT:LNM_AT + 512].rearrange("p (b k) -> p b k", b=2)
        tri = Z[:, TRI_AT:TRI_AT + P]
        iota = Z[:, IOTA_AT:IOTA_AT + P]
        router = Z[:, RW_AT:RW_AT + 64].rearrange("p (k e) -> p k e", k=KT)

        def rt(i, n):
            return Z[:, RT_AT + i:RT_AT + i + n]

        r_logit = rt(0, 32).rearrange("p (b n) -> p b n", b=NB)
        r_marked = rt(32, 32).rearrange("p (b n) -> p b n", b=NB)
        r_top = rt(64, 16).rearrange("p (b n) -> p b n", b=NB)
        r_take = rt(80, 16).rearrange("p (b n) -> p b n", b=NB)
        r_sel = rt(96, 16).rearrange("p (b n) -> p b n", b=NB)
        r_exp = rt(112, 16).rearrange("p (b n) -> p b n", b=NB)
        r_comb = rt(128, 16).rearrange("p (b n) -> p b n", b=NB)
        r_rank = rt(144, 16).rearrange("p (b n) -> p b n", b=NB)
        r_nv1 = rt(160, 2)
        r_e2 = rt(162, 2)
        r_den = rt(164, 2)
        r_cnt = rt(166, 1)
        r_rk = rt(168, 2)
        r_cb = rt(170, 2)

        sgt = FS[:, 0:512].rearrange("p (b n) -> p b n", b=2)
        hbuf = FS[:, 512:1024].rearrange("p (b n) -> p b n", b=2)
        hT = FS[:, 1024:1536].rearrange("p (b f n) -> p b f n", b=2, f=2)
        KB = FS[:, 0:768].rearrange("p (b h n) -> p b h n", b=2, h=4)
        KI4 = FS[:, 0:1024].rearrange("p (h n) -> p h n", h=4)
        SEL = [FS[:, 1280:1408], FS[:, 1024:1280]]
        TR = FS[:, 1280:1536].rearrange("p (i h n) -> p i h n", i=4, h=4)
        junk = FS[:, 1280:1536]
        lam_in = FS[:, 0:256].rearrange("p (l n) -> p l n", l=LAYERS)
        lam_pr = FS[:, 256:384].rearrange("p (l n) -> p l n", l=LAYERS)
        zero = sb("zero", [1, P], BF16)
        finite = unit[0:1, :].bitcast(BF16)

        full = [sem(f"ring_full{i}") for i in range(RING)]
        chunk_used = sem("chunk_used")
        full_o = [sem(f"ring_full_overflow{i}") for i in range(RING)]
        chunk_used_o = sem("chunk_used_overflow")
        ada_full = [sem(f"ada_full{i}") for i in range(ADA_RING)]
        ada_half, ada_used = sem("ada_half"), sem("ada_used")
        x_in, const_in, late_in, layer_in, rows_in, rows_in2 = (
            sem(n) for n in ("x_in", "const_in", "late_in", "layer_in", "rows_in", "rows_in2"))
        out_done = sem("out_done")
        zero_ready, csilu_ready, lam_exp_in, lam_exp_out = (sem(n) for n in ("zero_ready", "csilu_ready", "lam_exp_in", "lam_exp_out"))
        mod_ps, mod_ready, mod_cols = sem("mod_ps"), sem("mod_ready"), sem("mod_cols")
        sq_ready, xn_ready, xt_ps, xt_ready = (sem(n) for n in ("sq_ready", "xn_ready", "xt_ps", "xt_ready"))
        gemm_ps, gemm_out = sem("gemm_ps"), sem("gemm_out")
        up_ps, silu_ready, h_ready, hT_ps, hT_ready = (sem(n) for n in ("up_ps", "silu_ready", "h_ready", "hT_ps", "hT_ready"))
        y_ps, y_out = sem("y_ps"), sem("y_out")
        res_sq, x_ready = sem("res_sq"), sem("x_ready")
        fill_ps, filled = sem("fill_ps"), sem("filled")
        b_sq, b_normed, b_roped, c_ready = (sem(n) for n in ("b_sq", "b_normed", "b_roped", "c_ready"))
        scores, biased, probs, combined, idx_added = (sem(n) for n in ("scores", "biased", "probs", "combined", "idx_added"))
        pT_ps, pT_ready, o_ps, mixed = (sem(n) for n in ("pT_ps", "pT_ready", "o_ps", "mixed"))
        route_ps, route_max, route_exp, route_sel, rank_ps, route_ready = (
            sem(n) for n in ("route_ps", "route_max", "route_exp", "route_sel", "rank_ps", "route_ready"))
        dve_chain, root_in, root_out, half_ready = (sem(n) for n in ("dve_chain", "root_in", "root_out", "half_ready"))
        moe_sems = []
        for sweep, tag in enumerate(("", "_overflow")):
            m = {n: sem("moe_" + n + tag) for n in (
                "sel_copied", "psel", "wsel", "xg_ps", "xg_ready", "ct_ps", "ct_ready", "up_ps", "silu_ready",
                "h_ready", "hT_ps", "hT_ready", "ye_ps", "ye_ready", "sc_ps", "sc_added")}
            m["full"], m["used"] = (full, chunk_used) if sweep == 0 else (full_o, chunk_used_o)
            m["sweep"] = sweep
            moe_sems.append(m)

        stream, ada = d["stream"], d["ada"]

        def slot_ready(eng, chunk, turn):
            eng.wait_ge(full[chunk % RING], turn * 16 + 16 * (chunk // RING + 1))

        def ring_full_wait(eng, m, local, turn):
            before = (MOE_CHUNK if m["sweep"] == 0 else 0) + local
            eng.wait_ge(m["full"][moe_slot(local)], turn * 16 + 16 * (before // RING + 1))

        def moe_slot(local):
            return (MOE_CHUNK + local) % RING

        block = ctx.enter_context(nc.Block())

        @block.sync
        def _(sp):
            sp.dma_start(X[:, :, :], d["x"].rearrange("a (b p) n -> p (a b) n", p=P)).then_inc(x_in, 16)

            def load_chunks(first, count):
                def load(n, turn, s):
                    sp.wait_ge(chunk_used, turn * RING + (n - RING + 1))
                    src = stream[bass.ds(turn * RING + n, 1)].rearrange("a p n -> (a p) n")
                    sp.dma_start(ring[:, n % RING, :], src).then_inc(full[n % RING], 16)
                stream_turns(sp, count, 1, first, load)

            for n in range(RING):
                sp.dma_start(ring[:, n, :], stream[n]).then_inc(full[n], 16)
            load_chunks(RING, FFN1_CHUNK - RING)

            sp.wait_ge(route_ready, 1)
            over = sp.value_load(flag[0:1, 0:1], min_val=0, max_val=1)
            with sp.If(over > 0):
                sp.wait_ge(chunk_used, FFN1_CHUNK)
                s0 = MOE_CHUNK % RING
                for n in range(RING):
                    sp.dma_start(ring[:, (s0 + n) % RING, :], stream[MOE_CHUNK + n]).then_inc(full_o[(s0 + n) % RING], 16)
                with sp.Fori(1, EXPERTS * EX_CHUNKS // RING) as turn:
                    for n in range(RING):
                        sp.wait_ge(chunk_used_o, turn * RING + (n - RING + 1))
                        src = stream[bass.ds(turn * RING + (MOE_CHUNK + n), 1)].rearrange("a p n -> (a p) n")
                        sp.dma_start(ring[:, (s0 + n) % RING, :], src).then_inc(full_o[(s0 + n) % RING], 16)
                sp.wait_ge(chunk_used_o, EXPERTS * EX_CHUNKS)
            load_chunks(FFN1_CHUNK, N_CHUNKS - FFN1_CHUNK)

            sp.wait_ge(x_ready, 8)
            sp.dma_start(d["out"].rearrange("a (b p) n -> p (a b) n", p=P), X[:, :, :]).then_inc(out_done, 16)
            sp.wait_ge(out_done, 16)

        @block.gpsimd
        def _(pool):
            def load_ada(a, turn=0):
                pool.wait_ge(ada_used, turn * ADA_RING + (a - ADA_RING + 1))
                src = ada[bass.ds(turn * ADA_RING + a, 1)].rearrange("a p n -> (a p) n")
                pool.dma_start(ada_ring[:, a % ADA_RING, :], src).then_inc(ada_full[a % ADA_RING], 16)

            def load_adas(first, count):
                with pool.Fori(0, count // ADA_RING) as turn:
                    for a in range(first, first + ADA_RING):
                        load_ada(a, turn)

            roots = [0]

            def root(lo, hi):
                roots[0] += 1
                pool.wait_ge(root_in, roots[0])
                pool.tensor_tensor(rstd[:, lo:hi], rstd[:, lo:hi], minus_half[:, lo:hi], ALU.pow).then_inc(root_out, 1)

            def attention_roots():
                root(0, 4)
                for b in range(NB):
                    root(4, 8)

            for a in range(ADA_RING):
                pool.dma_start(ada_ring[:, a, :], ada[a]).then_inc(ada_full[a], 16)
            pool.memset(minus_half[:, :], -0.5).then_inc(half_ready, 1)
            pool.wait_ge(half_ready, 1)
            load_adas(ADA_RING, ADA_EARLY)
            root(0, 2)
            load_adas(ADA_RING + ADA_EARLY, ADA_MID - ADA_EARLY)
            attention_roots()
            root(0, 2)
            load_adas(ADA_RING + ADA_MID, ADA_CHUNKS - ADA_RING - ADA_MID)
            root(0, 2)
            pool.wait_ge(mod_ready, 12)
            pool.dma_start(Z[:, NA_AT:NA_AT + 4096], d["na"]).then_inc(late_in, 16)
            pool.dma_start(Z[:, DIL_AT:DIL_AT + 4096], d["dil"]).then_inc(late_in, 16)
            pool.dma_start(Z[:, TRI_AT:TRI_AT + 2 * P], d["tri_iota"]).then_inc(late_in, 16)
            pool.dma_start(Z[:, RW_AT:RW_AT + 64], d["router"]).then_inc(late_in, 16)
            pool.dma_start(Z[:, LNM_AT:LNM_AT + 512], d["lnm"]).then_inc(late_in, 16)
            attention_roots()
            root(0, 2)
            pool.dma_start(row0[:, :], d["rows"][4:5, :].broadcast_to([P, D])).then_inc(rows_in, 16)
            pool.dma_start(row1[:, :], d["rows"][5:6, :].broadcast_to([P, D])).then_inc(rows_in, 16)
            pool.wait_ge(x_ready, 4)
            pool.dma_start(gate_mix[:, :], d["rows"][6:7, :].broadcast_to([P, D])).then_inc(rows_in2, 16)
            pool.dma_start(gate_ffn[:, :], d["rows"][7:8, :].broadcast_to([P, D])).then_inc(rows_in2, 16)
            for lo, hi in ((4, 6), (0, 2), (4, 6), (0, 2), (0, 4), (4, 6), (0, 2), (4, 6)):
                root(lo, hi)

        @block.tensor
        def _(pe):
            def mark(s):
                nc.tensor.matmul(ps[0:1, 7, 0:2], zero[:, 0:1], finite[:, 0:2], start=True, stop=True,
                                 skip_group_check=True).then_inc(s, 1)

            def transpose_x(t):
                for j in range(4):
                    for kt in (2 * j, 2 * j + 1):
                        for b in range(NB):
                            m = nc.tensor.transpose(ps[:, j, (kt % 2) * T + b * P:(kt % 2) * T + (b + 1) * P],
                                                    XN[:, b, kt * P:(kt + 1) * P], ident[:, :])
                    m.then_inc(xt_ps, 1)

            def gemm(g):
                for q in range(GEMM_GROUPS[g]):
                    n = GEMM_CHUNK[g] + 2 * q
                    for b in range(NB):
                        k = 2 * q + b
                        if k >= 3:
                            pe.wait_ge(gemm_out, 2 * sum(GEMM_GROUPS[:g]) + k - 2)
                        for kt in range(KT):
                            if b == 0 and kt % 4 == 0:
                                slot_ready(pe, n + kt // 4, 0)
                            m = nc.tensor.matmul(ps[:, 4 + k % 3, :], XT[:, kt, b * P:(b + 1) * P],
                                                 ring[:, (n + kt // 4) % RING, (kt % 4) * 512:(kt % 4 + 1) * 512],
                                                 start=kt == 0, stop=kt == KT - 1)
                            if b == 1 and kt == 3 or b == 0 and kt == 0 and q > 0:
                                m.then_inc(chunk_used, 1)
                        m.then_inc(gemm_ps, 1)
                mark(chunk_used)

            def clear_y(banks):
                for j in banks:
                    nc.tensor.matmul(ps[:, j, :], zero[:, :], finite, start=True, stop=False,
                                     skip_group_check=True)

            def down(j0, h, chunk_slot, last, used=None):
                for f in range(2):
                    for half in range(2):
                        m = nc.tensor.matmul(ps[:, j0 + half, :], h[:, f, :],
                                             ring[:, chunk_slot, f * D + half * 512:f * D + (half + 1) * 512],
                                             start=False, stop=last and f == 1, skip_group_check=True)
                        if used is not None and f == 0 and half == 0:
                            m.then_inc(used, 1)
                return m

            def up(bank, lhs, slot, kts):
                for kt in kts:
                    m = nc.tensor.matmul(ps[:, bank, :], lhs(kt), ring[:, slot, (kt % 4) * 512:(kt % 4 + 1) * 512],
                                         start=kt == 0, stop=kt == KT - 1, skip_group_check=True)
                return m

            def turn_h(bank, b, used=None):
                for f in range(2):
                    if f == 1 and used is not None:
                        m.then_inc(used, 1)
                    m = nc.tensor.transpose(ps[:, bank, f * P:(f + 1) * P], hbuf[:, b, f * P:(f + 1) * P], ident[:, :])
                return m

            def ffn(i):
                n0 = FFN_CHUNK[i]
                h0 = 2 * FF_STEPS * i
                clear_y(range(4))

                def ups(b, n, turn):
                    for half in range(2):
                        if b == 0:
                            slot_ready(pe, n + half, turn)
                        m = up(4 + b, lambda kt: XT[:, kt, b * P:(b + 1) * P], (n + half) % RING,
                               range(4 * half, 4 * half + 4))
                        if b == 1 and half == 0:
                            m.then_inc(chunk_used, 1)
                    m.then_inc(up_ps, 1)

                ups(0, n0, 0)
                ups(1, n0, 0)
                pe.wait_ge(h_ready, h0 + 1)
                turn_h(6, 0, chunk_used).then_inc(hT_ps, 1)

                def step(n, turn, s):
                    k = turn * 4 + (h0 + 2 + 2 * s)
                    ups(0, n, turn)
                    pe.wait_ge(h_ready, k)
                    turn_h(7, 1).then_inc(hT_ps, 1)
                    slot_ready(pe, n + 2, turn)
                    pe.wait_ge(hT_ready, k - 1)
                    down(0, hT[:, 0], (n + 2) % RING, False)
                    ups(1, n, turn)
                    pe.wait_ge(h_ready, k + 1)
                    turn_h(6, 0, chunk_used).then_inc(hT_ps, 1)
                    pe.wait_ge(hT_ready, k)
                    down(2, hT[:, 1], (n + 2) % RING, False).then_inc(chunk_used, 1)

                stream_turns(pe, FF_STEPS - 1, 3, n0 + 2, step)
                k = h0 + 2 * FF_STEPS
                last = n0 + FF_CHUNKS - 1
                pe.wait_ge(h_ready, k)
                turn_h(7, 1).then_inc(hT_ps, 1)
                slot_ready(pe, last, 0)
                pe.wait_ge(hT_ready, k - 1)
                down(0, hT[:, 0], last % RING, True).then_inc(y_ps, 1)
                pe.wait_ge(hT_ready, k)
                down(2, hT[:, 1], last % RING, True).then_inc(y_ps, 1)
                mark(chunk_used)

            def mod_columns(first, count, fills_before, ada_needed):
                pe.wait_ge(ada_used, ada_needed)
                if fills_before:
                    pe.wait_ge(mod_ready, fills_before)
                for i, m6 in enumerate(range(first, first + count)):
                    for j in range(KT):
                        c = i * KT + j
                        m = nc.tensor.matmul(ps[:, 6, c:c + 1], ada_acc[:, m6, j * P:(j + 1) * P], ones[:, 0:1],
                                             start=True, stop=True)
                m.then_inc(mod_ps, 1)

            def mod_rows(m6, fills_before):
                for half in range(2):
                    pe.wait_ge(mod_ready, fills_before + half)
                    nc.tensor.matmul(ps[:, 6, :], ones[:, :], ada_acc[:, m6, half * 512:(half + 1) * 512],
                                     start=True, stop=True).then_inc(mod_ps, 1)

            def fills(g):
                qk = QK[:, g.gi % 2, :]
                f = g.fill0

                def begin(f):
                    if f >= 1:
                        pe.wait_ge(filled, f)

                def tiles(srcs):
                    for i, src in enumerate(srcs):
                        for b in range(NB):
                            a = src(b)
                            m = nc.tensor.transpose(ps[0:a.shape[-1], 7, i * T + b * P:i * T + (b + 1) * P], a, ident[:, :])
                    return m

                def pair(col):
                    return [lambda b, c=c: PROJ[:, b, c:c + P] for c in (col, col + P)]

                if g.kind in "AD" or g.kind in "NL":
                    base = {"A": (A_Q, A_K), "D": (D_Q, D_K)}.get(g.kind)
                    if base is None:
                        h0 = (8 if g.kind == "L" else 0) + 4 * g.half
                        base = (h0 * HD, D + h0 * HD)
                    for c in base:
                        begin(f)
                        tiles(pair(c)).then_inc(fill_ps, 1)
                        f += 1
                if g.kind == "C":
                    for c in (C_Q, C_K, C_QI):
                        begin(f)
                        tiles(pair(c)).then_inc(fill_ps, 1)
                        f += 1
                    begin(f)
                    pe.wait_ge(c_ready, g.layer + 1)
                    tiles([lambda b: PROJ[:, b, C_KIREP:C_KIREP + P]]).then_inc(fill_ps, 1)
                if g.kind == "B":
                    begin(f)
                    if g.layer == 1:
                        pe.wait_ge(layer_in, 16 * 3)
                    pe.wait_ge(b_normed, g.layer + 1)
                    tiles(pair(B_QD)).then_inc(fill_ps, 1)
                    begin(f + 1)
                    tiles([lambda b: PROJ[:, b, B_KVD:B_KVD + P]]).then_inc(fill_ps, 1)
                    for b in range(NB):
                        begin(f + 2 + b)
                        for kt in range(2):
                            m = nc.tensor.matmul(ps[:, 7, 0:384], qk[:, kt * T + b * P:kt * T + (b + 1) * P], UQ[:, kt, :],
                                                 start=kt == 0, stop=kt == 1)
                        m.then_inc(fill_ps, 1)
                    for b in range(NB):
                        begin(f + 4 + b)
                        nc.tensor.matmul(ps[:, 7, :], qk[:, 512 + b * P:512 + (b + 1) * P], UKV[:, :],
                                         start=True, stop=True).then_inc(fill_ps, 1)
                    for j in range(2):
                        begin(f + 6 + j)
                        if j == 0:
                            pe.wait_ge(b_roped, g.layer + 1)
                        tiles([lambda b, h=h: PROJ[:, b, B_UQ + 96 * h:B_UQ + 96 * (h + 1)]
                               for h in (2 * j, 2 * j + 1)]).then_inc(fill_ps, 1)
                    for j in range(2):
                        begin(f + 8 + j)
                        tiles([lambda b, h=h: KB[:, b, h, :] for h in (2 * j, 2 * j + 1)]).then_inc(fill_ps, 1)

            def score(u):
                qk = QK[:, u.g.gi % 2, :]
                pe.wait_ge(filled, u.g.fill0 + u.g.n_fills)
                if u.su >= 2:
                    pe.wait_ge(probs, u.su - 1)
                j0 = 2 * (u.su % 2)
                for h in range(4):
                    s = head_slot(h)
                    out = ps[:, j0 + s // 2, (s % 2) * T:(s % 2) * T + u.nk]
                    q0 = u.b * P
                    if u.kind == "I":
                        lhs, rhs = qk[:, (4 + u.part) * T + q0:(4 + u.part) * T + q0 + P], KI4[:, h, 0:u.nk]
                    elif u.kind == "B":
                        lhs, rhs = qk[0:96, h * T + q0:h * T + q0 + P], qk[0:96, D + h * T:D + h * T + u.nk]
                    else:
                        p0, rows = (h % 2) * HD, HD
                        if u.kind == "A":
                            p0, rows = p0 + 32 * u.part, 32
                        tq, tk = h // 2, 2 + h // 2
                        lhs = qk[p0:p0 + rows, tq * T + q0:tq * T + q0 + P]
                        rhs = qk[p0:p0 + rows, tk * T:tk * T + u.nk]
                    m = nc.tensor.matmul(out, lhs, rhs, start=True, stop=True)
                m.then_inc(scores, 1)

            def values(u):
                src = PR[:, (u.su - 1) % 2 if u.kind == "A" else u.su % 2]
                if u.kind == "A":
                    pe.wait_ge(combined, u.comb + 1)
                else:
                    pe.wait_ge(probs, u.su + 1)
                for h in range(4):
                    for kb in range(u.nk // P):
                        m = nc.tensor.transpose(ps[:, 4 + h // 2, (h % 2) * T + kb * P:(h % 2) * T + (kb + 1) * P],
                                                src[:, head_slot(h), kb * P:(kb + 1) * P], ident[:, :])
                m.then_inc(pT_ps, 1)
                pe.wait_ge(pT_ready, u.pu + 1)
                if u.pu >= 1:
                    pe.wait_ge(mixed, u.pu)
                for h in range(4):
                    for kb in range(u.nk // P):
                        if u.kind == "B":
                            c = B_UKV + h * P + HD
                        else:
                            c = {"A": A_V, "C": C_V, "D": D_V, "N": 2 * D, "L": 2 * D + 512}[u.kind] + (4 * u.g.half + h) * HD
                        m = nc.tensor.matmul(ps[:, 6, h * HD:(h + 1) * HD], PT[:, h, kb, :], PROJ[:, kb, c:c + HD],
                                             start=kb == 0, stop=kb == u.nk // P - 1)
                m.then_inc(o_ps, 1)

            def attention(layer):
                us = units_of(layer)
                pe.wait_ge(gemm_out, 2 * sum(GEMM_GROUPS[:2 * layer + 1]))
                fills(us[0].g)
                score(us[0])
                for n, u in enumerate(us):
                    if u.first_of_group and u.g.gi + 1 < len(GROUPS) and GROUPS[u.g.gi + 1].layer == layer:
                        fills(GROUPS[u.g.gi + 1])
                    if n + 1 < len(us):
                        score(us[n + 1])
                    if u.pu is not None:
                        values(u)

            def route():
                pe.wait_ge(late_in, 16 * 5)
                for b in range(NB):
                    for kt in range(KT):
                        m = nc.tensor.matmul(ps[:, 7, b * 8:(b + 1) * 8], XT[:, kt, b * P:(b + 1) * P], router[:, kt, :],
                                             start=kt == 0, stop=kt == KT - 1)
                m.then_inc(route_ps, 1)
                pe.wait_ge(route_sel, 1)
                nc.tensor.matmul(ps[:, 7, 0:8], tri, r_sel[:, 0, :], start=True, stop=True)
                nc.tensor.matmul(ps[:, 7, 8:16], tri, r_sel[:, 1, :], start=True, stop=False)
                nc.tensor.matmul(ps[:, 7, 8:16], ones[:, :], r_sel[:, 0, :], start=False, stop=True)
                nc.tensor.matmul(ps[:, 7, 16:24], ones[:, :], r_sel[:, 0, :], start=True, stop=False)
                nc.tensor.matmul(ps[:, 7, 16:24], ones[:, :], r_sel[:, 1, :], start=False, stop=True).then_inc(rank_ps, 1)

            def experts(m):
                with pe.Fori(0, EXPERTS) as e:
                    turn_e = e * (EX_CHUNKS // RING)
                    k_e = e * EX_STEPS
                    pe.wait_ge(m["psel"], e + 1)
                    for j in range(KT):
                        for b in range(NB):
                            mm = nc.tensor.matmul(ps[:, 2 + j // 4, (j % 4) * P:(j % 4 + 1) * P],
                                                  XN[:, b, j * P:(j + 1) * P], PSEL[:, b, :], start=b == 0, stop=b == 1)
                    mm.then_inc(m["xg_ps"], 1)
                    pe.wait_ge(m["wsel"], e + 1)
                    for b in range(NB):
                        mm = nc.tensor.transpose(ps[:, 7, b * P:(b + 1) * P], WSEL[:, b, :], ident[:, :])
                    mm.then_inc(m["ct_ps"], 1)
                    clear_y(range(2))
                    pe.wait_ge(m["xg_ready"], e + 1)
                    pe.wait_ge(m["ct_ready"], e + 1)

                    def ups(half, par, local, turn):
                        ring_full_wait(pe, m, local + half, turn)
                        return up(4 + par, lambda kt: XG[:, kt, :], moe_slot(local + half),
                                  range(4 * half, 4 * half + 4))

                    ups(0, 0, 0, turn_e).then_inc(m["used"], 1)
                    ups(1, 0, 0, turn_e).then_inc(m["up_ps"], 1)
                    mark(m["used"])

                    def step(local, turn, s):
                        turn = turn + turn_e
                        k = k_turn(s)
                        par = (1 + s) % 2
                        ups(0, par, local, turn).then_inc(m["used"], 1)
                        pe.wait_ge(m["h_ready"], k)
                        turn_h(6 + (1 - par), 1 - par).then_inc(m["hT_ps"], 1)
                        ups(1, par, local, turn).then_inc(m["up_ps"], 1)
                        ring_full_wait(pe, m, local + 2, turn)
                        pe.wait_ge(m["hT_ready"], k)
                        down(0, hT[:, 1 - par], moe_slot(local + 2), False, m["used"]).then_inc(m["used"], 1)

                    turns = (EX_STEPS - 1) // 2
                    with pe.Fori(0, turns) as t:
                        def k_turn(s):
                            return t * 2 + k_e + (1 + s)
                        for s in range(2):
                            step(2 + 3 * s, t, s)

                    def k_turn(s):
                        return k_e + (1 + s)
                    for s in range(2 * turns, EX_STEPS - 1):
                        step(2 + 3 * s, 0, s)
                    par = (EX_STEPS - 1) % 2
                    pe.wait_ge(m["h_ready"], k_e + EX_STEPS)
                    turn_h(6 + par, par).then_inc(m["hT_ps"], 1)
                    ring_full_wait(pe, m, EX_CHUNKS - 1, turn_e)
                    pe.wait_ge(m["hT_ready"], k_e + EX_STEPS)
                    down(0, hT[:, par], moe_slot(EX_CHUNKS - 1), True).then_inc(m["ye_ps"], 1)
                    mark(m["used"])
                    pe.wait_ge(m["ye_ready"], e + 1)
                    for b in range(NB):
                        if b == 1:
                            pe.wait_ge(m["sc_added"], e * 2 + 1)
                        for half in range(2):
                            mm = nc.tensor.matmul(ps[:, 2 + half, :], CT[:, b, :], YE[:, half * 512:(half + 1) * 512],
                                                  start=True, stop=True)
                        mm.then_inc(m["sc_ps"], 1)
                    pe.wait_ge(m["sc_added"], e * 2 + 2)

            pe.wait_ge(zero_ready, 1)
            pe.wait_ge(const_in, 16 * N_CONST)
            for layer in range(LAYERS):
                if layer == 0:
                    mod_columns(0, 2, 0, ADA_EARLY)
                else:
                    mod_columns(0, 2, 6, ADA_CHUNKS)
                    mod_rows(2, 7)
                    mod_columns(3, 2, 9, ADA_CHUNKS)
                    mod_rows(5, 10)
                pe.wait_ge(xn_ready, 2 * NORM_NO[3 * layer])
                transpose_x(3 * layer)
                pe.wait_ge(xt_ready, 4 * (3 * layer + 1))
                gemm(2 * layer)
                if layer == 0:
                    pe.wait_ge(gemm_out, 12)
                    pe.wait_ge(ada_used, 24)
                    mod_rows(2, 1)
                    mod_columns(3, 2, 3, 24)
                    mod_rows(5, 4)
                pe.wait_ge(mod_ready, 6 if layer == 0 else 12)
                attention(layer)
                pe.wait_ge(mixed, pu_end(layer))
                transpose_x(3 * layer + 1)
                pe.wait_ge(xt_ready, 4 * (3 * layer + 2))
                gemm(2 * layer + 1)
                pe.wait_ge(xn_ready, 2 * NORM_NO[3 * layer + 2])
                transpose_x(3 * layer + 2)
                pe.wait_ge(xt_ready, 4 * (3 * layer + 3))
                if layer == 0:
                    ffn(0)
                else:
                    route()
                    experts(moe_sems[0])
                    pe.wait_ge(route_ready, 1)
                    over = pe.value_load(flag[0:1, 0:1], min_val=0, max_val=1)
                    with pe.If(over > 0):
                        experts(moe_sems[1])
            pe.wait_ge(xn_ready, 10)
            transpose_x(6)
            pe.wait_ge(xt_ready, 28)
            ffn(1)
            pe.wait_ge(xn_ready, 12)
            transpose_x(7)
            pe.wait_ge(xt_ready, 32)
            gemm(4)
            attention(2)
            pe.wait_ge(xn_ready, 14)
            transpose_x(8)
            pe.wait_ge(xt_ready, 36)
            gemm(5)
            pe.wait_ge(xn_ready, 16)
            transpose_x(9)
            pe.wait_ge(xt_ready, 40)
            ffn(2)

        @block.scalar
        def _(act):
            def loads(pairs, s):
                for dst, src in pairs:
                    act.dma_start(dst, src).then_inc(s, 16)

            loads([(cols[:, :], d["cols"]), (unit[:, :], d["unit"]),
                   (lam_in, d["lam"].broadcast_to([P, 256]).rearrange("p (l n) -> p l n", l=LAYERS)),
                   (gate_mix[:, :], d["rows"][0:1, :].broadcast_to([P, D])),
                   (gate_ffn[:, :], d["rows"][1:2, :].broadcast_to([P, D])),
                   (row0[:, :], d["rows"][2:3, :].broadcast_to([P, D])),
                   (row1[:, :], d["rows"][3:4, :].broadcast_to([P, D])),
                   (gdiff[:, :, :].rearrange("p l n -> p (l n)"), d["gdiff"].broadcast_to([P, LAYERS * HD])),
                   (cossin[:, :, :, :].rearrange("p b c n -> p (b c n)"), d["cossin"]),
                   (alibi[:, :], d["alibi"]), (cmask[:, :], d["cmask"]), (band[:, :], d["band"][0]),
                   (UKV[:, :], d["ukv"][0]), (UQ[:, :, :].rearrange("p k n -> p (k n)"), d["uq"][0])], const_in)

            def squares(t):
                if t == 0:
                    act.wait_ge(x_in, 16)
                elif t == 8:
                    act.wait_ge(mixed, pu_end(LAYERS))
                else:
                    act.wait_ge(x_ready, X_READY[t])
                if t == 8:
                    for b in range(NB):
                        for half in range(2):
                            cs = slice(half * 512, (half + 1) * 512)
                            act.activation(YB[:, b, cs], XN[:, b, cs], ACT.Square,
                                           accum_out=ss[:, 2 * b + half:2 * b + half + 1]).then_inc(sq_ready, 1)
                else:
                    for b in range(NB):
                        act.activation(XN[:, b, :], X[:, b, :], ACT.Square,
                                       accum_out=ss[:, b:b + 1]).then_inc(sq_ready, 1)

            def gemm_copy(g):
                dst = PROJ if g % 2 == 0 else YB
                for q in range(GEMM_GROUPS[g]):
                    for b in range(NB):
                        k = 2 * q + b
                        act.wait_ge(gemm_ps, 2 * sum(GEMM_GROUPS[:g]) + k + 1)
                        act.activation(dst[:, b, q * 512:(q + 1) * 512], ps[:, 4 + k % 3, :], ACT.Copy).then_inc(gemm_out, 1)

            def silu(s_in, s_out, count, par):
                act.wait_ge(s_in, count)
                act.activation(sgt[:, par, :], ps[:, 4 + par, 0:FW], ACT.Silu).then_inc(s_out, 1)

            def copy_hT(s_in, s_out, count, par):
                act.wait_ge(s_in, count)
                act.activation(hT[:, par].rearrange("p f n -> p (f n)"), ps[:, 6 + par, 0:2 * P], ACT.Copy).then_inc(s_out, 1)

            def ffn(i):
                h0 = 2 * FF_STEPS * i
                silu(up_ps, silu_ready, h0 + 1, 0)
                silu(up_ps, silu_ready, h0 + 2, 1)
                copy_hT(hT_ps, hT_ready, h0 + 1, 0)

                def step(n, turn, s):
                    k = turn * 4 + (h0 + 2 + 2 * s)
                    silu(up_ps, silu_ready, k + 1, 0)
                    copy_hT(hT_ps, hT_ready, k, 1)
                    silu(up_ps, silu_ready, k + 2, 1)
                    copy_hT(hT_ps, hT_ready, k + 1, 0)

                stream_turns(act, FF_STEPS - 1, 3, 2, step)
                copy_hT(hT_ps, hT_ready, h0 + 2 * FF_STEPS, 1)
                for b in range(NB):
                    act.wait_ge(y_ps, 2 * i + b + 1)
                    act.activation(YB[:, b, :], ps[:, 2 * b:2 * b + 2, :].rearrange("p j n -> p (j n)"), ACT.Copy).then_inc(y_out, 1)

            def result_squares(src, number, s, count):
                act.wait_ge(s, count)
                for b in range(NB):
                    act.activation(XN[:, b, :], src[:, b, :], ACT.Square,
                                   accum_out=ss[:, 4 + b:5 + b]).then_inc(res_sq, 1)

            def copy_fills(g):
                qk = QK[:, g.gi % 2, :]
                f = g.fill0

                def fill(f, dst, src, scale=1.0, last=True):
                    act.wait_ge(fill_ps, f + 1)
                    ins = act.activation(dst, src, ACT.Copy, scale=scale)
                    if last:
                        ins.then_inc(filled, 1)

                if g.kind in "ADNL":
                    for i in range(2):
                        fill(f + i, qk[:, i * 512:(i + 1) * 512], ps[:, 7, :])
                if g.kind == "C":
                    for i in range(3):
                        fill(f + i, qk[:, i * 512:(i + 1) * 512], ps[:, 7, :])
                    for h in range(4):
                        fill(f + 3, KI4[32 * h:32 * (h + 1), h, :], ps[32 * h:32 * (h + 1), 7, 0:T], last=h == 3)
                if g.kind == "B":
                    for i, (c, w) in enumerate(((B_QD, 256), (B_KVD, 128))):
                        for b in range(NB):
                            if 2 * i + b > 0:
                                act.wait_ge(b_sq, 4 * g.layer + 2 * i + b)
                            act.activation(junk[:, 0:w], PROJ[:, b, c:c + w], ACT.Square,
                                           accum_out=ss[:, 2 * i + b:2 * i + b + 1]).then_inc(b_sq, 1)
                    for kt in range(2):
                        at = COL["q_g"] + 2 * g.layer + kt
                        fill(f, qk[:, kt * T:(kt + 1) * T], ps[:, 7, kt * T:(kt + 1) * T], cols[:, at:at + 1], kt == 1)
                    at = COL["kv_g"] + g.layer
                    fill(f + 1, qk[:, 512:768], ps[:, 7, 0:T], cols[:, at:at + 1])
                    for b in range(NB):
                        fill(f + 2 + b, PROJ[:, b, B_UQ:B_UQ + 384], ps[:, 7, 0:384])
                    for b in range(NB):
                        fill(f + 4 + b, PROJ[:, b, B_UKV:B_UKV + 512], ps[:, 7, :])
                    for i in range(4):
                        fill(f + 6 + i, qk[0:96, i * 512:(i + 1) * 512], ps[0:96, 7, :])

            def probabilities(u):
                par = u.su % 2
                if u.su >= 2:
                    name, number = release(UNITS[u.su - 2])
                    act.wait_ge({"idx": idx_added, "comb": combined, "pT": pT_ps}[name], number)
                src = ps[:, 2 * par:2 * par + 2, :].rearrange("p j (s k) -> p (j s) k", s=2)
                if u.kind == "I":
                    act.wait_ge(scores, u.su + 1)
                    act.activation(PR[:, par, :, 0:u.nk], src[:, :, 0:u.nk], ACT.Relu).then_inc(probs, 1)
                    return
                act.wait_ge(biased, u.bi + 1)
                for h in range(4):
                    s = head_slot(h)
                    ins = act.activation(PR[:, par, s, 0:u.nk], src[:, s, 0:u.nk], ACT.Exp, bias=nmax[:, par, s:s + 1],
                                         accum_out=den[:, par, h:h + 1])
                ins.then_inc(probs, 1)

            def copy_pT(u):
                act.wait_ge(pT_ps, u.pu + 1)
                src = ps[:, 4:6, :].rearrange("p j (h k) -> p (j h) k", h=2)
                act.activation(PT[:, :, :, :].rearrange("p h b q -> p h (b q)")[:, :, 0:u.nk], src[:, :, 0:u.nk],
                               ACT.Copy).then_inc(pT_ready, 1)

            def attention(layer):
                us = units_of(layer)
                copy_fills(us[0].g)
                probabilities(us[0])
                for n, u in enumerate(us):
                    if u.first_of_group and u.g.gi + 1 < len(GROUPS) and GROUPS[u.g.gi + 1].layer == layer:
                        copy_fills(GROUPS[u.g.gi + 1])
                    if n + 1 < len(us):
                        probabilities(us[n + 1])
                    if u.pu is not None:
                        copy_pT(u)

            def route():
                act.wait_ge(route_max, 1)
                for b in range(NB):
                    act.activation(r_exp[:, b, :], r_logit[:, b, 0:8], ACT.Exp, bias=r_nv1[:, b:b + 1])
                    ins = act.activation(r_e2[:, b:b + 1], r_top[:, b, 1:2], ACT.Exp, bias=r_nv1[:, b:b + 1])
                ins.then_inc(route_exp, 1)

            def experts(m):
                with act.Fori(0, EXPERTS) as e:
                    k_e = e * EX_STEPS
                    act.wait_ge(m["xg_ps"], e + 1)
                    for j in range(KT):
                        ins = act.activation(XG[:, j, :], ps[:, 2 + j // 4, (j % 4) * P:(j % 4 + 1) * P], ACT.Identity,
                                             scale=xscale[:, j:j + 1], bias=modc[:, 16 + j:17 + j])
                    ins.then_inc(m["xg_ready"], 1)
                    act.wait_ge(m["ct_ps"], e + 1)
                    act.activation(CT.rearrange("p b s -> p (b s)"), ps[:, 7, 0:T], ACT.Copy).then_inc(m["ct_ready"], 1)
                    silu(m["up_ps"], m["silu_ready"], k_e + 1, 0)
                    turns = (EX_STEPS - 1) // 2
                    with act.Fori(0, turns) as t:
                        for s in range(2):
                            k = t * 2 + k_e + (1 + s)
                            copy_hT(m["hT_ps"], m["hT_ready"], k, s)
                            silu(m["up_ps"], m["silu_ready"], k + 1, 1 - s)
                    for s in range(2 * turns, EX_STEPS - 1):
                        k = k_e + (1 + s)
                        copy_hT(m["hT_ps"], m["hT_ready"], k, s % 2)
                        silu(m["up_ps"], m["silu_ready"], k + 1, 1 - s % 2)
                    copy_hT(m["hT_ps"], m["hT_ready"], k_e + EX_STEPS, (EX_STEPS - 1) % 2)
                    act.wait_ge(m["ye_ps"], e + 1)
                    act.activation(YE, ps[:, 0:2, :].rearrange("p j n -> p (j n)"), ACT.Copy).then_inc(m["ye_ready"], 1)

            act.wait_ge(const_in, 16 * N_CONST)
            act.activation(csilu[:, :], cols[:, COL["c"]:COL["c"] + KT], ACT.Silu).then_inc(csilu_ready, 1)
            act.wait_ge(lam_exp_in, 1)
            act.activation(lamc[:, 0:4], lamc[:, 4:8], ACT.Exp).then_inc(lam_exp_out, 1)
            for layer in range(LAYERS):
                squares(3 * layer)
                gemm_copy(2 * layer)
                act.wait_ge(gemm_out, 2 * sum(GEMM_GROUPS[:2 * layer + 1]))
                attention(layer)
                if layer + 1 < LAYERS:
                    act.wait_ge(mixed, pu_end(layer))
                    act.wait_ge(filled, GROUPS[3].fill0)
                    loads([(band[:, :], d["band"][layer + 1]), (UKV[:, :], d["ukv"][layer + 1]),
                           (UQ[:, :, :].rearrange("p k n -> p (k n)"), d["uq"][layer + 1])], layer_in)
                gemm_copy(2 * layer + 1)
                squares(3 * layer + 2)
                if layer == 0:
                    ffn(0)
                else:
                    route()
                    experts(moe_sems[0])
                    act.wait_ge(route_ready, 1)
                    over = act.value_load(flag[0:1, 0:1], min_val=0, max_val=1)
                    with act.If(over > 0):
                        experts(moe_sems[1])
            result_squares(X, 0, x_ready, 4)
            squares(6)
            ffn(1)
            result_squares(YB, 1, y_out, 4)
            squares(7)
            gemm_copy(4)
            attention(2)
            squares(8)
            gemm_copy(5)
            result_squares(YB, 2, gemm_out, 2 * sum(GEMM_GROUPS))
            squares(9)
            ffn(2)
            result_squares(YB, 3, y_out, 6)

        @block.vector
        def _(dve):
            linked = [0]

            def link(ins):
                linked[0] += 1
                ins.then_inc(dve_chain, 1)
                dve.wait_ge(dve_chain, linked[0])

            def ada_step(a, turn=0, m6=None):
                q = a % 4
                acc = ada_acc[:, (a % 24) // 4, :] if m6 is None else ada_acc[:, bass.ds(m6, 1), :].rearrange("p a n -> p (a n)")
                dve.wait_ge(ada_full[a % ADA_RING], turn * (16 * 4 // ADA_RING) + 16 * (a // ADA_RING + 1))
                w = ada_ring[:, a % ADA_RING, :]
                if q == 0:
                    nc.vector.tensor_scalar(acc, w[:, 0:D], csilu[:, 0:1], None, ALU.mult).then_inc(ada_half, 1)
                else:
                    dve.wait_ge(ada_used, turn * 4 + a)
                    nc.vector.scalar_tensor_tensor(acc, w[:, 0:D], csilu[:, 2 * q:2 * q + 1], acc, ALU.mult,
                                                   ALU.add).then_inc(ada_half, 1)
                dve.wait_ge(ada_half, turn * 4 + (a + 1))
                nc.vector.scalar_tensor_tensor(acc, w[:, D:2 * D], csilu[:, 2 * q + 1:2 * q + 2], acc, ALU.mult,
                                               ALU.add).then_inc(ada_used, 1)

            def mod_columns_add(first, layer, number):
                dve.wait_ge(mod_ps, number)
                at = COL["ada_b"] + 48 * layer + 8 * first
                to = 0 if first == 0 else 16
                link(nc.vector.tensor_tensor(modc[:, to:to + 16], ps[:, 6, 0:16], cols[:, at:at + 16], ALU.add))
                g = COL["mix_g" if first == 0 else "ffn_g"] + 8 * layer
                return to, g

            def mod_columns(first, layer, number):
                to, g = mod_columns_add(first, layer, number)
                nc.vector.tensor_copy(ps[0:1, 6, 0:1], modc[0:1, 0:1]).then_inc(mod_ready, 1)

            def set_xscale(first, layer):
                to = 0 if first == 0 else 16
                g = COL["mix_g" if first == 0 else "ffn_g"] + 8 * layer
                link(nc.vector.scalar_tensor_tensor(xscale[:, :], modc[:, to + 8:to + 16], 1.0, cols[:, g:g + 8],
                                                    ALU.add, ALU.mult))

            def mod_rows(gate, bias, number):
                for half in range(2):
                    dve.wait_ge(mod_ps, number + half)
                    cs = slice(half * 512, (half + 1) * 512)
                    nc.vector.tensor_tensor(gate[:, cs], ps[:, 6, :], bias[:, cs], ALU.add).then_inc(mod_ready, 1)

            roots = [0]

            def inverse_root(*parts):
                for out, sums, width in parts:
                    ins = nc.vector.tensor_scalar(out, sums, 1.0 / width, EPS, ALU.mult, ALU.add)
                roots[0] += 1
                ins.then_inc(root_in, 1)
                dve.wait_ge(root_out, roots[0])

            def normalise(t):
                dve.wait_ge(sq_ready, SQUARES[t])
                if t == 8:
                    inverse_root((rstd[:, 0:4], ss[:, 0:4], 512))
                    for b in range(NB):
                        for half in range(2):
                            cs = slice(half * 512, (half + 1) * 512)
                            ins = nc.vector.tensor_scalar(XN[:, b, cs], XN[:, b, cs],
                                                          rstd[:, 2 * b + half:2 * b + half + 1], None, ALU.mult)
                        ins.then_inc(xn_ready, 1)
                else:
                    inverse_root((rstd[:, 0:2], ss[:, 0:2], D))
                    for b in range(NB):
                        nc.vector.tensor_scalar(XN[:, b, :], X[:, b, :], rstd[:, b:b + 1], None,
                                                ALU.mult).then_inc(xn_ready, 1)

            def copy_xt(t):
                gain = {6: "f1_g", 7: "mp_g", 8: "out_g", 9: "f2_g"}.get(t)
                for j in range(4):
                    dve.wait_ge(xt_ps, 4 * t + j + 1)
                    if t in (1, 4):
                        nc.vector.tensor_copy(XT[:, 2 * j:2 * j + 2, :].rearrange("p k n -> p (k n)"), ps[:, j, :]).then_inc(xt_ready, 1)
                        continue
                    for kt in (2 * j, 2 * j + 1):
                        src = ps[:, j, (kt % 2) * T:(kt % 2 + 1) * T]
                        if gain:
                            at = COL[gain] + kt
                            ins = nc.vector.tensor_scalar(XT[:, kt, :], src, cols[:, at:at + 1], None, ALU.mult)
                        else:
                            sh = (0 if t % 3 == 0 else 16) + kt
                            ins = nc.vector.tensor_scalar(XT[:, kt, :], src, xscale[:, kt:kt + 1], modc[:, sh:sh + 1],
                                                          ALU.mult, ALU.add)
                    ins.then_inc(xt_ready, 1)

            def add_gated(gate, s, count):
                dve.wait_ge(s, count)
                link(nc.vector.tensor_tensor(YB, YB, gate[:, :].unsqueeze(1).broadcast_to([P, NB, D]), ALU.mult))
                nc.vector.tensor_tensor(X[:, :, :], X[:, :, :], YB, ALU.add).then_inc(x_ready, 1)

            def add_normed(row, number, factor):
                dve.wait_ge(res_sq, 2 * number)
                inverse_root((rstd[:, 4:6], ss[:, 4:6], D))
                for b in range(NB):
                    link(nc.vector.scalar_tensor_tensor(YB[:, b, :], YB[:, b, :], rstd[:, 4 + b:5 + b], row[:, :],
                                                        ALU.mult, ALU.mult))
                for b in range(NB):
                    ins = nc.vector.scalar_tensor_tensor(X[:, b, :], YB[:, b, :], factor, X[:, b, :], ALU.mult, ALU.add)
                ins.then_inc(x_ready, 1)

            def h_product(s_in, s_out, count, par):
                dve.wait_ge(s_in, count)
                nc.vector.tensor_tensor(hbuf[:, par, :], sgt[:, par, :], ps[:, 4 + par, FW:2 * FW], ALU.mult).then_inc(s_out, 1)

            def ffn(i):
                h0 = 2 * FF_STEPS * i
                h_product(silu_ready, h_ready, h0 + 1, 0)
                h_product(silu_ready, h_ready, h0 + 2, 1)
                if i == 0:
                    ada_step(26)
                    ada_step(27)

                def step(n, turn, s):
                    k = turn * 4 + (h0 + 2 + 2 * s)
                    h_product(silu_ready, h_ready, k + 1, 0)
                    h_product(silu_ready, h_ready, k + 2, 1)
                    if i == 0:
                        for a in range(28 + 2 * s, 30 + 2 * s):
                            ada_step(a, turn, turn + 1)

                stream_turns(dve, FF_STEPS - 1, 3, 2, step)

            def bias_table(u):
                at = 0 if u.b == 0 else 512
                if u.kind in "AC":
                    return alibi[:, at:at + 4 * u.nk].rearrange("p (s k) -> p s k", s=4)
                if u.kind == "D":
                    return band[:, at:at + 4 * u.nk].rearrange("p (s k) -> p s k", s=4)
                if u.kind == "B":
                    at = 0 if u.b == 0 else 128
                    return cmask[:, at:at + u.nk].unsqueeze(1).broadcast_to([P, 4, u.nk])
                return (na_bias if u.kind == "N" else dil_bias)[:, u.b, u.g.half]

            def bias(u):
                par = u.su % 2
                dve.wait_ge(scores, u.su + 1)
                if u.kind == "D" and u.layer == 1 and u.b == 0:
                    dve.wait_ge(layer_in, 16 * 3)
                src = ps[:, 2 * par:2 * par + 2, :].rearrange("p j (s k) -> p (j s) k", s=2)[:, :, 0:u.nk]
                scale = {"A": 32 ** -0.5, "B": 96 ** -0.5}.get(u.kind, HD ** -0.5)
                link(nc.vector.scalar_tensor_tensor(src, src, scale, bias_table(u), ALU.mult, ALU.add))
                if u.kind == "C":
                    link(nc.vector.tensor_tensor(src, src, SEL[u.b].unsqueeze(1).broadcast_to([P, 4, u.nk]), ALU.add))
                nc.vector.tensor_reduce(nmax[:, par, :], src, AX_X, ALU.max, negate=True).then_inc(biased, 1)

            def index_add(u):
                par, b, nk = u.su % 2, u.b, u.nk
                work = [PROJ[:, i, C_WORK:C_WORK + nk] for i in range(2)]
                dve.wait_ge(probs, u.su + 1)
                for h in range(4):
                    src = PR[:, par, head_slot(h), 0:nk]
                    at = 0 if b == 0 else 128
                    prev = cmask[:, at:at + nk] if u.part == 0 and h == 0 else work[0]
                    ins = nc.vector.scalar_tensor_tensor(work[0], src, w16[:, b, 4 * u.part + h:4 * u.part + h + 1], prev,
                                                         ALU.mult, ALU.add)
                    if h < 3:
                        link(ins)
                ins.then_inc(idx_added, 1)
                if u.part == 0:
                    dve.wait_ge(idx_added, u.idx + 1)
                    return
                dve.wait_ge(idx_added, u.idx + 1)
                for r in range(N_SEL // 8):
                    link(nc.vector.max(top8[:, :], work[r % 2]))
                    link(nc.vector.match_replace(work[1 - r % 2], top8[:, :], work[r % 2], TAKEN))
                link(nc.vector.tensor_scalar(SEL[b], work[0], TAKEN / 1.5, MASK, ALU.is_gt, ALU.mult))

            def finish(u):
                par = u.su % 2
                if u.kind == "I":
                    index_add(u)
                    return
                dve.wait_ge(probs, u.su + 1)
                done = [v.pu for v in UNITS[:max(u.su - 1, 0)] if v.pu is not None]
                if done:
                    dve.wait_ge(mixed, done[-1] + 1)
                link(nc.vector.reciprocal(rden[:, par, :], den[:, par, :]))
                if u.comb is None:
                    return
                link(nc.vector.tensor_scalar(rden[:, par, :], rden[:, par, :], lamc[:, 4 + u.layer:5 + u.layer], None, ALU.mult))
                for h in range(4):
                    s = head_slot(h)
                    p0 = PR[:, 1 - par, s, 0:u.nk]
                    ins = nc.vector.tensor_scalar(p0, p0, rden[:, 1 - par, h:h + 1], None, ALU.mult)
                link(ins)
                for h in range(4):
                    s = head_slot(h)
                    p0, p1 = PR[:, 1 - par, s, 0:u.nk], PR[:, par, s, 0:u.nk]
                    ins = nc.vector.scalar_tensor_tensor(p0, p1, rden[:, par, h:h + 1], p0, ALU.mult, ALU.add)
                ins.then_inc(combined, 1)

            def store(u):
                dve.wait_ge(o_ps, u.pu + 1)
                c = {"A": 0, "B": 256, "C": 512, "D": 768, "N": 0, "L": 512}[u.kind] + 256 * u.g.half
                dst = XN[:, u.b, c:c + 256].rearrange("p (h e) -> p h e", h=4)
                src = ps[:, 6, 0:256].rearrange("p (h e) -> p h e", h=4)
                if u.kind != "A":
                    nc.vector.tensor_tensor(dst, src, rden[:, u.su % 2, :].unsqueeze(2).broadcast_to([P, 4, HD]),
                                            ALU.mult).then_inc(mixed, 1)
                    return
                sq = FS[:, 1024:1280].rearrange("p (h e) -> p h e", h=4)
                link(nc.vector.tensor_copy(dst, src))
                link(nc.vector.tensor_tensor(sq, dst, dst, ALU.mult))
                link(nc.vector.tensor_reduce(rstd[:, 4:8], sq, AX_X, ALU.add))
                inverse_root((rstd[:, 4:8], rstd[:, 4:8], HD))
                link(nc.vector.tensor_tensor(dst, dst, rstd[:, 4:8].unsqueeze(2).broadcast_to([P, 4, HD]), ALU.mult))
                nc.vector.tensor_tensor(dst, dst, gdiff[:, u.layer, :].unsqueeze(1).broadcast_to([P, 4, HD]),
                                        ALU.mult).then_inc(mixed, 1)

            def rope(x, b):
                n = x.shape[1]
                cos = cossin[:, b, 0, :].unsqueeze(1).broadcast_to([P, n, 16])
                sin = cossin[:, b, 1, :].unsqueeze(1).broadcast_to([P, n, 16])
                x1, x2 = x[:, :, 0:16], x[:, :, 16:32]
                nc.vector.tensor_tensor(TR[:, 0, 0:n], x1, cos, ALU.mult)
                nc.vector.tensor_tensor(TR[:, 1, 0:n], x2, sin, ALU.mult)
                nc.vector.tensor_tensor(TR[:, 2, 0:n], x1, sin, ALU.mult)
                link(nc.vector.tensor_tensor(TR[:, 3, 0:n], x2, cos, ALU.mult))
                nc.vector.tensor_tensor(x1, TR[:, 0, 0:n], TR[:, 1, 0:n], ALU.subtract)
                link(nc.vector.tensor_tensor(x2, TR[:, 2, 0:n], TR[:, 3, 0:n], ALU.add))

            def prepare(g):
                if g.kind == "B":
                    dve.wait_ge(b_sq, 4 * (g.layer + 1))
                    inverse_root((rstd[:, 0:2], ss[:, 0:2], 256), (rstd[:, 2:4], ss[:, 2:4], 128))
                    for i, (c, w) in enumerate(((B_QD, 256), (B_KVD, 128))):
                        for b in range(NB):
                            ins = nc.vector.tensor_scalar(PROJ[:, b, c:c + w], PROJ[:, b, c:c + w],
                                                          rstd[:, 2 * i + b:2 * i + b + 1], None, ALU.mult)
                    ins.then_inc(b_normed, 1)
                    dve.wait_ge(filled, g.fill0 + 6)
                    for b in range(NB):
                        q = PROJ[:, b, B_UQ:B_UQ + 384].rearrange("p (h n) -> p h n", h=4)
                        rope(q[:, :, 64:96], b)
                        rope(PROJ[:, b, B_KR:B_KR + 32].unsqueeze(1), b)
                        kv = PROJ[:, b, B_UKV:B_UKV + 512].rearrange("p (h n) -> p h n", h=4)
                        nc.vector.tensor_copy(KB[:, b, :, 0:64], kv[:, :, 0:64])
                        ins = nc.vector.tensor_copy(KB[:, b, :, 64:96],
                                                    PROJ[:, b, B_KR:B_KR + 32].unsqueeze(1).broadcast_to([P, 4, 32]))
                    ins.then_inc(b_roped, 1)
                if g.kind == "C":
                    dve.wait_ge(fill_ps, g.fill0)
                    nc.vector.memset(KI4, 0.0)
                    for b in range(NB):
                        nc.vector.tensor_scalar(w16[:, b, :], PROJ[:, b, C_WI:C_WI + 8], (8 * 32) ** -0.5, None, ALU.mult)
                        ins = nc.vector.tensor_copy(PROJ[:, b, C_KIREP:C_KIREP + P].rearrange("p (h n) -> p h n", h=4),
                                                    PROJ[:, b, C_KI:C_KI + 32].unsqueeze(1).broadcast_to([P, 4, 32]))
                    ins.then_inc(c_ready, 1)

            def attention(layer):
                us = units_of(layer)
                dve.wait_ge(gemm_out, 2 * sum(GEMM_GROUPS[:2 * layer + 1]))
                bias(us[0])
                for n, u in enumerate(us):
                    if u.first_of_group and u.g.gi + 1 < len(GROUPS) and GROUPS[u.g.gi + 1].layer == layer:
                        prepare(GROUPS[u.g.gi + 1])
                    if n + 1 < len(us) and us[n + 1].kind != "I":
                        bias(us[n + 1])
                    finish(u)
                    if n >= 1 and us[n - 1].pu is not None:
                        store(us[n - 1])
                store(us[-1])

            def route():
                dve.wait_ge(late_in, 16 * 5)
                nc.vector.memset(r_logit, -3.0e38)
                link(nc.vector.memset(r_take, -3.0e38))
                dve.wait_ge(route_ps, 1)
                link(nc.vector.tensor_copy(r_logit[:, :, 0:8], ps[:, 7, 0:16].rearrange("p (b n) -> p b n", b=NB)))
                for b in range(NB):
                    ins = nc.vector.max(r_top[:, b, :], r_logit[:, b, 0:8])
                link(ins)
                nc.vector.tensor_scalar(r_nv1, r_top[:, :, 0:1].rearrange("p b a -> p (b a)"), -1.0, None, ALU.mult).then_inc(route_max, 1)
                link(nc.vector.tensor_copy(r_take[:, :, 0:2], r_top[:, :, 0:2]))
                for b in range(NB):
                    ins = nc.vector.match_replace(r_marked[:, b, :], r_take[:, b, :], r_logit[:, b, :], 3.0e38)
                link(ins)
                nc.vector.tensor_scalar(r_sel, r_marked[:, :, 0:8], 1.0e38, None, ALU.is_ge).then_inc(route_sel, 1)
                dve.wait_ge(route_exp, 1)
                link(nc.vector.tensor_scalar(r_den, r_e2, 1.0, None, ALU.add))
                link(nc.vector.reciprocal(r_den, r_den))
                dve.wait_ge(route_sel, 1)
                link(nc.vector.tensor_tensor(r_comb, r_exp, r_sel, ALU.mult))
                link(nc.vector.tensor_tensor(r_comb, r_comb, r_den.unsqueeze(2).broadcast_to([P, NB, 8]), ALU.mult))
                dve.wait_ge(rank_ps, 1)
                link(nc.vector.scalar_tensor_tensor(r_rank, ps[:, 7, 0:16].rearrange("p (b n) -> p b n", b=NB), 1000.0,
                                                    r_sel, ALU.add, ALU.mult))
                link(nc.vector.tensor_scalar(r_rank, r_rank, -1000.0, None, ALU.add))
                link(nc.vector.tensor_reduce(r_cnt[0:1, :], ps[0:1, 7, 16:24], AX_X, ALU.max))
                link(nc.vector.memset(YB, 0.0))
                nc.vector.tensor_scalar(flag[:, :], r_cnt[0:1, :], float(P), None, ALU.is_gt).then_inc(route_ready, 1)

            def experts(m):
                with dve.Fori(0, EXPERTS) as e:
                    k_e = e * EX_STEPS
                    nc.vector.tensor_scalar(r_rk, r_rank[:, :, bass.ds(e, 1)].rearrange("p b a -> p (b a)"),
                                            -float(P) * m["sweep"], None, ALU.add)
                    nc.vector.tensor_copy(r_cb, r_comb[:, :, bass.ds(e, 1)].rearrange("p b a -> p (b a)")).then_inc(m["sel_copied"], 1)
                    dve.wait_ge(m["sel_copied"], e + 1)
                    for b in range(NB):
                        ins = nc.vector.tensor_scalar(PSEL[:, b, :], iota, r_rk[:, b:b + 1], None, ALU.is_equal)
                    ins.then_inc(m["psel"], 1)
                    dve.wait_ge(m["psel"], e + 1)
                    for b in range(NB):
                        ins = nc.vector.tensor_scalar(WSEL[:, b, :], PSEL[:, b, :], r_cb[:, b:b + 1], None, ALU.mult)
                    ins.then_inc(m["wsel"], 1)
                    with dve.Fori(0, EX_STEPS // 2) as t:
                        for s in range(2):
                            h_product(m["silu_ready"], m["h_ready"], t * 2 + k_e + (1 + s), s)
                    for b in range(NB):
                        dve.wait_ge(m["sc_ps"], e * 2 + (b + 1))
                        nc.vector.tensor_tensor(YB[:, b, :], YB[:, b, :], ps[:, 2:4, :].rearrange("p j n -> p (j n)"),
                                                ALU.add).then_inc(m["sc_added"], 1)

            nc.vector.memset(zero[:, :], 0.0).then_inc(zero_ready, 1)
            dve.wait_ge(const_in, 16 * N_CONST)
            v = lam_in.rearrange("p l (i a n) -> p l i a n", i=2, a=2)
            for l in range(LAYERS):
                for i in range(2):
                    link(nc.vector.tensor_tensor(lam_pr[:, l, 32 * i:32 * (i + 1)], v[:, l, i, 0, :], v[:, l, i, 1, :], ALU.mult))
            nc.vector.tensor_reduce(lamc[:, 4:8], lam_pr[:, :, :].rearrange("p l (i n) -> p (l i) n", i=2), AX_X,
                                    ALU.add).then_inc(lam_exp_in, 1)
            dve.wait_ge(lam_exp_out, 1)
            for l in range(LAYERS):
                lam_init = 0.8 - 0.6 * math.exp(-0.3 * l)
                link(nc.vector.tensor_tensor(lamc[:, 4 + l:5 + l], lamc[:, 2 * l + 1:2 * l + 2], lamc[:, 2 * l:2 * l + 1],
                                             ALU.subtract))
                link(nc.vector.tensor_scalar(lamc[:, 4 + l:5 + l], lamc[:, 4 + l:5 + l], -lam_init, None, ALU.add))
                link(nc.vector.tensor_scalar(gdiff[:, l, :], gdiff[:, l, :], 1.0 - lam_init, None, ALU.mult))
            dve.wait_ge(csilu_ready, 1)
            for a in range(ADA_EARLY):
                ada_step(a)
            for layer in range(LAYERS):
                mod_columns(0, layer, 1 + 6 * layer)
                if layer == 1:
                    mod_rows(gate_mix, row0, 8)
                    mod_columns(3, layer, 10)
                    mod_rows(gate_ffn, row1, 11)
                set_xscale(0, layer)
                normalise(3 * layer)
                copy_xt(3 * layer)
                if layer == 0:
                    for a in range(ADA_EARLY, ADA_MID):
                        ada_step(a)
                    mod_rows(gate_mix, gate_mix, 2)
                    mod_columns(3, layer, 4)
                    mod_rows(gate_ffn, gate_ffn, 5)
                attention(layer)
                copy_xt(3 * layer + 1)
                add_gated(gate_mix, gemm_out, 2 * sum(GEMM_GROUPS[:2 * layer + 2]))
                set_xscale(3, layer)
                normalise(3 * layer + 2)
                copy_xt(3 * layer + 2)
                if layer == 0:
                    ffn(0)
                    add_gated(gate_ffn, y_out, 2)
                else:
                    route()
                    experts(moe_sems[0])
                    dve.wait_ge(route_ready, 1)
                    over = dve.value_load(flag[0:1, 0:1], min_val=0, max_val=1)
                    with dve.If(over > 0):
                        experts(moe_sems[1])
                        dve.wait_ge(moe_sems[1]["sc_added"], 2 * EXPERTS)
                    add_gated(gate_ffn, moe_sems[0]["sc_added"], 2 * EXPERTS)
            dve.wait_ge(res_sq, 2)
            dve.wait_ge(rows_in, 32)
            inverse_root((rstd[:, 4:6], ss[:, 4:6], D))
            for b in range(NB):
                ins = nc.vector.scalar_tensor_tensor(X[:, b, :], X[:, b, :], rstd[:, 4 + b:5 + b], row0[:, :], ALU.mult, ALU.mult)
            ins.then_inc(x_ready, 1)
            for b in range(NB):
                for g in range(2):
                    link(nc.vector.tensor_tensor(dil_bias[:, b, g], dil_bias[:, b, g],
                                                 lnm[:, b, :].unsqueeze(1).broadcast_to([P, 4, T]), ALU.add))
            normalise(6)
            copy_xt(6)
            ffn(1)
            add_normed(row1, 2, 0.5)
            normalise(7)
            copy_xt(7)
            attention(2)
            normalise(8)
            copy_xt(8)
            dve.wait_ge(rows_in2, 32)
            add_normed(gate_mix, 3, 1.0)
            normalise(9)
            copy_xt(9)
            ffn(2)
            add_normed(gate_ffn, 4, 0.5)



def product_chunks(w, groups):
    w = np.pad(w, ((0, 0), (0, groups * 512 - w.shape[1])))
    return w.reshape(2, 4, P, groups, 512).transpose(3, 0, 2, 1, 4).reshape(2 * groups, P, CHW)


def ffn_chunks(w1, w3, w2):
    steps = w1.shape[1] // FW
    up = np.stack([w1.reshape(2, 4, P, steps, FW), w3.reshape(2, 4, P, steps, FW)], axis=4)
    up = up.transpose(3, 0, 2, 1, 4, 5).reshape(steps, 2, P, CHW)
    down = w2.reshape(steps, 2, P, D).transpose(0, 2, 1, 3).reshape(steps, 1, P, CHW)
    out = np.empty((3 * steps, P, CHW), np.float32)
    out[0:2] = up[0]
    mid = out[2:-1].reshape(steps - 1, 3, P, CHW)
    mid[:, 0:2] = up[1:]
    mid[:, 2:3] = down[:-1]
    out[-1] = down[-1, 0]
    return out


def columns(v):
    return v.reshape(-1, P).T


def slotted(table):
    order = [h for s in range(4) for h in range(4) if head_slot(h) == s]
    t = table.reshape(-1, 4, NB, P, T)[:, order]
    return t.transpose(3, 2, 0, 1, 4)


def causal_pack(t):
    return np.concatenate([t[:, 0, 0, :, 0:P].reshape(P, -1), t[:, 1, 0].reshape(P, -1)], axis=1)


def arrays_of(i):
    i = {k: np.asarray(v) for k, v in i.items()}
    q, k = np.arange(T)[:, None], np.arange(T)[None, :]
    allowed = k // 64 <= q // 64
    slopes = (2.0 ** (-8.0 * np.arange(1, 5) / 4)).astype(np.float32)
    alibi = np.where(allowed, -slopes[:, None, None] * np.abs(q - k).astype(np.float32), np.float32(MASK)).astype(np.float32)
    cmask = np.where(allowed, np.float32(0), np.float32(MASK)).astype(np.float32)
    cm = cmask.reshape(NB, P, T)
    rel = np.clip(q - k, -128, 128) + 128
    band = np.stack([causal_pack(slotted(np.where(allowed, i["band_rel_bias"][l][:, rel], np.float32(MASK)))) for l in range(LAYERS)])
    qr, qc, kr, kc = q // 64, q % 64, k // 64, k % 64
    start = np.clip(qc - 8, 0, 48)
    near = (kc >= start) & (kc < start + 16)
    na = np.where(near, i["na_rel_bias_2"][0][:, kr - qr + 7, np.clip(kc - qc + 15, 0, 30)], np.float32(MASK))
    off = k - q
    member = [np.abs(off) <= 64, off % 4 == 0, off % 16 == 0]
    times = sum(m.astype(np.int64) for m in member)
    dist = np.abs(off)
    large = 8 + (np.log(np.maximum(dist, 1).astype(np.float32) / 8) / math.log(1024 / 8) * 8).astype(np.int32)
    bucket = np.where(off > 0, 16, 0) + np.where(dist < 8, dist, np.minimum(large, 15))
    dil = np.where(times > 0, i["t5_rel_bias_2"][:, bucket], np.float32(MASK))
    lnm = np.log(np.maximum(times, 1)).astype(np.float32).reshape(NB, P, T).transpose(1, 0, 2).reshape(P, NB * T)
    inv = np.float32(10000.0) ** (-np.arange(0, 32, 2, dtype=np.float32) / np.float32(32))
    ang = np.arange(T, dtype=np.float32)[:, None] * inv[None, :]
    cossin = np.stack([np.cos(ang), np.sin(ang)], axis=1).reshape(NB, P, 2, 16).transpose(1, 0, 2, 3).reshape(P, 64)
    ada_b = i["ada_b"].reshape(LAYERS, 6, D)
    stream = np.concatenate([
        product_chunks(i["w_in"][0], 6), product_chunks(i["w_out"][0], 2),
        ffn_chunks(i["ffn_w1"][0], i["ffn_w3"][0], i["ffn_w2"][0]),
        product_chunks(i["w_in"][1], 6), product_chunks(i["w_out"][1], 2),
        *[ffn_chunks(i["moe_w1"][0, e], i["moe_w3"][0, e], i["moe_w2"][0, e]) for e in range(EXPERTS)],
        ffn_chunks(i["ffn1_w_gate_2"][0], i["ffn1_w_up_2"][0], i["ffn1_w_down_2"][0]),
        product_chunks(i["w_qkv_2"][0], 6), product_chunks(i["w_out_2"][0], 2),
        ffn_chunks(i["ffn2_w_gate_2"][0], i["ffn2_w_up_2"][0], i["ffn2_w_down_2"][0])])
    ada = i["ada_w"].reshape(LAYERS, 4, 2, P, 6, D).transpose(0, 4, 1, 3, 2, 5).reshape(ADA_CHUNKS, P, CHW)
    cols = np.concatenate([columns(v) for v in (
        i["mix_norm_g"], i["ffn_norm_g"], i["ffn1_pre_g_2"], i["mix_pre_g_2"], i["ffn2_pre_g_2"],
        np.concatenate([i["na_out_g_2"][0], i["dil_out_g_2"][0]]), ada_b, i["mla_q_norm_g"], i["mla_kv_norm_g"], i["c"])], axis=1)
    rows = np.stack([ada_b[0, 2], ada_b[0, 5], ada_b[1, 2], ada_b[1, 5], i["final_norm_g"], i["ffn1_post_g_2"][0],
                     i["mix_post_g_2"][0], i["ffn2_post_g_2"][0]])
    tri = (np.arange(P)[:, None] < np.arange(P)[None, :]).astype(np.float32)
    iota = np.broadcast_to(np.arange(P, dtype=np.float32), (P, P))
    out = dict(
        x=i["x"], stream=stream, ada=ada, cols=cols, rows=rows,
        lam=i["diff_lambda"].reshape(1, 256), gdiff=i["diff_norm_g"].reshape(1, 128),
        unit=np.concatenate([np.eye(P), np.ones((P, P))], axis=1), cossin=cossin,
        alibi=causal_pack(slotted(alibi)), cmask=np.concatenate([cm[0, :, 0:P], cm[1]], axis=1), band=band,
        uq=i["mla_w_uq"].reshape(LAYERS, 2, P, 384).transpose(0, 2, 1, 3).reshape(LAYERS, P, 768), ukv=i["mla_w_ukv"],
        na=slotted(na).reshape(P, -1), dil=slotted(dil).reshape(P, -1), lnm=lnm,
        tri_iota=np.concatenate([tri, iota], axis=1),
        router=i["moe_router"][0].reshape(KT, P, 8).transpose(1, 0, 2).reshape(P, 64))
    return {n: np.ascontiguousarray(a, dtype=np.float32) for n, a in out.items()}


def kernel(**inputs):
    import concourse.bacc as bacc
    from concourse.bass_utils import run_bass_kernel_spmd

    nc = bacc.Bacc("TRN2", target_bir_lowering=False, num_devices=1)
    arrays = {f"in_{n}": a for n, a in arrays_of(inputs).items()}
    aps = {n[3:]: nc.dram_tensor(n, a.shape, F32, kind="ExternalInput").ap() for n, a in arrays.items()}
    aps["out"] = nc.dram_tensor("out", (1, T, D), F32, kind="ExternalOutput").ap()
    program(nc, aps)
    r = run_bass_kernel_spmd(nc, [arrays], core_ids=[0])
    return r.results[0]["out"]
```

```python
import math
from contextlib import ExitStack

import concourse.bass as bass
import numpy as np
from concourse import mybir

F32 = mybir.dt.float32
F32R = mybir.dt.float32r
BF16 = mybir.dt.bfloat16
I32 = mybir.dt.int32
ALU = mybir.AluOpType
ACT = mybir.ActivationFunctionType
AX_X = mybir.AxisListType.X

P = 128
T = 256
NB = T // P
D = 1024
KT = D // P
CHW = 2048
RING = 6
PIECE = CHW // 2
SPLITS = 3
ADA_RING = 2
LAYERS = 2
D_IN, D_IN_PAD = 3016, 3072
FW = 256
FF_STEPS = 2816 // FW
EX_STEPS = 3584 // FW
EXPERTS = 8
EPS = 1e-6
MASK = -1e30
TAKEN = -3.0e38
N_SEL = 64
HD = 64

A_Q, A_K, A_V, B_QD, B_KVD, B_KR = 0, 256, 512, 768, 1024, 1152
C_Q, C_K, C_V, C_QI, C_KI, C_WI, D_Q, D_K, D_V = 1184, 1440, 1696, 1952, 2208, 2240, 2248, 2504, 2760
B_UQ = B_QD
B_UKV = A_Q
C_WORK = B_QD + P
C_KIREP = B_QD

GEMM_GROUPS = [6, 2, 6, 2, 6, 2]
FF_CHUNKS, EX_CHUNKS = 3 * FF_STEPS, 3 * EX_STEPS
IN0_CHUNK = 0
OUT0_CHUNK = IN0_CHUNK + 12
FFN0_CHUNK = OUT0_CHUNK + 4
IN1_CHUNK = FFN0_CHUNK + FF_CHUNKS
OUT1_CHUNK = IN1_CHUNK + 12
MOE_CHUNK = OUT1_CHUNK + 4
FFN1_CHUNK = MOE_CHUNK + EXPERTS * EX_CHUNKS
QKV_CHUNK = FFN1_CHUNK + FF_CHUNKS
OUT2_CHUNK = QKV_CHUNK + 12
FFN2_CHUNK = OUT2_CHUNK + 4
N_CHUNKS = FFN2_CHUNK + FF_CHUNKS
GEMM_CHUNK = [IN0_CHUNK, OUT0_CHUNK, IN1_CHUNK, OUT1_CHUNK, QKV_CHUNK, OUT2_CHUNK]
FFN_CHUNK = [FFN0_CHUNK, FFN1_CHUNK, FFN2_CHUNK]
EX_TOTAL = EXPERTS * EX_CHUNKS
assert EX_CHUNKS % RING == 0 and 2 * EX_TOTAL % SPLITS == 0 and 2 * RING % SPLITS == 0
N_WORK = 8448
LOW_AT, XTL_AT = SPLITS * PIECE, 2 * SPLITS * PIECE
HTH_AT, HTL_AT = 5120, 5632
ADA_AHEAD = [(0, 0), (0, CHW), (0, 2 * CHW), (1, 0), (1, CHW), (1, 2 * CHW)]

ADA_CHUNKS = LAYERS * 6 * 4
ADA_EARLY = 8
ADA_MID = 26

COL = {}
_at = 0
for _name, _n in (("mix_g", 16), ("ffn_g", 16), ("f1_g", 8), ("mp_g", 8), ("f2_g", 8), ("out_g", 8), ("ada_b", 96),
                  ("q_g", 4), ("kv_g", 2), ("c", 8)):
    COL[_name] = _at
    _at += _n
N_COLS = _at

XG_AT, YE_AT, PS_AT, WS_AT, CT_AT = 2048, 3072, 4096, 4352, 4608
Z_WORDS = 6 * D + ADA_RING * CHW
NA_AT, DIL_AT, TRI_AT, IOTA_AT, RW_AT, LNM_AT, RT_AT = 0, 4096, 8192, 8320, 8448, 8512, 9024
FS_WORDS = 1536


def head_slot(h):
    return (h % 2) * 2 + h // 2


class Group:
    def __init__(self, kind, half, layer, gi):
        self.kind, self.half, self.layer, self.gi = kind, half, layer, gi
        self.units, self.fill0, self.n_fills = [], 0, 0


class Unit:
    def __init__(self, kind, b, part, g, su):
        self.kind, self.b, self.part, self.g, self.layer, self.su = kind, b, part, g, g.layer, su
        self.nk = P * (b + 1) if g.layer < LAYERS else T
        self.bi = self.pu = self.idx = self.comb = None
        self.first_of_group = not g.units


def attention_plan():
    groups, units = [], []
    count = {"su": 0, "bi": 0, "pu": 0, "fill": 0, "idx": 0, "comb": 0}

    def take(name):
        count[name] += 1
        return count[name] - 1

    for layer in range(LAYERS + 1):
        kinds = "ABCD" if layer < LAYERS else ["N0", "N1", "L0", "L1"]
        first = len(groups)
        for kind in kinds:
            groups.append(Group(kind[0], int(kind[1]) if len(kind) > 1 else 0, layer, len(groups)))
        for g in groups[first:]:
            g.fill0 = count["fill"]
            g.n_fills = {"A": 2, "B": 10, "C": 4, "D": 2, "N": 2, "L": 2}[g.kind]
            count["fill"] += g.n_fills
        for g in groups[first:]:
            todo = {"A": [("A", b, c) for b in range(NB) for c in range(2)],
                    "C": [("I", b, hg) for b in range(NB) for hg in range(2)] + [("C", b, 0) for b in range(NB)]}
            for kind, b, part in todo.get(g.kind, [(g.kind, b, 0) for b in range(NB)]):
                u = Unit(kind, b, part, g, take("su"))
                if kind == "I":
                    u.idx = take("idx")
                else:
                    u.bi = take("bi")
                    if not (kind == "A" and part == 0):
                        u.pu = take("pu")
                    if kind == "A" and part == 1:
                        u.comb = take("comb")
                g.units.append(u)
                units.append(u)
    return groups, units


GROUPS, UNITS = attention_plan()
N_CONST = 12
SPLIT_NO = {t: t if t < 5 else t - 1 for t in range(10) if t != 5}
NORM_NO = {0: 1, 2: 2, 3: 3, 5: 4, 6: 5, 7: 6, 8: 7, 9: 8}
SQUARES = {0: 2, 2: 4, 3: 6, 5: 8, 6: 10, 7: 12, 8: 16, 9: 18}
X_READY = {2: 1, 3: 2, 5: 3, 6: 5, 7: 6, 9: 7}


def release(u):
    if u.kind == "I":
        return "idx", u.idx + 1
    if u.kind == "A" and u.part == 1:
        return "comb", u.comb + 1
    return "pT", (UNITS[u.su + 1] if u.kind == "A" else u).pu + 1


def piece_no(chunk, half=0):
    return 2 * (chunk - (EX_TOTAL if chunk >= FFN1_CHUNK else 0)) + half


def units_of(layer):
    return [u for u in UNITS if u.layer == layer]


def pu_end(layer):
    return max(u.pu for u in UNITS if u.layer == layer and u.pu is not None) + 1


def stream_turns(eng, n_steps, per_step, first_chunk, body):
    per_turn = RING // per_step
    turns = n_steps // per_turn
    if turns > 1:
        with eng.Fori(0, turns) as turn:
            for s in range(per_turn):
                body(first_chunk + s * per_step, turn, s)
    else:
        turns = 0
    for s in range(turns * per_turn, n_steps):
        body(first_chunk + s * per_step, 0, s)


def program(nc, d):
    with ExitStack() as ctx:
        def sb(name, shape, dt=F32):
            return ctx.enter_context(nc.sbuf_tensor(name, shape, dt))

        def sem(name):
            return ctx.enter_context(nc.semaphore(name))

        arena = sb("arena", [P, N_WORK + NB * D_IN_PAD])
        arena_at = nc.sbuf_base - 4 * (N_WORK + NB * D_IN_PAD)

        def split(name, shape, word):
            return nc.alloc_sbuf_tensor_at(name, [P] + shape, F32R, offset=arena_at + 4 * word)

        WH = split("weights_high", [SPLITS, PIECE], 0)
        WL = split("weights_low", [SPLITS, PIECE], LOW_AT)
        XTL = split("xt_low", [KT, T], XTL_AT)
        hTH = split("hT_high", [NB, 2, P], N_WORK + HTH_AT)
        hTL = split("hT_low", [NB, 2, P], N_WORK + HTL_AT)
        XTH = sb("xt_high", [P, KT, T], F32R)
        ring = sb("ring", [P, RING, CHW])
        X = sb("X", [P, NB, D])
        XN = sb("XN", [P, NB, D])
        gate_mix = sb("gate_mix", [P, D])
        gate_ffn = sb("gate_ffn", [P, D])
        row0 = sb("row0", [P, D])
        row1 = sb("row1", [P, D])
        Z = sb("Z", [P, Z_WORDS])
        alibi = sb("alibi", [P, 1536])
        band = sb("band", [P, 1536])
        cmask = sb("cmask", [P, 384])
        FS = sb("FS", [P, FS_WORDS])
        unit = sb("unit", [P, 2 * P])
        ident, ones = unit[:, 0:P], unit[:, P:2 * P]
        cols = sb("cols", [P, N_COLS])
        cossin = sb("cossin", [P, NB, 2, 16])
        gdiff = sb("gdiff", [P, LAYERS, HD])
        modc = sb("modc", [P, 32])
        xscale = sb("xscale", [P, KT])
        csilu = sb("csilu", [P, KT])
        ss = sb("ss", [P, 8])
        rstd = sb("rstd", [P, 8])
        nmax = sb("nmax", [P, 2, 4])
        den = sb("den", [P, 2, 4])
        rden = sb("rden", [P, 2, 4])
        lamc = sb("lamc", [P, 8])
        w16 = sb("w16", [P, NB, 8])
        top8 = sb("top8", [P, 8])
        minus_half = sb("minus_half", [P, 8])
        flag = sb("flag", [1, 1], I32)
        ps = ctx.enter_context(nc.psum_tensor("ps", [P, 8, 512], F32))

        QK = arena[:, 0:4096].rearrange("p (g n) -> p g n", g=2)
        PR = arena[:, 4096:6144].rearrange("p (u s k) -> p u s k", u=2, s=4)
        PT = arena[:, 6144:7168].rearrange("p (h b q) -> p h b q", h=4, b=NB)
        UQ = arena[:, 7168:7936].rearrange("p (k n) -> p k n", k=2)
        UKV = arena[:, 7936:8448]
        proj_words = arena[:, N_WORK:]
        PROJ = proj_words.rearrange("p (b n) -> p b n", b=NB)
        XT = proj_words[:, 0:KT * T].rearrange("p (k n) -> p k n", k=KT)
        YB = proj_words[:, 0:NB * D].rearrange("p (b n) -> p b n", b=NB)
        XG = proj_words[:, XG_AT:XG_AT + D].rearrange("p (k s) -> p k s", k=KT)
        YE = proj_words[:, YE_AT:YE_AT + D]
        PSEL = proj_words[:, PS_AT:PS_AT + T].rearrange("p (b s) -> p b s", b=NB)
        WSEL = proj_words[:, WS_AT:WS_AT + T].rearrange("p (b s) -> p b s", b=NB)
        CT = proj_words[:, CT_AT:CT_AT + T].rearrange("p (b s) -> p b s", b=NB)
        ada_acc = Z[:, 0:6 * D].rearrange("p (m n) -> p m n", m=6)
        ada_ring = Z[:, 6 * D:Z_WORDS].rearrange("p (s n) -> p s n", s=ADA_RING)
        ada_places = [(proj_words if in_proj else arena)[:, word:word + CHW] for in_proj, word in ADA_AHEAD]
        na_bias = Z[:, NA_AT:NA_AT + 4096].rearrange("p (b g h k) -> p b g h k", b=2, g=2, h=4)
        dil_bias = Z[:, DIL_AT:DIL_AT + 4096].rearrange("p (b g h k) -> p b g h k", b=2, g=2, h=4)
        lnm = Z[:, LNM_AT:LNM_AT + 512].rearrange("p (b k) -> p b k", b=2)
        tri = Z[:, TRI_AT:TRI_AT + P]
        iota = Z[:, IOTA_AT:IOTA_AT + P]
        router = Z[:, RW_AT:RW_AT + 64].rearrange("p (k e) -> p k e", k=KT)

        def rt(i, n):
            return Z[:, RT_AT + i:RT_AT + i + n]

        r_logit = rt(0, 32).rearrange("p (b n) -> p b n", b=NB)
        r_marked = rt(32, 32).rearrange("p (b n) -> p b n", b=NB)
        r_top = rt(64, 16).rearrange("p (b n) -> p b n", b=NB)
        r_take = rt(80, 16).rearrange("p (b n) -> p b n", b=NB)
        r_sel = rt(96, 16).rearrange("p (b n) -> p b n", b=NB)
        r_exp = rt(112, 16).rearrange("p (b n) -> p b n", b=NB)
        r_comb = rt(128, 16).rearrange("p (b n) -> p b n", b=NB)
        r_rank = rt(144, 16).rearrange("p (b n) -> p b n", b=NB)
        r_nv1 = rt(160, 2)
        r_e2 = rt(162, 2)
        r_den = rt(164, 2)
        r_cnt = rt(166, 1)
        r_rk = rt(168, 2)
        r_cb = rt(170, 2)

        sgt = FS[:, 0:512].rearrange("p (b n) -> p b n", b=2)
        hbuf = FS[:, 512:1024].rearrange("p (b n) -> p b n", b=2)
        hT = FS[:, 1024:1536].rearrange("p (b f n) -> p b f n", b=2, f=2)
        KB = FS[:, 0:768].rearrange("p (b h n) -> p b h n", b=2, h=4)
        KI4 = FS[:, 0:1024].rearrange("p (h n) -> p h n", h=4)
        SEL = [FS[:, 1280:1408], FS[:, 1024:1280]]
        TR = FS[:, 1280:1536].rearrange("p (i h n) -> p i h n", i=4, h=4)
        junk = FS[:, 1280:1536]
        lam_in = FS[:, 0:256].rearrange("p (l n) -> p l n", l=LAYERS)
        lam_pr = FS[:, 256:384].rearrange("p (l n) -> p l n", l=LAYERS)
        zero = sb("zero", [1, P], BF16)
        finite = unit[0:1, :].bitcast(BF16)

        full = [sem(f"ring_full{i}") for i in range(RING)]
        chunk_used = sem("chunk_used")
        hi_ready, lo_ready, piece_done = sem("hi_ready"), sem("lo_ready"), sem("piece_done")
        xt_full, xt_hi, hT_hi, latent_in = (sem(n) for n in ("xt_full", "xt_hi", "hT_hi", "latent_in"))
        ada_ahead = [sem(f"ada_ahead{i}") for i in range(len(ADA_AHEAD))]
        full_o = [sem(f"ring_full_overflow{i}") for i in range(RING)]
        chunk_used_o = sem("chunk_used_overflow")
        ada_full = [sem(f"ada_full{i}") for i in range(ADA_RING)]
        ada_half, ada_used = sem("ada_half"), sem("ada_used")
        x_in, const_in, late_in, layer_in, rows_in, rows_in2 = (
            sem(n) for n in ("x_in", "const_in", "late_in", "layer_in", "rows_in", "rows_in2"))
        out_done = sem("out_done")
        zero_ready, csilu_ready, lam_exp_in, lam_exp_out = (sem(n) for n in ("zero_ready", "csilu_ready", "lam_exp_in", "lam_exp_out"))
        mod_ps, mod_ready, mod_cols = sem("mod_ps"), sem("mod_ready"), sem("mod_cols")
        sq_ready, xn_ready, xt_ps, xt_ready = (sem(n) for n in ("sq_ready", "xn_ready", "xt_ps", "xt_ready"))
        gemm_out = sem("gemm_out")
        silu_ready, h_ready, hT_ps, hT_ready = (sem(n) for n in ("silu_ready", "h_ready", "hT_ps", "hT_ready"))
        y_out = sem("y_out")
        res_sq, x_ready = sem("res_sq"), sem("x_ready")
        fill_ps, filled = sem("fill_ps"), sem("filled")
        b_sq, b_normed, b_roped, c_ready = (sem(n) for n in ("b_sq", "b_normed", "b_roped", "c_ready"))
        scores, biased, probs, combined, idx_added = (sem(n) for n in ("scores", "biased", "probs", "combined", "idx_added"))
        pT_ps, pT_ready, o_ps, mixed = (sem(n) for n in ("pT_ps", "pT_ready", "o_ps", "mixed"))
        route_ps, route_max, route_exp, route_sel, rank_ps, route_ready = (
            sem(n) for n in ("route_ps", "route_max", "route_exp", "route_sel", "rank_ps", "route_ready"))
        dve_chain, root_in, root_out, half_ready = (sem(n) for n in ("dve_chain", "root_in", "root_out", "half_ready"))
        moe_sems = []
        for sweep, tag in enumerate(("", "_overflow")):
            m = {n: sem("moe_" + n + tag) for n in (
                "sel_copied", "psel", "wsel", "xg_ps", "xg_ready", "ct_ps", "ct_ready", "up_ps", "silu_ready",
                "h_ready", "hT_ps", "hT_ready", "ye_ps", "ye_ready", "sc_ps", "sc_added")}
            m["full"], m["used"] = (full, chunk_used) if sweep == 0 else (full_o, chunk_used_o)
            m["sweep"] = sweep
            moe_sems.append(m)

        stream, ada = d["stream"], d["ada"]

        def slot_ready(eng, chunk, turn):
            eng.wait_ge(full[chunk % RING], turn * 16 + 16 * (chunk // RING + 1))

        def ring_full_wait(eng, m, local, turn):
            before = (MOE_CHUNK if m["sweep"] == 0 else 0) + local
            eng.wait_ge(m["full"][moe_slot(local)], turn * 16 + 16 * (before // RING + 1))

        def moe_slot(local):
            return (MOE_CHUNK + local) % RING

        block = ctx.enter_context(nc.Block())

        @block.sync
        def _(sp):
            sp.dma_start(X[:, :, :], d["x"].rearrange("a (b p) n -> p (a b) n", p=P)).then_inc(x_in, 16)

            def load_chunks(first, count):
                split_before = not MOE_CHUNK <= first - RING < FFN1_CHUNK

                def load(n, turn, s):
                    if split_before:
                        sp.wait_ge(lo_ready, turn * (2 * RING) + piece_no(n - RING, 2))
                    else:
                        sp.wait_ge(chunk_used, turn * RING + (n - RING - MOE_CHUNK + 1))
                    src = stream[bass.ds(turn * RING + n, 1)].rearrange("a p n -> (a p) n")
                    sp.dma_start(ring[:, n % RING, :], src).then_inc(full[n % RING], 16)
                stream_turns(sp, count, 1, first, load)

            for n in range(RING):
                if n == 2:
                    sp.wait_ge(ada_ahead[-1], 16)
                sp.dma_start(ring[:, n, :], stream[n]).then_inc(full[n], 16)
            load_chunks(RING, MOE_CHUNK)
            load_chunks(MOE_CHUNK + RING, EX_TOTAL - RING)

            sp.wait_ge(route_ready, 1)
            over = sp.value_load(flag[0:1, 0:1], min_val=0, max_val=1)
            with sp.If(over > 0):
                sp.wait_ge(chunk_used, EX_TOTAL)
                s0 = MOE_CHUNK % RING
                for n in range(RING):
                    sp.dma_start(ring[:, (s0 + n) % RING, :], stream[MOE_CHUNK + n]).then_inc(full_o[(s0 + n) % RING], 16)
                with sp.Fori(1, EXPERTS * EX_CHUNKS // RING) as turn:
                    for n in range(RING):
                        sp.wait_ge(chunk_used_o, turn * RING + (n - RING + 1))
                        src = stream[bass.ds(turn * RING + (MOE_CHUNK + n), 1)].rearrange("a p n -> (a p) n")
                        sp.dma_start(ring[:, (s0 + n) % RING, :], src).then_inc(full_o[(s0 + n) % RING], 16)
                sp.wait_ge(chunk_used_o, EXPERTS * EX_CHUNKS)
            load_chunks(FFN1_CHUNK, RING)
            load_chunks(FFN1_CHUNK + RING, N_CHUNKS - FFN1_CHUNK - RING)

            sp.wait_ge(x_ready, 8)
            sp.dma_start(d["out"].rearrange("a (b p) n -> p (a b) n", p=P), X[:, :, :]).then_inc(out_done, 16)
            sp.wait_ge(out_done, 16)

        @block.gpsimd
        def _(pool):
            def load_ada(a, turn=0):
                before = a - ADA_RING if a >= ADA_EARLY + ADA_RING else a - ADA_EARLY
                pool.wait_ge(ada_used, turn * ADA_RING + (before + 1))
                src = ada[bass.ds(turn * ADA_RING + a, 1)].rearrange("a p n -> (a p) n")
                pool.dma_start(ada_ring[:, a % ADA_RING, :], src).then_inc(ada_full[a % ADA_RING], 16)

            def load_adas(first, count):
                with pool.Fori(0, count // ADA_RING) as turn:
                    for a in range(first, first + ADA_RING):
                        load_ada(a, turn)

            roots = [0]

            def root(lo, hi):
                roots[0] += 1
                pool.wait_ge(root_in, roots[0])
                pool.tensor_tensor(rstd[:, lo:hi], rstd[:, lo:hi], minus_half[:, lo:hi], ALU.pow).then_inc(root_out, 1)

            def attention_roots():
                root(0, 4)
                for b in range(NB):
                    root(4, 8)

            for a in range(ADA_RING):
                pool.dma_start(ada_ring[:, a, :], ada[a]).then_inc(ada_full[a], 16)
            for i, dst in enumerate(ada_places):
                pool.dma_start(dst, ada[ADA_RING + i]).then_inc(ada_ahead[i], 16)
            pool.memset(minus_half[:, :], -0.5).then_inc(half_ready, 1)
            pool.wait_ge(half_ready, 1)
            load_adas(ADA_EARLY, ADA_RING)
            root(0, 2)
            load_adas(ADA_RING + ADA_EARLY, ADA_MID - ADA_EARLY)
            attention_roots()
            root(0, 2)
            load_adas(ADA_RING + ADA_MID, ADA_CHUNKS - ADA_RING - ADA_MID)
            root(0, 2)
            pool.wait_ge(mod_ready, 12)
            pool.dma_start(Z[:, NA_AT:NA_AT + 4096], d["na"]).then_inc(late_in, 16)
            pool.dma_start(Z[:, DIL_AT:DIL_AT + 4096], d["dil"]).then_inc(late_in, 16)
            pool.dma_start(Z[:, TRI_AT:TRI_AT + 2 * P], d["tri_iota"]).then_inc(late_in, 16)
            pool.dma_start(Z[:, RW_AT:RW_AT + 64], d["router"]).then_inc(late_in, 16)
            pool.dma_start(Z[:, LNM_AT:LNM_AT + 512], d["lnm"]).then_inc(late_in, 16)
            attention_roots()
            root(0, 2)
            pool.dma_start(row0[:, :], d["rows"][4:5, :].broadcast_to([P, D])).then_inc(rows_in, 16)
            pool.dma_start(row1[:, :], d["rows"][5:6, :].broadcast_to([P, D])).then_inc(rows_in, 16)
            pool.wait_ge(x_ready, 4)
            pool.dma_start(gate_mix[:, :], d["rows"][6:7, :].broadcast_to([P, D])).then_inc(rows_in2, 16)
            pool.dma_start(gate_ffn[:, :], d["rows"][7:8, :].broadcast_to([P, D])).then_inc(rows_in2, 16)
            for lo, hi in ((4, 6), (0, 2), (4, 6), (0, 2), (0, 4), (4, 6), (0, 2), (4, 6)):
                root(lo, hi)

        @block.tensor
        def _(pe):
            def mark(s):
                nc.tensor.matmul(ps[0:1, 7, 0:2], zero[:, 0:1], finite[:, 0:2], start=True, stop=True,
                                 skip_group_check=True).then_inc(s, 1)

            def transpose_x(t):
                for j in range(4):
                    for kt in (2 * j, 2 * j + 1):
                        for b in range(NB):
                            m = nc.tensor.transpose(ps[:, j, (kt % 2) * T + b * P:(kt % 2) * T + (b + 1) * P],
                                                    XN[:, b, kt * P:(kt + 1) * P], ident[:, :])
                    m.then_inc(xt_ps, 1)

            def product(out, xh, xl, at, n, last):
                slot, c = at
                wh, wl = WH[:, slot, c:c + 512], WL[:, slot, c:c + 512]
                nc.tensor.matmul(out, xh, wh, start=n, stop=False, skip_group_check=True)
                nc.tensor.matmul(out, xh, wl, start=False, stop=False, skip_group_check=True)
                return nc.tensor.matmul(out, xl, wh, start=False, stop=last, skip_group_check=True)

            def up_piece(chunk, half, turn, banks, pair):
                pe.wait_ge(lo_ready, turn * (2 * RING) + (piece_no(chunk, half) + 1))
                for b in range(NB):
                    for i in range(2):
                        kt = 2 * pair + i
                        xs = slice(b * P, (b + 1) * P)
                        m = product(ps[:, banks[b], :], XTH[:, kt, xs], XTL[:, kt, xs],
                                    (piece_no(chunk, half) % SPLITS, i * 512), kt == 0, kt == KT - 1)
                m.then_inc(piece_done, 1)

            def gemm(g):
                for q in range(GEMM_GROUPS[g]):
                    if q >= 2:
                        pe.wait_ge(gemm_out, 2 * sum(GEMM_GROUPS[:g]) + 2 * (q - 1))
                    banks = [4 + 2 * (q % 2) + b for b in range(NB)]
                    for pair in range(4):
                        up_piece(GEMM_CHUNK[g] + 2 * q + pair // 2, pair % 2, 0, banks, pair)

            def clear_y(banks):
                for j in banks:
                    nc.tensor.matmul(ps[:, j, :], zero[:, :], finite, start=True, stop=False,
                                     skip_group_check=True)

            def down(j0, h, chunk_slot, last, used=None):
                for f in range(2):
                    for half in range(2):
                        m = nc.tensor.matmul(ps[:, j0 + half, :], h[:, f, :],
                                             ring[:, chunk_slot, f * D + half * 512:f * D + (half + 1) * 512],
                                             start=False, stop=last and f == 1, skip_group_check=True)
                        if used is not None and f == 0 and half == 0:
                            m.then_inc(used, 1)
                return m

            def up(bank, lhs, slot, kts):
                for kt in kts:
                    m = nc.tensor.matmul(ps[:, bank, :], lhs(kt), ring[:, slot, (kt % 4) * 512:(kt % 4 + 1) * 512],
                                         start=kt == 0, stop=kt == KT - 1, skip_group_check=True)
                return m

            def turn_h(bank, b, used=None):
                for f in range(2):
                    if f == 1 and used is not None:
                        m.then_inc(used, 1)
                    m = nc.tensor.transpose(ps[:, bank, f * P:(f + 1) * P], hbuf[:, b, f * P:(f + 1) * P], ident[:, :])
                return m

            def ffn(i):
                n0 = FFN_CHUNK[i]
                h0 = FF_STEPS * i
                clear_y(range(4))

                def turn_both():
                    for b in range(NB):
                        for f in range(2):
                            m = nc.tensor.transpose(ps[:, 6 + b, f * P:(f + 1) * P], hbuf[:, b, f * P:(f + 1) * P], ident[:, :])
                    m.then_inc(hT_ps, 1)

                def down_piece(chunk, f, turn, last):
                    pe.wait_ge(lo_ready, turn * (2 * RING) + (piece_no(chunk, f) + 1))
                    for b in range(NB):
                        for half in range(2):
                            m = product(ps[:, 2 * b + half, :], hTH[:, b, f, :], hTL[:, b, f, :],
                                        (piece_no(chunk, f) % SPLITS, half * 512), False, last and f == 1)
                    m.then_inc(piece_done, 1)

                for pair in range(4):
                    up_piece(n0 + pair // 2, pair % 2, 0, (4, 5), pair)

                def step(n, turn, s):
                    k = turn * 2 + (h0 + 1 + s)
                    for pair in range(4):
                        if pair == 0:
                            pe.wait_ge(h_ready, k)
                        up_piece(n + pair // 2, pair % 2, turn, (4, 5), pair)
                        if pair == 0:
                            turn_both()
                    pe.wait_ge(hT_ready, k)
                    for f in range(2):
                        down_piece(n + 2, f, turn, False)

                stream_turns(pe, FF_STEPS - 1, 3, n0 + 2, step)
                pe.wait_ge(h_ready, h0 + FF_STEPS)
                turn_both()
                pe.wait_ge(hT_ready, h0 + FF_STEPS)
                for f in range(2):
                    down_piece(n0 + FF_CHUNKS - 1, f, 0, True)

            def mod_columns(first, count, fills_before, ada_needed):
                pe.wait_ge(ada_used, ada_needed)
                if fills_before:
                    pe.wait_ge(mod_ready, fills_before)
                for i, m6 in enumerate(range(first, first + count)):
                    for j in range(KT):
                        c = i * KT + j
                        m = nc.tensor.matmul(ps[:, 6, c:c + 1], ada_acc[:, m6, j * P:(j + 1) * P], ones[:, 0:1],
                                             start=True, stop=True)
                m.then_inc(mod_ps, 1)

            def mod_rows(m6, fills_before):
                for half in range(2):
                    pe.wait_ge(mod_ready, fills_before + half)
                    nc.tensor.matmul(ps[:, 6, :], ones[:, :], ada_acc[:, m6, half * 512:(half + 1) * 512],
                                     start=True, stop=True).then_inc(mod_ps, 1)

            def fills(g):
                qk = QK[:, g.gi % 2, :]
                f = g.fill0

                def begin(f):
                    if f >= 1:
                        pe.wait_ge(filled, f)

                def tiles(srcs):
                    for i, src in enumerate(srcs):
                        for b in range(NB):
                            a = src(b)
                            m = nc.tensor.transpose(ps[0:a.shape[-1], 7, i * T + b * P:i * T + (b + 1) * P], a, ident[:, :])
                    return m

                def pair(col):
                    return [lambda b, c=c: PROJ[:, b, c:c + P] for c in (col, col + P)]

                if g.kind in "AD" or g.kind in "NL":
                    base = {"A": (A_Q, A_K), "D": (D_Q, D_K)}.get(g.kind)
                    if base is None:
                        h0 = (8 if g.kind == "L" else 0) + 4 * g.half
                        base = (h0 * HD, D + h0 * HD)
                    for c in base:
                        begin(f)
                        tiles(pair(c)).then_inc(fill_ps, 1)
                        f += 1
                if g.kind == "C":
                    for c in (C_Q, C_K, C_QI):
                        begin(f)
                        tiles(pair(c)).then_inc(fill_ps, 1)
                        f += 1
                    begin(f)
                    pe.wait_ge(c_ready, g.layer + 1)
                    tiles([lambda b: PROJ[:, b, C_KIREP:C_KIREP + P]]).then_inc(fill_ps, 1)
                if g.kind == "B":
                    begin(f)
                    pe.wait_ge(latent_in, 32 * (g.layer + 1))
                    pe.wait_ge(b_normed, g.layer + 1)
                    tiles(pair(B_QD)).then_inc(fill_ps, 1)
                    begin(f + 1)
                    tiles([lambda b: PROJ[:, b, B_KVD:B_KVD + P]]).then_inc(fill_ps, 1)
                    for b in range(NB):
                        begin(f + 2 + b)
                        for kt in range(2):
                            m = nc.tensor.matmul(ps[:, 7, 0:384], qk[:, kt * T + b * P:kt * T + (b + 1) * P], UQ[:, kt, :],
                                                 start=kt == 0, stop=kt == 1)
                        m.then_inc(fill_ps, 1)
                    for b in range(NB):
                        begin(f + 4 + b)
                        nc.tensor.matmul(ps[:, 7, :], qk[:, 512 + b * P:512 + (b + 1) * P], UKV,
                                         start=True, stop=True).then_inc(fill_ps, 1)
                    for j in range(2):
                        begin(f + 6 + j)
                        if j == 0:
                            pe.wait_ge(b_roped, g.layer + 1)
                        tiles([lambda b, h=h: PROJ[:, b, B_UQ + 96 * h:B_UQ + 96 * (h + 1)]
                               for h in (2 * j, 2 * j + 1)]).then_inc(fill_ps, 1)
                    for j in range(2):
                        begin(f + 8 + j)
                        tiles([lambda b, h=h: KB[:, b, h, :] for h in (2 * j, 2 * j + 1)]).then_inc(fill_ps, 1)

            def score(u):
                qk = QK[:, u.g.gi % 2, :]
                pe.wait_ge(filled, u.g.fill0 + u.g.n_fills)
                if u.su >= 2:
                    pe.wait_ge(probs, u.su - 1)
                j0 = 2 * (u.su % 2)
                for h in range(4):
                    s = head_slot(h)
                    out = ps[:, j0 + s // 2, (s % 2) * T:(s % 2) * T + u.nk]
                    q0 = u.b * P
                    if u.kind == "I":
                        lhs, rhs = qk[:, (4 + u.part) * T + q0:(4 + u.part) * T + q0 + P], KI4[:, h, 0:u.nk]
                    elif u.kind == "B":
                        lhs, rhs = qk[0:96, h * T + q0:h * T + q0 + P], qk[0:96, D + h * T:D + h * T + u.nk]
                    else:
                        p0, rows = (h % 2) * HD, HD
                        if u.kind == "A":
                            p0, rows = p0 + 32 * u.part, 32
                        tq, tk = h // 2, 2 + h // 2
                        lhs = qk[p0:p0 + rows, tq * T + q0:tq * T + q0 + P]
                        rhs = qk[p0:p0 + rows, tk * T:tk * T + u.nk]
                    m = nc.tensor.matmul(out, lhs, rhs, start=True, stop=True)
                m.then_inc(scores, 1)

            def values(u):
                src = PR[:, (u.su - 1) % 2 if u.kind == "A" else u.su % 2]
                if u.kind == "A":
                    pe.wait_ge(combined, u.comb + 1)
                else:
                    pe.wait_ge(probs, u.su + 1)
                for h in range(4):
                    for kb in range(u.nk // P):
                        m = nc.tensor.transpose(ps[:, 4 + h // 2, (h % 2) * T + kb * P:(h % 2) * T + (kb + 1) * P],
                                                src[:, head_slot(h), kb * P:(kb + 1) * P], ident[:, :])
                m.then_inc(pT_ps, 1)
                pe.wait_ge(pT_ready, u.pu + 1)
                if u.pu >= 1:
                    pe.wait_ge(mixed, u.pu)
                for h in range(4):
                    for kb in range(u.nk // P):
                        if u.kind == "B":
                            c = B_UKV + h * P + HD
                        else:
                            c = {"A": A_V, "C": C_V, "D": D_V, "N": 2 * D, "L": 2 * D + 512}[u.kind] + (4 * u.g.half + h) * HD
                        m = nc.tensor.matmul(ps[:, 6, h * HD:(h + 1) * HD], PT[:, h, kb, :], PROJ[:, kb, c:c + HD],
                                             start=kb == 0, stop=kb == u.nk // P - 1)
                m.then_inc(o_ps, 1)

            def attention(layer):
                us = units_of(layer)
                pe.wait_ge(gemm_out, 2 * sum(GEMM_GROUPS[:2 * layer + 1]))
                fills(us[0].g)
                score(us[0])
                for n, u in enumerate(us):
                    if u.first_of_group and u.g.gi + 1 < len(GROUPS) and GROUPS[u.g.gi + 1].layer == layer:
                        fills(GROUPS[u.g.gi + 1])
                    if n + 1 < len(us):
                        score(us[n + 1])
                    if u.pu is not None:
                        values(u)

            def route():
                pe.wait_ge(late_in, 16 * 5)
                for b in range(NB):
                    for kt in range(KT):
                        m = nc.tensor.matmul(ps[:, 7, b * 8:(b + 1) * 8], XT[:, kt, b * P:(b + 1) * P], router[:, kt, :],
                                             start=kt == 0, stop=kt == KT - 1)
                m.then_inc(route_ps, 1)
                pe.wait_ge(route_sel, 1)
                nc.tensor.matmul(ps[:, 7, 0:8], tri, r_sel[:, 0, :], start=True, stop=True)
                nc.tensor.matmul(ps[:, 7, 8:16], tri, r_sel[:, 1, :], start=True, stop=False)
                nc.tensor.matmul(ps[:, 7, 8:16], ones[:, :], r_sel[:, 0, :], start=False, stop=True)
                nc.tensor.matmul(ps[:, 7, 16:24], ones[:, :], r_sel[:, 0, :], start=True, stop=False)
                nc.tensor.matmul(ps[:, 7, 16:24], ones[:, :], r_sel[:, 1, :], start=False, stop=True).then_inc(rank_ps, 1)

            def experts(m):
                with pe.Fori(0, EXPERTS) as e:
                    turn_e = e * (EX_CHUNKS // RING)
                    k_e = e * EX_STEPS
                    pe.wait_ge(m["psel"], e + 1)
                    for j in range(KT):
                        for b in range(NB):
                            mm = nc.tensor.matmul(ps[:, 2 + j // 4, (j % 4) * P:(j % 4 + 1) * P],
                                                  XN[:, b, j * P:(j + 1) * P], PSEL[:, b, :], start=b == 0, stop=b == 1)
                    mm.then_inc(m["xg_ps"], 1)
                    pe.wait_ge(m["wsel"], e + 1)
                    for b in range(NB):
                        mm = nc.tensor.transpose(ps[:, 7, b * P:(b + 1) * P], WSEL[:, b, :], ident[:, :])
                    mm.then_inc(m["ct_ps"], 1)
                    clear_y(range(2))
                    pe.wait_ge(m["xg_ready"], e + 1)
                    pe.wait_ge(m["ct_ready"], e + 1)

                    def ups(half, par, local, turn):
                        ring_full_wait(pe, m, local + half, turn)
                        return up(4 + par, lambda kt: XG[:, kt, :], moe_slot(local + half),
                                  range(4 * half, 4 * half + 4))

                    ups(0, 0, 0, turn_e).then_inc(m["used"], 1)
                    ups(1, 0, 0, turn_e).then_inc(m["up_ps"], 1)
                    mark(m["used"])

                    def step(local, turn, s):
                        turn = turn + turn_e
                        k = k_turn(s)
                        par = (1 + s) % 2
                        ups(0, par, local, turn).then_inc(m["used"], 1)
                        pe.wait_ge(m["h_ready"], k)
                        turn_h(6 + (1 - par), 1 - par).then_inc(m["hT_ps"], 1)
                        ups(1, par, local, turn).then_inc(m["up_ps"], 1)
                        ring_full_wait(pe, m, local + 2, turn)
                        pe.wait_ge(m["hT_ready"], k)
                        down(0, hT[:, 1 - par], moe_slot(local + 2), False, m["used"]).then_inc(m["used"], 1)

                    turns = (EX_STEPS - 1) // 2
                    with pe.Fori(0, turns) as t:
                        def k_turn(s):
                            return t * 2 + k_e + (1 + s)
                        for s in range(2):
                            step(2 + 3 * s, t, s)

                    def k_turn(s):
                        return k_e + (1 + s)
                    for s in range(2 * turns, EX_STEPS - 1):
                        step(2 + 3 * s, 0, s)
                    par = (EX_STEPS - 1) % 2
                    pe.wait_ge(m["h_ready"], k_e + EX_STEPS)
                    turn_h(6 + par, par).then_inc(m["hT_ps"], 1)
                    ring_full_wait(pe, m, EX_CHUNKS - 1, turn_e)
                    pe.wait_ge(m["hT_ready"], k_e + EX_STEPS)
                    down(0, hT[:, par], moe_slot(EX_CHUNKS - 1), True).then_inc(m["ye_ps"], 1)
                    mark(m["used"])
                    pe.wait_ge(m["ye_ready"], e + 1)
                    for b in range(NB):
                        if b == 1:
                            pe.wait_ge(m["sc_added"], e * 2 + 1)
                        for half in range(2):
                            mm = nc.tensor.matmul(ps[:, 2 + half, :], CT[:, b, :], YE[:, half * 512:(half + 1) * 512],
                                                  start=True, stop=True)
                        mm.then_inc(m["sc_ps"], 1)
                    pe.wait_ge(m["sc_added"], e * 2 + 2)

            pe.wait_ge(zero_ready, 1)
            pe.wait_ge(const_in, 16 * N_CONST)
            for layer in range(LAYERS):
                if layer == 0:
                    mod_columns(0, 2, 0, ADA_EARLY)
                else:
                    mod_columns(0, 2, 6, ADA_CHUNKS)
                    mod_rows(2, 7)
                    mod_columns(3, 2, 9, ADA_CHUNKS)
                    mod_rows(5, 10)
                pe.wait_ge(xn_ready, 2 * NORM_NO[3 * layer])
                transpose_x(3 * layer)
                pe.wait_ge(xt_ready, 4 * (3 * layer + 1))
                gemm(2 * layer)
                if layer == 0:
                    pe.wait_ge(gemm_out, 12)
                    pe.wait_ge(ada_used, 24)
                    mod_rows(2, 1)
                    mod_columns(3, 2, 3, 24)
                    mod_rows(5, 4)
                pe.wait_ge(mod_ready, 6 if layer == 0 else 12)
                attention(layer)
                pe.wait_ge(mixed, pu_end(layer))
                transpose_x(3 * layer + 1)
                pe.wait_ge(xt_ready, 4 * (3 * layer + 2))
                gemm(2 * layer + 1)
                pe.wait_ge(xn_ready, 2 * NORM_NO[3 * layer + 2])
                transpose_x(3 * layer + 2)
                pe.wait_ge(xt_ready, 4 * (3 * layer + 3))
                if layer == 0:
                    ffn(0)
                else:
                    route()
                    experts(moe_sems[0])
                    pe.wait_ge(route_ready, 1)
                    over = pe.value_load(flag[0:1, 0:1], min_val=0, max_val=1)
                    with pe.If(over > 0):
                        experts(moe_sems[1])
            pe.wait_ge(xn_ready, 10)
            transpose_x(6)
            pe.wait_ge(xt_ready, 28)
            ffn(1)
            pe.wait_ge(xn_ready, 12)
            transpose_x(7)
            pe.wait_ge(xt_ready, 32)
            gemm(4)
            attention(2)
            pe.wait_ge(xn_ready, 14)
            transpose_x(8)
            pe.wait_ge(xt_ready, 36)
            gemm(5)
            pe.wait_ge(xn_ready, 16)
            transpose_x(9)
            pe.wait_ge(xt_ready, 40)
            ffn(2)

        @block.scalar
        def _(act):
            def loads(pairs, s):
                for dst, src in pairs:
                    act.dma_start(dst, src).then_inc(s, 16)

            loads([(cols[:, :], d["cols"]), (unit[:, :], d["unit"]),
                   (lam_in, d["lam"].broadcast_to([P, 256]).rearrange("p (l n) -> p l n", l=LAYERS)),
                   (gate_mix[:, :], d["rows"][0:1, :].broadcast_to([P, D])),
                   (gate_ffn[:, :], d["rows"][1:2, :].broadcast_to([P, D])),
                   (row0[:, :], d["rows"][2:3, :].broadcast_to([P, D])),
                   (row1[:, :], d["rows"][3:4, :].broadcast_to([P, D])),
                   (gdiff[:, :, :].rearrange("p l n -> p (l n)"), d["gdiff"].broadcast_to([P, LAYERS * HD])),
                   (cossin[:, :, :, :].rearrange("p b c n -> p (b c n)"), d["cossin"]),
                   (alibi[:, :], d["alibi"]), (cmask[:, :], d["cmask"]), (band[:, :], d["band"][0])], const_in)

            def squares(t):
                if t == 0:
                    act.wait_ge(x_in, 16)
                elif t == 8:
                    act.wait_ge(mixed, pu_end(LAYERS))
                else:
                    act.wait_ge(x_ready, X_READY[t])
                if t == 8:
                    for b in range(NB):
                        for half in range(2):
                            cs = slice(half * 512, (half + 1) * 512)
                            act.activation(YB[:, b, cs], XN[:, b, cs], ACT.Square,
                                           accum_out=ss[:, 2 * b + half:2 * b + half + 1]).then_inc(sq_ready, 1)
                else:
                    for b in range(NB):
                        act.activation(XN[:, b, :], X[:, b, :], ACT.Square,
                                       accum_out=ss[:, b:b + 1]).then_inc(sq_ready, 1)

            def split_hi(chunk, half, turn=0):
                if half == 0:
                    act.wait_ge(full[chunk % RING], turn * 16 + 16 * (chunk // RING + 1))
                p = piece_no(chunk, half)
                if p >= SPLITS:
                    act.wait_ge(piece_done, turn * (2 * RING) + (p - SPLITS + 1))
                act.activation(WH[:, p % SPLITS, :], ring[:, chunk % RING, half * PIECE:(half + 1) * PIECE],
                               ACT.Copy).then_inc(hi_ready, 1)

            def ahead_hi(first):
                for half in range(SPLITS):
                    split_hi(first + half // 2, half % 2)

            def xt_split_hi(t):
                for j in range(4):
                    act.wait_ge(xt_full, 4 * SPLIT_NO[t] + j + 1)
                    act.activation(XTH[:, 2 * j:2 * j + 2, :], XT[:, 2 * j:2 * j + 2, :], ACT.Copy).then_inc(xt_hi, 1)

            def gemm_copy(g):
                dst = PROJ if g % 2 == 0 else YB

                def copy_out(q):
                    act.wait_ge(piece_done, piece_no(GEMM_CHUNK[g] + 2 * q + 1, 2))
                    for b in range(NB):
                        act.activation(dst[:, b, q * 512:(q + 1) * 512], ps[:, 4 + 2 * (q % 2) + b, :],
                                       ACT.Copy).then_inc(gemm_out, 1)

                for q in range(GEMM_GROUPS[g]):
                    for i in range(4):
                        if q > 0 or i >= SPLITS:
                            split_hi(GEMM_CHUNK[g] + 2 * q + i // 2, i % 2)
                        if q > 0 and i == 2:
                            copy_out(q - 1)
                copy_out(GEMM_GROUPS[g] - 1)

            def silu(s_in, s_out, count, par):
                act.wait_ge(s_in, count)
                act.activation(sgt[:, par, :], ps[:, 4 + par, 0:FW], ACT.Silu).then_inc(s_out, 1)

            def copy_hT(s_in, s_out, count, par):
                act.wait_ge(s_in, count)
                act.activation(hT[:, par].rearrange("p f n -> p (f n)"), ps[:, 6 + par, 0:2 * P], ACT.Copy).then_inc(s_out, 1)

            def ffn(i):
                h0 = FF_STEPS * i
                n0 = FFN_CHUNK[i]

                def silu_both(n, turn):
                    act.wait_ge(piece_done, turn * (2 * RING) + piece_no(n + 1, 2))
                    act.activation(sgt[:, :, :], ps[:, 4:6, 0:FW], ACT.Silu).then_inc(silu_ready, 1)

                def hT_high(k):
                    act.wait_ge(hT_ps, k)
                    act.activation(hTH[:, :, :, :].rearrange("p b f n -> p b (f n)"), ps[:, 6:8, 0:2 * P],
                                   ACT.Copy).then_inc(hT_hi, 1)

                split_hi(n0 + 1, 1)

                def step(n, turn, k):
                    silu_both(n - 2 if isinstance(k, int) and k == h0 + 1 else n - 3, turn)
                    for half in range(2):
                        split_hi(n, half, turn)
                    for half in range(2):
                        split_hi(n + 1, half, turn)
                    hT_high(k)
                    for half in range(2):
                        split_hi(n + 2, half, turn)

                for s in range(2):
                    step(n0 + 2 + 3 * s, 0, h0 + 1 + s)
                stream_turns(act, FF_STEPS - 3, 3, n0 + 8, lambda n, turn, s: step(n, turn, turn * 2 + (h0 + 3 + s)))
                silu_both(n0 + FF_CHUNKS - 4, 0)
                for half in range(2):
                    split_hi(n0 + FF_CHUNKS - 1, half)
                hT_high(h0 + FF_STEPS)
                act.wait_ge(piece_done, piece_no(n0 + FF_CHUNKS - 1, 2))
                for b in range(NB):
                    act.activation(YB[:, b, :], ps[:, 2 * b:2 * b + 2, :].rearrange("p j n -> p (j n)"), ACT.Copy).then_inc(y_out, 1)

            def result_squares(src, number, s, count):
                act.wait_ge(s, count)
                for b in range(NB):
                    act.activation(XN[:, b, :], src[:, b, :], ACT.Square,
                                   accum_out=ss[:, 4 + b:5 + b]).then_inc(res_sq, 1)

            def copy_fills(g):
                qk = QK[:, g.gi % 2, :]
                f = g.fill0

                def fill(f, dst, src, scale=1.0, last=True):
                    act.wait_ge(fill_ps, f + 1)
                    ins = act.activation(dst, src, ACT.Copy, scale=scale)
                    if last:
                        ins.then_inc(filled, 1)

                if g.kind in "ADNL":
                    for i in range(2):
                        fill(f + i, qk[:, i * 512:(i + 1) * 512], ps[:, 7, :])
                if g.kind == "C":
                    for i in range(3):
                        fill(f + i, qk[:, i * 512:(i + 1) * 512], ps[:, 7, :])
                    for h in range(4):
                        fill(f + 3, KI4[32 * h:32 * (h + 1), h, :], ps[32 * h:32 * (h + 1), 7, 0:T], last=h == 3)
                if g.kind == "B":
                    for i, (c, w) in enumerate(((B_QD, 256), (B_KVD, 128))):
                        for b in range(NB):
                            if 2 * i + b > 0:
                                act.wait_ge(b_sq, 4 * g.layer + 2 * i + b)
                            act.activation(junk[:, 0:w], PROJ[:, b, c:c + w], ACT.Square,
                                           accum_out=ss[:, 2 * i + b:2 * i + b + 1]).then_inc(b_sq, 1)
                    for kt in range(2):
                        at = COL["q_g"] + 2 * g.layer + kt
                        fill(f, qk[:, kt * T:(kt + 1) * T], ps[:, 7, kt * T:(kt + 1) * T], cols[:, at:at + 1], kt == 1)
                    at = COL["kv_g"] + g.layer
                    fill(f + 1, qk[:, 512:768], ps[:, 7, 0:T], cols[:, at:at + 1])
                    for b in range(NB):
                        fill(f + 2 + b, PROJ[:, b, B_UQ:B_UQ + 384], ps[:, 7, 0:384])
                    for b in range(NB):
                        fill(f + 4 + b, PROJ[:, b, B_UKV:B_UKV + 512], ps[:, 7, :])
                    for i in range(4):
                        fill(f + 6 + i, qk[0:96, i * 512:(i + 1) * 512], ps[0:96, 7, :])

            def probabilities(u):
                par = u.su % 2
                if u.su >= 2:
                    name, number = release(UNITS[u.su - 2])
                    act.wait_ge({"idx": idx_added, "comb": combined, "pT": pT_ps}[name], number)
                src = ps[:, 2 * par:2 * par + 2, :].rearrange("p j (s k) -> p (j s) k", s=2)
                if u.kind == "I":
                    act.wait_ge(scores, u.su + 1)
                    act.activation(PR[:, par, :, 0:u.nk], src[:, :, 0:u.nk], ACT.Relu).then_inc(probs, 1)
                    return
                act.wait_ge(biased, u.bi + 1)
                for h in range(4):
                    s = head_slot(h)
                    ins = act.activation(PR[:, par, s, 0:u.nk], src[:, s, 0:u.nk], ACT.Exp, bias=nmax[:, par, s:s + 1],
                                         accum_out=den[:, par, h:h + 1])
                ins.then_inc(probs, 1)

            def copy_pT(u):
                act.wait_ge(pT_ps, u.pu + 1)
                src = ps[:, 4:6, :].rearrange("p j (h k) -> p (j h) k", h=2)
                act.activation(PT.rearrange("p h b q -> p h (b q)")[:, :, 0:u.nk], src[:, :, 0:u.nk],
                               ACT.Copy).then_inc(pT_ready, 1)

            def attention(layer):
                us = units_of(layer)
                copy_fills(us[0].g)
                probabilities(us[0])
                for n, u in enumerate(us):
                    if u.first_of_group and u.g.gi + 1 < len(GROUPS) and GROUPS[u.g.gi + 1].layer == layer:
                        copy_fills(GROUPS[u.g.gi + 1])
                    if n + 1 < len(us):
                        probabilities(us[n + 1])
                    if u.pu is not None:
                        copy_pT(u)

            def route():
                act.wait_ge(route_max, 1)
                for b in range(NB):
                    act.activation(r_exp[:, b, :], r_logit[:, b, 0:8], ACT.Exp, bias=r_nv1[:, b:b + 1])
                    ins = act.activation(r_e2[:, b:b + 1], r_top[:, b, 1:2], ACT.Exp, bias=r_nv1[:, b:b + 1])
                ins.then_inc(route_exp, 1)

            def experts(m):
                with act.Fori(0, EXPERTS) as e:
                    k_e = e * EX_STEPS
                    act.wait_ge(m["xg_ps"], e + 1)
                    for j in range(KT):
                        ins = act.activation(XG[:, j, :], ps[:, 2 + j // 4, (j % 4) * P:(j % 4 + 1) * P], ACT.Identity,
                                             scale=xscale[:, j:j + 1], bias=modc[:, 16 + j:17 + j])
                    ins.then_inc(m["xg_ready"], 1)
                    act.wait_ge(m["ct_ps"], e + 1)
                    act.activation(CT.rearrange("p b s -> p (b s)"), ps[:, 7, 0:T], ACT.Copy).then_inc(m["ct_ready"], 1)
                    silu(m["up_ps"], m["silu_ready"], k_e + 1, 0)
                    turns = (EX_STEPS - 1) // 2
                    with act.Fori(0, turns) as t:
                        for s in range(2):
                            k = t * 2 + k_e + (1 + s)
                            copy_hT(m["hT_ps"], m["hT_ready"], k, s)
                            silu(m["up_ps"], m["silu_ready"], k + 1, 1 - s)
                    for s in range(2 * turns, EX_STEPS - 1):
                        k = k_e + (1 + s)
                        copy_hT(m["hT_ps"], m["hT_ready"], k, s % 2)
                        silu(m["up_ps"], m["silu_ready"], k + 1, 1 - s % 2)
                    copy_hT(m["hT_ps"], m["hT_ready"], k_e + EX_STEPS, (EX_STEPS - 1) % 2)
                    act.wait_ge(m["ye_ps"], e + 1)
                    act.activation(YE, ps[:, 0:2, :].rearrange("p j n -> p (j n)"), ACT.Copy).then_inc(m["ye_ready"], 1)

            act.wait_ge(const_in, 16 * N_CONST)
            act.activation(csilu[:, :], cols[:, COL["c"]:COL["c"] + KT], ACT.Silu).then_inc(csilu_ready, 1)
            act.wait_ge(lam_exp_in, 1)
            act.activation(lamc[:, 0:4], lamc[:, 4:8], ACT.Exp).then_inc(lam_exp_out, 1)
            for layer in range(LAYERS):
                squares(3 * layer)
                if layer == 0:
                    act.wait_ge(ada_used, ADA_EARLY)
                ahead_hi(GEMM_CHUNK[2 * layer])
                xt_split_hi(3 * layer)
                gemm_copy(2 * layer)
                act.wait_ge(gemm_out, 2 * sum(GEMM_GROUPS[:2 * layer + 1]))
                loads([(UKV, d["ukv"][layer]), (UQ.rearrange("p k n -> p (k n)"), d["uq"][layer])], latent_in)
                attention(layer)
                act.wait_ge(mixed, pu_end(layer))
                if layer + 1 < LAYERS:
                    loads([(band[:, :], d["band"][layer + 1])], layer_in)
                ahead_hi(GEMM_CHUNK[2 * layer + 1])
                xt_split_hi(3 * layer + 1)
                gemm_copy(2 * layer + 1)
                squares(3 * layer + 2)
                if layer == 0:
                    ahead_hi(FFN_CHUNK[0])
                    xt_split_hi(2)
                    ffn(0)
                else:
                    route()
                    experts(moe_sems[0])
                    act.wait_ge(route_ready, 1)
                    over = act.value_load(flag[0:1, 0:1], min_val=0, max_val=1)
                    with act.If(over > 0):
                        experts(moe_sems[1])
            result_squares(X, 0, x_ready, 4)
            squares(6)
            ahead_hi(FFN_CHUNK[1])
            xt_split_hi(6)
            ffn(1)
            result_squares(YB, 1, y_out, 4)
            squares(7)
            ahead_hi(GEMM_CHUNK[4])
            xt_split_hi(7)
            gemm_copy(4)
            attention(2)
            squares(8)
            ahead_hi(GEMM_CHUNK[5])
            xt_split_hi(8)
            gemm_copy(5)
            result_squares(YB, 2, gemm_out, 2 * sum(GEMM_GROUPS))
            squares(9)
            ahead_hi(FFN_CHUNK[2])
            xt_split_hi(9)
            ffn(2)
            result_squares(YB, 3, y_out, 6)

        @block.vector
        def _(dve):
            linked = [0]

            def link(ins):
                linked[0] += 1
                ins.then_inc(dve_chain, 1)
                dve.wait_ge(dve_chain, linked[0])

            def ada_step(a, turn=0, m6=None):
                q = a % 4
                acc = ada_acc[:, (a % 24) // 4, :] if m6 is None else ada_acc[:, bass.ds(m6, 1), :].rearrange("p a n -> p (a n)")
                if m6 is None and ADA_RING <= a < ADA_EARLY:
                    dve.wait_ge(ada_ahead[a - ADA_RING], 16)
                    w = ada_places[a - ADA_RING]
                else:
                    loads = (a if a < ADA_RING else a - len(ADA_AHEAD)) // ADA_RING + 1
                    dve.wait_ge(ada_full[a % ADA_RING], turn * (16 * 4 // ADA_RING) + 16 * loads)
                    w = ada_ring[:, a % ADA_RING, :]
                if q == 0:
                    nc.vector.tensor_scalar(acc, w[:, 0:D], csilu[:, 0:1], None, ALU.mult).then_inc(ada_half, 1)
                else:
                    dve.wait_ge(ada_used, turn * 4 + a)
                    nc.vector.scalar_tensor_tensor(acc, w[:, 0:D], csilu[:, 2 * q:2 * q + 1], acc, ALU.mult,
                                                   ALU.add).then_inc(ada_half, 1)
                dve.wait_ge(ada_half, turn * 4 + (a + 1))
                nc.vector.scalar_tensor_tensor(acc, w[:, D:2 * D], csilu[:, 2 * q + 1:2 * q + 2], acc, ALU.mult,
                                               ALU.add).then_inc(ada_used, 1)

            def mod_columns_add(first, layer, number):
                dve.wait_ge(mod_ps, number)
                at = COL["ada_b"] + 48 * layer + 8 * first
                to = 0 if first == 0 else 16
                link(nc.vector.tensor_tensor(modc[:, to:to + 16], ps[:, 6, 0:16], cols[:, at:at + 16], ALU.add))
                g = COL["mix_g" if first == 0 else "ffn_g"] + 8 * layer
                return to, g

            def mod_columns(first, layer, number):
                to, g = mod_columns_add(first, layer, number)
                nc.vector.tensor_copy(ps[0:1, 6, 0:1], modc[0:1, 0:1]).then_inc(mod_ready, 1)

            def set_xscale(first, layer):
                to = 0 if first == 0 else 16
                g = COL["mix_g" if first == 0 else "ffn_g"] + 8 * layer
                link(nc.vector.scalar_tensor_tensor(xscale[:, :], modc[:, to + 8:to + 16], 1.0, cols[:, g:g + 8],
                                                    ALU.add, ALU.mult))

            def mod_rows(gate, bias, number):
                for half in range(2):
                    dve.wait_ge(mod_ps, number + half)
                    cs = slice(half * 512, (half + 1) * 512)
                    nc.vector.tensor_tensor(gate[:, cs], ps[:, 6, :], bias[:, cs], ALU.add).then_inc(mod_ready, 1)

            roots = [0]

            def inverse_root(*parts):
                for out, sums, width in parts:
                    ins = nc.vector.tensor_scalar(out, sums, 1.0 / width, EPS, ALU.mult, ALU.add)
                roots[0] += 1
                ins.then_inc(root_in, 1)
                dve.wait_ge(root_out, roots[0])

            def normalise(t):
                dve.wait_ge(sq_ready, SQUARES[t])
                if t == 8:
                    inverse_root((rstd[:, 0:4], ss[:, 0:4], 512))
                    for b in range(NB):
                        for half in range(2):
                            cs = slice(half * 512, (half + 1) * 512)
                            ins = nc.vector.tensor_scalar(XN[:, b, cs], XN[:, b, cs],
                                                          rstd[:, 2 * b + half:2 * b + half + 1], None, ALU.mult)
                        ins.then_inc(xn_ready, 1)
                else:
                    inverse_root((rstd[:, 0:2], ss[:, 0:2], D))
                    for b in range(NB):
                        nc.vector.tensor_scalar(XN[:, b, :], X[:, b, :], rstd[:, b:b + 1], None,
                                                ALU.mult).then_inc(xn_ready, 1)

            def copy_xt(t):
                gain = {6: "f1_g", 7: "mp_g", 8: "out_g", 9: "f2_g"}.get(t)
                for j in range(4):
                    dve.wait_ge(xt_ps, 4 * t + j + 1)
                    if t in (1, 4):
                        nc.vector.tensor_copy(XT[:, 2 * j:2 * j + 2, :].rearrange("p k n -> p (k n)"), ps[:, j, :]).then_inc(xt_full, 1)
                        continue
                    for kt in (2 * j, 2 * j + 1):
                        src = ps[:, j, (kt % 2) * T:(kt % 2 + 1) * T]
                        if gain:
                            at = COL[gain] + kt
                            ins = nc.vector.tensor_scalar(XT[:, kt, :], src, cols[:, at:at + 1], None, ALU.mult)
                        else:
                            sh = (0 if t % 3 == 0 else 16) + kt
                            ins = nc.vector.tensor_scalar(XT[:, kt, :], src, xscale[:, kt:kt + 1], modc[:, sh:sh + 1],
                                                          ALU.mult, ALU.add)
                    ins.then_inc(xt_ready if t == 5 else xt_full, 1)
                if t == 5:
                    return
                for j in range(4):
                    dve.wait_ge(xt_hi, 4 * SPLIT_NO[t] + j + 1)
                    ks = slice(2 * j, 2 * j + 2)
                    nc.vector.tensor_tensor(XTL[:, ks, :], XT[:, ks, :], XTH[:, ks, :].bitcast(F32),
                                            ALU.subtract).then_inc(xt_ready, 1)

            def split_lo(chunk, half, turn=0):
                p = piece_no(chunk, half)
                dve.wait_ge(hi_ready, turn * (2 * RING) + (p + 1))
                nc.vector.tensor_tensor(WL[:, p % SPLITS, :], ring[:, chunk % RING, half * PIECE:(half + 1) * PIECE],
                                        WH[:, p % SPLITS, :].bitcast(F32), ALU.subtract).then_inc(lo_ready, 1)

            def ahead_lo(first):
                for half in range(SPLITS):
                    split_lo(first + half // 2, half % 2)

            def gemm_lo(g, beside=lambda p: None):
                for p in range(SPLITS, 4 * GEMM_GROUPS[g]):
                    split_lo(GEMM_CHUNK[g] + p // 2, p % 2)
                    beside(p)

            def add_gated(gate, s, count):
                dve.wait_ge(s, count)
                link(nc.vector.tensor_tensor(YB, YB, gate[:, :].unsqueeze(1).broadcast_to([P, NB, D]), ALU.mult))
                nc.vector.tensor_tensor(X[:, :, :], X[:, :, :], YB, ALU.add).then_inc(x_ready, 1)

            def add_normed(row, number, factor):
                dve.wait_ge(res_sq, 2 * number)
                inverse_root((rstd[:, 4:6], ss[:, 4:6], D))
                for b in range(NB):
                    link(nc.vector.scalar_tensor_tensor(YB[:, b, :], YB[:, b, :], rstd[:, 4 + b:5 + b], row[:, :],
                                                        ALU.mult, ALU.mult))
                for b in range(NB):
                    ins = nc.vector.scalar_tensor_tensor(X[:, b, :], YB[:, b, :], factor, X[:, b, :], ALU.mult, ALU.add)
                ins.then_inc(x_ready, 1)

            def h_product(s_in, s_out, count, par):
                dve.wait_ge(s_in, count)
                nc.vector.tensor_tensor(hbuf[:, par, :], sgt[:, par, :], ps[:, 4 + par, FW:2 * FW], ALU.mult).then_inc(s_out, 1)

            def ffn(i):
                h0, n0 = FF_STEPS * i, FFN_CHUNK[i]

                def h_both(k):
                    dve.wait_ge(silu_ready, k)
                    nc.vector.tensor_tensor(hbuf[:, :, :], sgt[:, :, :], ps[:, 4:6, FW:2 * FW], ALU.mult).then_inc(h_ready, 1)

                def hT_low(k):
                    dve.wait_ge(hT_hi, k)
                    nc.vector.tensor_tensor(hTL[:, :, :, :].rearrange("p b f n -> p b (f n)"), ps[:, 6:8, 0:2 * P],
                                            hTH[:, :, :, :].rearrange("p b f n -> p b (f n)").bitcast(F32),
                                            ALU.subtract).then_inc(hT_ready, 1)

                split_lo(n0 + 1, 1)
                if i == 0:
                    ada_step(26)
                    ada_step(27)

                def step(n, turn, s):
                    k = turn * 2 + (h0 + 1 + s)
                    h_both(k)
                    for half in range(2):
                        split_lo(n, half, turn)
                    if i == 0:
                        ada_step(28 + 2 * s, turn, turn + 1)
                    for half in range(2):
                        split_lo(n + 1, half, turn)
                    hT_low(k)
                    for half in range(2):
                        split_lo(n + 2, half, turn)
                        if i == 0 and half == 0:
                            ada_step(29 + 2 * s, turn, turn + 1)

                stream_turns(dve, FF_STEPS - 1, 3, n0 + 2, step)
                h_both(h0 + FF_STEPS)
                for half in range(2):
                    split_lo(n0 + FF_CHUNKS - 1, half)
                hT_low(h0 + FF_STEPS)

            def bias_table(u):
                at = 0 if u.b == 0 else 512
                if u.kind in "AC":
                    return alibi[:, at:at + 4 * u.nk].rearrange("p (s k) -> p s k", s=4)
                if u.kind == "D":
                    return band[:, at:at + 4 * u.nk].rearrange("p (s k) -> p s k", s=4)
                if u.kind == "B":
                    at = 0 if u.b == 0 else 128
                    return cmask[:, at:at + u.nk].unsqueeze(1).broadcast_to([P, 4, u.nk])
                return (na_bias if u.kind == "N" else dil_bias)[:, u.b, u.g.half]

            def bias(u):
                par = u.su % 2
                dve.wait_ge(scores, u.su + 1)
                if u.kind == "D" and u.layer == 1 and u.b == 0:
                    dve.wait_ge(layer_in, 16)
                src = ps[:, 2 * par:2 * par + 2, :].rearrange("p j (s k) -> p (j s) k", s=2)[:, :, 0:u.nk]
                scale = {"A": 32 ** -0.5, "B": 96 ** -0.5}.get(u.kind, HD ** -0.5)
                link(nc.vector.scalar_tensor_tensor(src, src, scale, bias_table(u), ALU.mult, ALU.add))
                if u.kind == "C":
                    link(nc.vector.tensor_tensor(src, src, SEL[u.b].unsqueeze(1).broadcast_to([P, 4, u.nk]), ALU.add))
                nc.vector.tensor_reduce(nmax[:, par, :], src, AX_X, ALU.max, negate=True).then_inc(biased, 1)

            def index_add(u):
                par, b, nk = u.su % 2, u.b, u.nk
                work = [PROJ[:, i, C_WORK:C_WORK + nk] for i in range(2)]
                dve.wait_ge(probs, u.su + 1)
                for h in range(4):
                    src = PR[:, par, head_slot(h), 0:nk]
                    at = 0 if b == 0 else 128
                    prev = cmask[:, at:at + nk] if u.part == 0 and h == 0 else work[0]
                    ins = nc.vector.scalar_tensor_tensor(work[0], src, w16[:, b, 4 * u.part + h:4 * u.part + h + 1], prev,
                                                         ALU.mult, ALU.add)
                    if h < 3:
                        link(ins)
                ins.then_inc(idx_added, 1)
                if u.part == 0:
                    dve.wait_ge(idx_added, u.idx + 1)
                    return
                dve.wait_ge(idx_added, u.idx + 1)
                for r in range(N_SEL // 8):
                    link(nc.vector.max(top8[:, :], work[r % 2]))
                    link(nc.vector.match_replace(work[1 - r % 2], top8[:, :], work[r % 2], TAKEN))
                link(nc.vector.tensor_scalar(SEL[b], work[0], TAKEN / 1.5, MASK, ALU.is_gt, ALU.mult))

            def finish(u):
                par = u.su % 2
                if u.kind == "I":
                    index_add(u)
                    return
                dve.wait_ge(probs, u.su + 1)
                done = [v.pu for v in UNITS[:max(u.su - 1, 0)] if v.pu is not None]
                if done:
                    dve.wait_ge(mixed, done[-1] + 1)
                link(nc.vector.reciprocal(rden[:, par, :], den[:, par, :]))
                if u.comb is None:
                    return
                link(nc.vector.tensor_scalar(rden[:, par, :], rden[:, par, :], lamc[:, 4 + u.layer:5 + u.layer], None, ALU.mult))
                for h in range(4):
                    s = head_slot(h)
                    p0 = PR[:, 1 - par, s, 0:u.nk]
                    ins = nc.vector.tensor_scalar(p0, p0, rden[:, 1 - par, h:h + 1], None, ALU.mult)
                link(ins)
                for h in range(4):
                    s = head_slot(h)
                    p0, p1 = PR[:, 1 - par, s, 0:u.nk], PR[:, par, s, 0:u.nk]
                    ins = nc.vector.scalar_tensor_tensor(p0, p1, rden[:, par, h:h + 1], p0, ALU.mult, ALU.add)
                ins.then_inc(combined, 1)

            def store(u):
                dve.wait_ge(o_ps, u.pu + 1)
                c = {"A": 0, "B": 256, "C": 512, "D": 768, "N": 0, "L": 512}[u.kind] + 256 * u.g.half
                dst = XN[:, u.b, c:c + 256].rearrange("p (h e) -> p h e", h=4)
                src = ps[:, 6, 0:256].rearrange("p (h e) -> p h e", h=4)
                if u.kind != "A":
                    nc.vector.tensor_tensor(dst, src, rden[:, u.su % 2, :].unsqueeze(2).broadcast_to([P, 4, HD]),
                                            ALU.mult).then_inc(mixed, 1)
                    return
                sq = FS[:, 1024:1280].rearrange("p (h e) -> p h e", h=4)
                link(nc.vector.tensor_copy(dst, src))
                link(nc.vector.tensor_tensor(sq, dst, dst, ALU.mult))
                link(nc.vector.tensor_reduce(rstd[:, 4:8], sq, AX_X, ALU.add))
                inverse_root((rstd[:, 4:8], rstd[:, 4:8], HD))
                link(nc.vector.tensor_tensor(dst, dst, rstd[:, 4:8].unsqueeze(2).broadcast_to([P, 4, HD]), ALU.mult))
                nc.vector.tensor_tensor(dst, dst, gdiff[:, u.layer, :].unsqueeze(1).broadcast_to([P, 4, HD]),
                                        ALU.mult).then_inc(mixed, 1)

            def rope(x, b):
                n = x.shape[1]
                cos = cossin[:, b, 0, :].unsqueeze(1).broadcast_to([P, n, 16])
                sin = cossin[:, b, 1, :].unsqueeze(1).broadcast_to([P, n, 16])
                x1, x2 = x[:, :, 0:16], x[:, :, 16:32]
                nc.vector.tensor_tensor(TR[:, 0, 0:n], x1, cos, ALU.mult)
                nc.vector.tensor_tensor(TR[:, 1, 0:n], x2, sin, ALU.mult)
                nc.vector.tensor_tensor(TR[:, 2, 0:n], x1, sin, ALU.mult)
                link(nc.vector.tensor_tensor(TR[:, 3, 0:n], x2, cos, ALU.mult))
                nc.vector.tensor_tensor(x1, TR[:, 0, 0:n], TR[:, 1, 0:n], ALU.subtract)
                link(nc.vector.tensor_tensor(x2, TR[:, 2, 0:n], TR[:, 3, 0:n], ALU.add))

            def prepare(g):
                if g.kind == "B":
                    dve.wait_ge(b_sq, 4 * (g.layer + 1))
                    inverse_root((rstd[:, 0:2], ss[:, 0:2], 256), (rstd[:, 2:4], ss[:, 2:4], 128))
                    for i, (c, w) in enumerate(((B_QD, 256), (B_KVD, 128))):
                        for b in range(NB):
                            ins = nc.vector.tensor_scalar(PROJ[:, b, c:c + w], PROJ[:, b, c:c + w],
                                                          rstd[:, 2 * i + b:2 * i + b + 1], None, ALU.mult)
                    ins.then_inc(b_normed, 1)
                    dve.wait_ge(filled, g.fill0 + 6)
                    for b in range(NB):
                        q = PROJ[:, b, B_UQ:B_UQ + 384].rearrange("p (h n) -> p h n", h=4)
                        rope(q[:, :, 64:96], b)
                        rope(PROJ[:, b, B_KR:B_KR + 32].unsqueeze(1), b)
                        kv = PROJ[:, b, B_UKV:B_UKV + 512].rearrange("p (h n) -> p h n", h=4)
                        nc.vector.tensor_copy(KB[:, b, :, 0:64], kv[:, :, 0:64])
                        ins = nc.vector.tensor_copy(KB[:, b, :, 64:96],
                                                    PROJ[:, b, B_KR:B_KR + 32].unsqueeze(1).broadcast_to([P, 4, 32]))
                    ins.then_inc(b_roped, 1)
                if g.kind == "C":
                    dve.wait_ge(fill_ps, g.fill0)
                    nc.vector.memset(KI4, 0.0)
                    for b in range(NB):
                        nc.vector.tensor_scalar(w16[:, b, :], PROJ[:, b, C_WI:C_WI + 8], (8 * 32) ** -0.5, None, ALU.mult)
                        ins = nc.vector.tensor_copy(PROJ[:, b, C_KIREP:C_KIREP + P].rearrange("p (h n) -> p h n", h=4),
                                                    PROJ[:, b, C_KI:C_KI + 32].unsqueeze(1).broadcast_to([P, 4, 32]))
                    ins.then_inc(c_ready, 1)

            def attention(layer):
                us = units_of(layer)
                dve.wait_ge(gemm_out, 2 * sum(GEMM_GROUPS[:2 * layer + 1]))
                bias(us[0])
                for n, u in enumerate(us):
                    if u.first_of_group and u.g.gi + 1 < len(GROUPS) and GROUPS[u.g.gi + 1].layer == layer:
                        prepare(GROUPS[u.g.gi + 1])
                    if n + 1 < len(us) and us[n + 1].kind != "I":
                        bias(us[n + 1])
                    finish(u)
                    if n >= 1 and us[n - 1].pu is not None:
                        store(us[n - 1])
                store(us[-1])

            def route():
                dve.wait_ge(late_in, 16 * 5)
                nc.vector.memset(r_logit, -3.0e38)
                link(nc.vector.memset(r_take, -3.0e38))
                dve.wait_ge(route_ps, 1)
                link(nc.vector.tensor_copy(r_logit[:, :, 0:8], ps[:, 7, 0:16].rearrange("p (b n) -> p b n", b=NB)))
                for b in range(NB):
                    ins = nc.vector.max(r_top[:, b, :], r_logit[:, b, 0:8])
                link(ins)
                nc.vector.tensor_scalar(r_nv1, r_top[:, :, 0:1].rearrange("p b a -> p (b a)"), -1.0, None, ALU.mult).then_inc(route_max, 1)
                link(nc.vector.tensor_copy(r_take[:, :, 0:2], r_top[:, :, 0:2]))
                for b in range(NB):
                    ins = nc.vector.match_replace(r_marked[:, b, :], r_take[:, b, :], r_logit[:, b, :], 3.0e38)
                link(ins)
                nc.vector.tensor_scalar(r_sel, r_marked[:, :, 0:8], 1.0e38, None, ALU.is_ge).then_inc(route_sel, 1)
                dve.wait_ge(route_exp, 1)
                link(nc.vector.tensor_scalar(r_den, r_e2, 1.0, None, ALU.add))
                link(nc.vector.reciprocal(r_den, r_den))
                dve.wait_ge(route_sel, 1)
                link(nc.vector.tensor_tensor(r_comb, r_exp, r_sel, ALU.mult))
                link(nc.vector.tensor_tensor(r_comb, r_comb, r_den.unsqueeze(2).broadcast_to([P, NB, 8]), ALU.mult))
                dve.wait_ge(rank_ps, 1)
                link(nc.vector.scalar_tensor_tensor(r_rank, ps[:, 7, 0:16].rearrange("p (b n) -> p b n", b=NB), 1000.0,
                                                    r_sel, ALU.add, ALU.mult))
                link(nc.vector.tensor_scalar(r_rank, r_rank, -1000.0, None, ALU.add))
                link(nc.vector.tensor_reduce(r_cnt[0:1, :], ps[0:1, 7, 16:24], AX_X, ALU.max))
                link(nc.vector.memset(YB, 0.0))
                nc.vector.tensor_scalar(flag[:, :], r_cnt[0:1, :], float(P), None, ALU.is_gt).then_inc(route_ready, 1)

            def experts(m):
                with dve.Fori(0, EXPERTS) as e:
                    k_e = e * EX_STEPS
                    nc.vector.tensor_scalar(r_rk, r_rank[:, :, bass.ds(e, 1)].rearrange("p b a -> p (b a)"),
                                            -float(P) * m["sweep"], None, ALU.add)
                    nc.vector.tensor_copy(r_cb, r_comb[:, :, bass.ds(e, 1)].rearrange("p b a -> p (b a)")).then_inc(m["sel_copied"], 1)
                    dve.wait_ge(m["sel_copied"], e + 1)
                    for b in range(NB):
                        ins = nc.vector.tensor_scalar(PSEL[:, b, :], iota, r_rk[:, b:b + 1], None, ALU.is_equal)
                    ins.then_inc(m["psel"], 1)
                    dve.wait_ge(m["psel"], e + 1)
                    for b in range(NB):
                        ins = nc.vector.tensor_scalar(WSEL[:, b, :], PSEL[:, b, :], r_cb[:, b:b + 1], None, ALU.mult)
                    ins.then_inc(m["wsel"], 1)
                    with dve.Fori(0, EX_STEPS // 2) as t:
                        for s in range(2):
                            h_product(m["silu_ready"], m["h_ready"], t * 2 + k_e + (1 + s), s)
                    for b in range(NB):
                        dve.wait_ge(m["sc_ps"], e * 2 + (b + 1))
                        nc.vector.tensor_tensor(YB[:, b, :], YB[:, b, :], ps[:, 2:4, :].rearrange("p j n -> p (j n)"),
                                                ALU.add).then_inc(m["sc_added"], 1)

            nc.vector.memset(zero[:, :], 0.0).then_inc(zero_ready, 1)
            dve.wait_ge(const_in, 16 * N_CONST)
            v = lam_in.rearrange("p l (i a n) -> p l i a n", i=2, a=2)
            for l in range(LAYERS):
                for i in range(2):
                    link(nc.vector.tensor_tensor(lam_pr[:, l, 32 * i:32 * (i + 1)], v[:, l, i, 0, :], v[:, l, i, 1, :], ALU.mult))
            nc.vector.tensor_reduce(lamc[:, 4:8], lam_pr[:, :, :].rearrange("p l (i n) -> p (l i) n", i=2), AX_X,
                                    ALU.add).then_inc(lam_exp_in, 1)
            dve.wait_ge(lam_exp_out, 1)
            for l in range(LAYERS):
                lam_init = 0.8 - 0.6 * math.exp(-0.3 * l)
                link(nc.vector.tensor_tensor(lamc[:, 4 + l:5 + l], lamc[:, 2 * l + 1:2 * l + 2], lamc[:, 2 * l:2 * l + 1],
                                             ALU.subtract))
                link(nc.vector.tensor_scalar(lamc[:, 4 + l:5 + l], lamc[:, 4 + l:5 + l], -lam_init, None, ALU.add))
                link(nc.vector.tensor_scalar(gdiff[:, l, :], gdiff[:, l, :], 1.0 - lam_init, None, ALU.mult))
            dve.wait_ge(csilu_ready, 1)
            for a in range(ADA_EARLY):
                ada_step(a)
            for layer in range(LAYERS):
                mod_columns(0, layer, 1 + 6 * layer)
                if layer == 1:
                    mod_rows(gate_mix, row0, 8)
                    mod_columns(3, layer, 10)
                    mod_rows(gate_ffn, row1, 11)
                set_xscale(0, layer)
                normalise(3 * layer)
                ahead_lo(GEMM_CHUNK[2 * layer])
                copy_xt(3 * layer)
                if layer == 1:
                    gemm_lo(2)
                else:
                    gemm_lo(0, lambda p: ada_step(ADA_EARLY + p - SPLITS) if p - SPLITS < ADA_MID - ADA_EARLY else None)
                    mod_rows(gate_mix, gate_mix, 2)
                    mod_columns(3, layer, 4)
                    mod_rows(gate_ffn, gate_ffn, 5)
                attention(layer)
                ahead_lo(GEMM_CHUNK[2 * layer + 1])
                copy_xt(3 * layer + 1)
                gemm_lo(2 * layer + 1)
                add_gated(gate_mix, gemm_out, 2 * sum(GEMM_GROUPS[:2 * layer + 2]))
                set_xscale(3, layer)
                normalise(3 * layer + 2)
                if layer == 0:
                    ahead_lo(FFN_CHUNK[0])
                copy_xt(3 * layer + 2)
                if layer == 0:
                    ffn(0)
                    add_gated(gate_ffn, y_out, 2)
                else:
                    route()
                    experts(moe_sems[0])
                    dve.wait_ge(route_ready, 1)
                    over = dve.value_load(flag[0:1, 0:1], min_val=0, max_val=1)
                    with dve.If(over > 0):
                        experts(moe_sems[1])
                        dve.wait_ge(moe_sems[1]["sc_added"], 2 * EXPERTS)
                    add_gated(gate_ffn, moe_sems[0]["sc_added"], 2 * EXPERTS)
            dve.wait_ge(res_sq, 2)
            dve.wait_ge(rows_in, 32)
            inverse_root((rstd[:, 4:6], ss[:, 4:6], D))
            for b in range(NB):
                ins = nc.vector.scalar_tensor_tensor(X[:, b, :], X[:, b, :], rstd[:, 4 + b:5 + b], row0[:, :], ALU.mult, ALU.mult)
            ins.then_inc(x_ready, 1)
            for b in range(NB):
                for g in range(2):
                    link(nc.vector.tensor_tensor(dil_bias[:, b, g], dil_bias[:, b, g],
                                                 lnm[:, b, :].unsqueeze(1).broadcast_to([P, 4, T]), ALU.add))
            normalise(6)
            ahead_lo(FFN_CHUNK[1])
            copy_xt(6)
            ffn(1)
            add_normed(row1, 2, 0.5)
            normalise(7)
            ahead_lo(GEMM_CHUNK[4])
            copy_xt(7)
            gemm_lo(4)
            attention(2)
            normalise(8)
            ahead_lo(GEMM_CHUNK[5])
            copy_xt(8)
            gemm_lo(5)
            dve.wait_ge(rows_in2, 32)
            add_normed(gate_mix, 3, 1.0)
            normalise(9)
            ahead_lo(FFN_CHUNK[2])
            copy_xt(9)
            ffn(2)
            add_normed(gate_ffn, 4, 0.5)



def product_chunks(w, groups):
    w = np.pad(w, ((0, 0), (0, groups * 512 - w.shape[1])))
    return w.reshape(2, 4, P, groups, 512).transpose(3, 0, 2, 1, 4).reshape(2 * groups, P, CHW)


def ffn_chunks(w1, w3, w2):
    steps = w1.shape[1] // FW
    up = np.stack([w1.reshape(2, 4, P, steps, FW), w3.reshape(2, 4, P, steps, FW)], axis=4)
    up = up.transpose(3, 0, 2, 1, 4, 5).reshape(steps, 2, P, CHW)
    down = w2.reshape(steps, 2, P, D).transpose(0, 2, 1, 3).reshape(steps, 1, P, CHW)
    out = np.empty((3 * steps, P, CHW), np.float32)
    out[0:2] = up[0]
    mid = out[2:-1].reshape(steps - 1, 3, P, CHW)
    mid[:, 0:2] = up[1:]
    mid[:, 2:3] = down[:-1]
    out[-1] = down[-1, 0]
    return out


def columns(v):
    return v.reshape(-1, P).T


def slotted(table):
    order = [h for s in range(4) for h in range(4) if head_slot(h) == s]
    t = table.reshape(-1, 4, NB, P, T)[:, order]
    return t.transpose(3, 2, 0, 1, 4)


def causal_pack(t):
    return np.concatenate([t[:, 0, 0, :, 0:P].reshape(P, -1), t[:, 1, 0].reshape(P, -1)], axis=1)


def arrays_of(i):
    i = {k: np.asarray(v) for k, v in i.items()}
    q, k = np.arange(T)[:, None], np.arange(T)[None, :]
    allowed = k // 64 <= q // 64
    slopes = (2.0 ** (-8.0 * np.arange(1, 5) / 4)).astype(np.float32)
    alibi = np.where(allowed, -slopes[:, None, None] * np.abs(q - k).astype(np.float32), np.float32(MASK)).astype(np.float32)
    cmask = np.where(allowed, np.float32(0), np.float32(MASK)).astype(np.float32)
    cm = cmask.reshape(NB, P, T)
    rel = np.clip(q - k, -128, 128) + 128
    band = np.stack([causal_pack(slotted(np.where(allowed, i["band_rel_bias"][l][:, rel], np.float32(MASK)))) for l in range(LAYERS)])
    qr, qc, kr, kc = q // 64, q % 64, k // 64, k % 64
    start = np.clip(qc - 8, 0, 48)
    near = (kc >= start) & (kc < start + 16)
    na = np.where(near, i["na_rel_bias_2"][0][:, kr - qr + 7, np.clip(kc - qc + 15, 0, 30)], np.float32(MASK))
    off = k - q
    member = [np.abs(off) <= 64, off % 4 == 0, off % 16 == 0]
    times = sum(m.astype(np.int64) for m in member)
    dist = np.abs(off)
    large = 8 + (np.log(np.maximum(dist, 1).astype(np.float32) / 8) / math.log(1024 / 8) * 8).astype(np.int32)
    bucket = np.where(off > 0, 16, 0) + np.where(dist < 8, dist, np.minimum(large, 15))
    dil = np.where(times > 0, i["t5_rel_bias_2"][:, bucket], np.float32(MASK))
    lnm = np.log(np.maximum(times, 1)).astype(np.float32).reshape(NB, P, T).transpose(1, 0, 2).reshape(P, NB * T)
    inv = np.float32(10000.0) ** (-np.arange(0, 32, 2, dtype=np.float32) / np.float32(32))
    ang = np.arange(T, dtype=np.float32)[:, None] * inv[None, :]
    cossin = np.stack([np.cos(ang), np.sin(ang)], axis=1).reshape(NB, P, 2, 16).transpose(1, 0, 2, 3).reshape(P, 64)
    ada_b = i["ada_b"].reshape(LAYERS, 6, D)
    stream = np.concatenate([
        product_chunks(i["w_in"][0], 6), product_chunks(i["w_out"][0], 2),
        ffn_chunks(i["ffn_w1"][0], i["ffn_w3"][0], i["ffn_w2"][0]),
        product_chunks(i["w_in"][1], 6), product_chunks(i["w_out"][1], 2),
        *[ffn_chunks(i["moe_w1"][0, e], i["moe_w3"][0, e], i["moe_w2"][0, e]) for e in range(EXPERTS)],
        ffn_chunks(i["ffn1_w_gate_2"][0], i["ffn1_w_up_2"][0], i["ffn1_w_down_2"][0]),
        product_chunks(i["w_qkv_2"][0], 6), product_chunks(i["w_out_2"][0], 2),
        ffn_chunks(i["ffn2_w_gate_2"][0], i["ffn2_w_up_2"][0], i["ffn2_w_down_2"][0])])
    ada = i["ada_w"].reshape(LAYERS, 4, 2, P, 6, D).transpose(0, 4, 1, 3, 2, 5).reshape(ADA_CHUNKS, P, CHW)
    cols = np.concatenate([columns(v) for v in (
        i["mix_norm_g"], i["ffn_norm_g"], i["ffn1_pre_g_2"], i["mix_pre_g_2"], i["ffn2_pre_g_2"],
        np.concatenate([i["na_out_g_2"][0], i["dil_out_g_2"][0]]), ada_b, i["mla_q_norm_g"], i["mla_kv_norm_g"], i["c"])], axis=1)
    rows = np.stack([ada_b[0, 2], ada_b[0, 5], ada_b[1, 2], ada_b[1, 5], i["final_norm_g"], i["ffn1_post_g_2"][0],
                     i["mix_post_g_2"][0], i["ffn2_post_g_2"][0]])
    tri = (np.arange(P)[:, None] < np.arange(P)[None, :]).astype(np.float32)
    iota = np.broadcast_to(np.arange(P, dtype=np.float32), (P, P))
    out = dict(
        x=i["x"], stream=stream, ada=ada, cols=cols, rows=rows,
        lam=i["diff_lambda"].reshape(1, 256), gdiff=i["diff_norm_g"].reshape(1, 128),
        unit=np.concatenate([np.eye(P), np.ones((P, P))], axis=1), cossin=cossin,
        alibi=causal_pack(slotted(alibi)), cmask=np.concatenate([cm[0, :, 0:P], cm[1]], axis=1), band=band,
        uq=i["mla_w_uq"].reshape(LAYERS, 2, P, 384).transpose(0, 2, 1, 3).reshape(LAYERS, P, 768), ukv=i["mla_w_ukv"],
        na=slotted(na).reshape(P, -1), dil=slotted(dil).reshape(P, -1), lnm=lnm,
        tri_iota=np.concatenate([tri, iota], axis=1),
        router=i["moe_router"][0].reshape(KT, P, 8).transpose(1, 0, 2).reshape(P, 64))
    return {n: np.ascontiguousarray(a, dtype=np.float32) for n, a in out.items()}


def kernel(**inputs):
    import concourse.bacc as bacc
    from concourse.bass_utils import run_bass_kernel_spmd

    nc = bacc.Bacc("TRN2", target_bir_lowering=False, num_devices=1)
    arrays = {f"in_{n}": a for n, a in arrays_of(inputs).items()}
    aps = {n[3:]: nc.dram_tensor(n, a.shape, F32, kind="ExternalInput").ap() for n, a in arrays.items()}
    aps["out"] = nc.dram_tensor("out", (1, T, D), F32, kind="ExternalOutput").ap()
    program(nc, aps)
    r = run_bass_kernel_spmd(nc, [arrays], core_ids=[0])
    return r.results[0]["out"]
```

```python
import math
from contextlib import ExitStack

import concourse.bass as bass
import numpy as np
from concourse import mybir

F32 = mybir.dt.float32
F32R = mybir.dt.float32r
BF16 = mybir.dt.bfloat16
I32 = mybir.dt.int32
ALU = mybir.AluOpType
ACT = mybir.ActivationFunctionType
AX_X = mybir.AxisListType.X

P = 128
T = 256
NB = T // P
D = 1024
KT = D // P
CHW = 2048
RING = 6
PIECE = CHW // 2
SPLITS = 4
ADA_RING = 2
LAYERS = 2
D_IN, D_IN_PAD = 3016, 3072
FW = 256
FF_STEPS = 2816 // FW
EX_STEPS = 3584 // FW
EXPERTS = 8
EPS = 1e-6
MASK = -1e30
TAKEN = -3.0e38
N_SEL = 64
HD = 64

A_Q, A_K, A_V, B_QD, B_KVD, B_KR = 0, 256, 512, 768, 1024, 1152
C_Q, C_K, C_V, C_QI, C_KI, C_WI, D_Q, D_K, D_V = 1184, 1440, 1696, 1952, 2208, 2240, 2248, 2504, 2760
B_UQ = B_QD
B_UKV = A_Q
C_WORK = B_QD + P
C_KIREP = B_QD

GEMM_GROUPS = [6, 2, 6, 2, 6, 2]
FF_CHUNKS, EX_CHUNKS = 3 * FF_STEPS, 3 * EX_STEPS
IN0_CHUNK = 0
OUT0_CHUNK = IN0_CHUNK + 12
FFN0_CHUNK = OUT0_CHUNK + 4
IN1_CHUNK = FFN0_CHUNK + FF_CHUNKS
OUT1_CHUNK = IN1_CHUNK + 12
MOE_CHUNK = OUT1_CHUNK + 4
FFN1_CHUNK = MOE_CHUNK + EXPERTS * EX_CHUNKS
QKV_CHUNK = FFN1_CHUNK + FF_CHUNKS
OUT2_CHUNK = QKV_CHUNK + 12
FFN2_CHUNK = OUT2_CHUNK + 4
N_CHUNKS = FFN2_CHUNK + FF_CHUNKS
GEMM_CHUNK = [IN0_CHUNK, OUT0_CHUNK, IN1_CHUNK, OUT1_CHUNK, QKV_CHUNK, OUT2_CHUNK]
FFN_CHUNK = [FFN0_CHUNK, FFN1_CHUNK, FFN2_CHUNK]
EX_TOTAL = EXPERTS * EX_CHUNKS
assert EX_CHUNKS % RING == 0 and 2 * RING % SPLITS == 0 and EX_STEPS % 2 == 0
N_WORK = 8448
HTH_AT, HTL_AT = 5120, 5632
ADA_AHEAD = [(0, 0), (0, CHW), (0, 2 * CHW), (1, 0), (1, CHW), (1, 2 * CHW)]

ADA_CHUNKS = LAYERS * 6 * 4
ADA_EARLY = 8
ADA_MID = 26
ADA_IN_B = 5

COL = {}
_at = 0
for _name, _n in (("mix_g", 16), ("ffn_g", 16), ("f1_g", 8), ("mp_g", 8), ("f2_g", 8), ("out_g", 8), ("ada_b", 96),
                  ("q_g", 4), ("kv_g", 2), ("c", 8)):
    COL[_name] = _at
    _at += _n
N_COLS = _at

XG_AT, YE_AT, PS_AT, WS_AT, CT_AT = 2048, 3072, 4096, 4352, 4608
Z_WORDS = 6 * D + ADA_RING * CHW
NA_AT, DIL_AT, TRI_AT, IOTA_AT, RW_AT, LNM_AT, RT_AT = 0, 4096, 8192, 8320, 8448, 8512, 9024
FS_WORDS = 1536


def head_slot(h):
    return (h % 2) * 2 + h // 2


class Group:
    def __init__(self, kind, half, layer, gi):
        self.kind, self.half, self.layer, self.gi = kind, half, layer, gi
        self.units, self.fill0, self.n_fills = [], 0, 0


class Unit:
    def __init__(self, kind, b, part, g, su):
        self.kind, self.b, self.part, self.g, self.layer, self.su = kind, b, part, g, g.layer, su
        self.nk = P * (b + 1) if g.layer < LAYERS else T
        self.bi = self.pu = self.idx = self.comb = None
        self.first_of_group = not g.units


def attention_plan():
    groups, units = [], []
    count = {"su": 0, "bi": 0, "pu": 0, "fill": 0, "idx": 0, "comb": 0}

    def take(name):
        count[name] += 1
        return count[name] - 1

    for layer in range(LAYERS + 1):
        kinds = "ABCD" if layer < LAYERS else ["N0", "N1", "L0", "L1"]
        first = len(groups)
        for kind in kinds:
            groups.append(Group(kind[0], int(kind[1]) if len(kind) > 1 else 0, layer, len(groups)))
        for g in groups[first:]:
            g.fill0 = count["fill"]
            g.n_fills = {"A": 2, "B": 10, "C": 4, "D": 2, "N": 2, "L": 2}[g.kind]
            count["fill"] += g.n_fills
        for g in groups[first:]:
            todo = {"A": [("A", b, c) for b in range(NB) for c in range(2)],
                    "C": [("I", b, hg) for b in range(NB) for hg in range(2)] + [("C", b, 0) for b in range(NB)]}
            for kind, b, part in todo.get(g.kind, [(g.kind, b, 0) for b in range(NB)]):
                u = Unit(kind, b, part, g, take("su"))
                if kind == "I":
                    u.idx = take("idx")
                else:
                    u.bi = take("bi")
                    if not (kind == "A" and part == 0):
                        u.pu = take("pu")
                    if kind == "A" and part == 1:
                        u.comb = take("comb")
                g.units.append(u)
                units.append(u)
    return groups, units


GROUPS, UNITS = attention_plan()
N_CONST = 8
SPLIT_NO = {t: t if t < 5 else t - 1 for t in range(10) if t != 5}
NORM_NO = {0: 1, 2: 2, 3: 3, 5: 4, 6: 5, 7: 6, 8: 7, 9: 8}
SQUARES = {0: 2, 2: 4, 3: 6, 5: 8, 6: 10, 7: 12, 8: 16, 9: 18}
X_READY = {2: 1, 3: 2, 5: 3, 6: 5, 7: 6, 9: 7}


def release(u):
    if u.kind == "I":
        return "idx", u.idx + 1
    if u.kind == "A" and u.part == 1:
        return "comb", u.comb + 1
    return "pT", (UNITS[u.su + 1] if u.kind == "A" else u).pu + 1


def piece_no(chunk, half=0):
    return 2 * chunk + half


def fill_part(u):
    if u.g.gi + 1 == len(GROUPS) or GROUPS[u.g.gi + 1].layer != u.layer:
        return None
    g, i = GROUPS[u.g.gi + 1], u.g.units.index(u)
    parts = [(0, 4), (4, 6), (6, 8), (8, 10)] if g.kind == "B" else [(0, g.n_fills)]
    return (g, *parts[i]) if i < len(parts) else None


def last_of_group(u):
    return u is u.g.units[-1]


def units_of(layer):
    return [u for u in UNITS if u.layer == layer]


def pu_end(layer):
    return max(u.pu for u in UNITS if u.layer == layer and u.pu is not None) + 1


def stream_turns(eng, n_steps, per_step, first_chunk, body):
    per_turn = RING // per_step
    turns = n_steps // per_turn
    if turns > 1:
        with eng.Fori(0, turns) as turn:
            for s in range(per_turn):
                body(first_chunk + s * per_step, turn, s)
    else:
        turns = 0
    for s in range(turns * per_turn, n_steps):
        body(first_chunk + s * per_step, 0, s)


def program(nc, d):
    with ExitStack() as ctx:
        def sb(name, shape, dt=F32):
            return ctx.enter_context(nc.sbuf_tensor(name, shape, dt))

        def sem(name):
            return ctx.enter_context(nc.semaphore(name))

        arena = sb("arena", [P, N_WORK + NB * D_IN_PAD])
        arena_at = nc.sbuf_base - 4 * (N_WORK + NB * D_IN_PAD)

        def split(name, shape, word):
            return nc.alloc_sbuf_tensor_at(name, [P] + shape, F32R, offset=arena_at + 4 * word)

        WH = split("weights_high", [SPLITS, PIECE], 0)
        WL = split("weights_low", [SPLITS, PIECE], SPLITS * PIECE)
        hTH = split("hT_high", [NB, 2, P], N_WORK + HTH_AT)
        hTL = split("hT_low", [NB, 2, P], N_WORK + HTL_AT)
        XTH = sb("xt_high", [P, KT, T], F32R)
        XTL = sb("xt_low", [P, KT, T], F32R)
        ring = sb("ring", [P, RING, CHW])
        X = sb("X", [P, NB, D])
        XN = sb("XN", [P, NB, D])
        gate_mix = sb("gate_mix", [P, D])
        gate_ffn = sb("gate_ffn", [P, D])
        Z = sb("Z", [P, Z_WORDS])
        alibi = sb("alibi", [P, 1536])
        band = sb("band", [P, 1536])
        cmask = sb("cmask", [P, 384])
        FS = sb("FS", [P, FS_WORDS])
        unit = sb("unit", [P, 2 * P])
        ident, ones = unit[:, 0:P], unit[:, P:2 * P]
        cols = sb("cols", [P, N_COLS])
        cossin = sb("cossin", [P, NB, 2, 16])
        gdiff = sb("gdiff", [P, LAYERS, HD])
        modc = sb("modc", [P, 32])
        xscale = sb("xscale", [P, KT])
        csilu = sb("csilu", [P, KT])
        ss = sb("ss", [P, 8])
        rstd = sb("rstd", [P, 8])
        nmax = sb("nmax", [P, 2, 4])
        den = sb("den", [P, 2, 4])
        rden = sb("rden", [P, 2, 4])
        lamc = sb("lamc", [P, 8])
        w16 = sb("w16", [P, NB, 8])
        top8 = sb("top8", [P, 8])
        minus_half = sb("minus_half", [P, 8])
        flag = sb("flag", [1, 1], I32)
        ps = ctx.enter_context(nc.psum_tensor("ps", [P, 8, 512], F32))

        QK = arena[:, 0:4096].rearrange("p (g n) -> p g n", g=2)
        PR = arena[:, 4096:6144].rearrange("p (u s k) -> p u s k", u=2, s=4)
        PT = arena[:, 6144:7168].rearrange("p (h b q) -> p h b q", h=4, b=NB)
        UQ = arena[:, 7168:7936].rearrange("p (k n) -> p k n", k=2)
        UKV = arena[:, 7936:8448]
        proj_words = arena[:, N_WORK:]
        PROJ = proj_words.rearrange("p (b n) -> p b n", b=NB)
        XT = proj_words[:, 0:KT * T].rearrange("p (k n) -> p k n", k=KT)
        YB = proj_words[:, 0:NB * D].rearrange("p (b n) -> p b n", b=NB)
        XG = proj_words[:, XG_AT:XG_AT + D].rearrange("p (k s) -> p k s", k=KT)
        YE = proj_words[:, YE_AT:YE_AT + D]
        PSEL = proj_words[:, PS_AT:PS_AT + T].rearrange("p (b s) -> p b s", b=NB)
        WSEL = proj_words[:, WS_AT:WS_AT + T].rearrange("p (b s) -> p b s", b=NB)
        CT = proj_words[:, CT_AT:CT_AT + T].rearrange("p (b s) -> p b s", b=NB)
        ada_acc = Z[:, 0:6 * D].rearrange("p (m n) -> p m n", m=6)
        ada_ring = Z[:, 6 * D:Z_WORDS].rearrange("p (s n) -> p s n", s=ADA_RING)
        final_g, f1_post_g = alibi[:, 0:D], band[:, 0:D]
        ada_places = [(proj_words if in_proj else arena)[:, word:word + CHW] for in_proj, word in ADA_AHEAD]
        na_bias = Z[:, NA_AT:NA_AT + 4096].rearrange("p (b g h k) -> p b g h k", b=2, g=2, h=4)
        dil_bias = Z[:, DIL_AT:DIL_AT + 4096].rearrange("p (b g h k) -> p b g h k", b=2, g=2, h=4)
        lnm = Z[:, LNM_AT:LNM_AT + 512].rearrange("p (b k) -> p b k", b=2)
        tri = Z[:, TRI_AT:TRI_AT + P]
        iota = Z[:, IOTA_AT:IOTA_AT + P]
        router = Z[:, RW_AT:RW_AT + 64].rearrange("p (k e) -> p k e", k=KT)

        def rt(i, n):
            return Z[:, RT_AT + i:RT_AT + i + n]

        r_logit = rt(0, 32).rearrange("p (b n) -> p b n", b=NB)
        r_marked = rt(32, 32).rearrange("p (b n) -> p b n", b=NB)
        r_top = rt(64, 16).rearrange("p (b n) -> p b n", b=NB)
        r_take = rt(80, 16).rearrange("p (b n) -> p b n", b=NB)
        r_sel = rt(96, 16).rearrange("p (b n) -> p b n", b=NB)
        r_exp = rt(112, 16).rearrange("p (b n) -> p b n", b=NB)
        r_comb = rt(128, 16).rearrange("p (b n) -> p b n", b=NB)
        r_rank = rt(176, 18).rearrange("p (b n) -> p b n", b=NB)
        r_nv1 = rt(160, 2)
        r_e2 = rt(162, 2)
        r_den = rt(164, 2)
        r_cnt = rt(166, 1)
        r_rk = rt(168, 2)
        r_cb = rt(170, 2)

        sgt = FS[:, 0:512].rearrange("p (b n) -> p b n", b=2)
        XGH = XTH[:, 0:4, :].rearrange("p a (c s) -> p (a c) s", c=2)
        XGL = XTL[:, 0:4, :].rearrange("p a (c s) -> p (a c) s", c=2)
        hbuf = FS[:, 512:1024].rearrange("p (b n) -> p b n", b=2)
        KB = FS[:, 0:768].rearrange("p (b h n) -> p b h n", b=2, h=4)
        KI4 = FS[:, 0:1024].rearrange("p (h n) -> p h n", h=4)
        SEL = [FS[:, 1280:1408], FS[:, 1024:1280]]
        TR = FS[:, 1280:1536].rearrange("p (i h n) -> p i h n", i=4, h=4)
        junk = FS[:, 1280:1536]
        lam_in = FS[:, 0:256].rearrange("p (l n) -> p l n", l=LAYERS)
        lam_pr = FS[:, 256:384].rearrange("p (l n) -> p l n", l=LAYERS)
        zero = sb("zero", [1, P], BF16)
        finite = unit[0:1, :].bitcast(BF16)

        full = [sem(f"ring_full{i}") for i in range(RING)]
        hi_ready, lo_ready, piece_done = sem("hi_ready"), sem("lo_ready"), sem("piece_done")
        xt_full, xt_hi, hT_hi, latent_in = (sem(n) for n in ("xt_full", "xt_hi", "hT_hi", "latent_in"))
        ada_ahead = [sem(f"ada_ahead{i}") for i in range(len(ADA_AHEAD))]
        full_o = [sem(f"ring_full_overflow{i}") for i in range(RING)]
        lo_ready_o = sem("lo_ready_overflow")
        ada_full = [sem(f"ada_full{i}") for i in range(ADA_RING)]
        ada_half, ada_used = sem("ada_half"), sem("ada_used")
        cols_in, gates_in = sem("cols_in"), sem("gates_in")
        x_in, const_in, late_in, layer_in, rows_in, rows_in2 = (
            sem(n) for n in ("x_in", "const_in", "late_in", "layer_in", "rows_in", "rows_in2"))
        out_done = sem("out_done")
        zero_ready, csilu_ready, lam_exp_in, lam_exp_out = (sem(n) for n in ("zero_ready", "csilu_ready", "lam_exp_in", "lam_exp_out"))
        mod_ps, mod_ready, mod_cols = sem("mod_ps"), sem("mod_ready"), sem("mod_cols")
        sq_ready, xn_ready, xt_ps, xt_ready = (sem(n) for n in ("sq_ready", "xn_ready", "xt_ps", "xt_ready"))
        gemm_out = sem("gemm_out")
        silu_ready, h_ready, hT_ps, hT_ready = (sem(n) for n in ("silu_ready", "h_ready", "hT_ps", "hT_ready"))
        y_out = sem("y_out")
        res_sq, x_ready = sem("res_sq"), sem("x_ready")
        fill_ps, filled = sem("fill_ps"), sem("filled")
        b_sq, b_normed, b_roped, c_ready = (sem(n) for n in ("b_sq", "b_normed", "b_roped", "c_ready"))
        scores, biased, probs, combined, idx_added = (sem(n) for n in ("scores", "biased", "probs", "combined", "idx_added"))
        pT_ps, pT_ready, o_ps, mixed = (sem(n) for n in ("pT_ps", "pT_ready", "o_ps", "mixed"))
        route_ps, route_max, route_exp, route_sel, rank_ps, route_ready = (
            sem(n) for n in ("route_ps", "route_max", "route_exp", "route_sel", "rank_ps", "route_ready"))
        dve_chain, root_in, root_out, half_ready = (sem(n) for n in ("dve_chain", "root_in", "root_out", "half_ready"))
        moe_sems = []
        for sweep, tag in enumerate(("", "_overflow")):
            m = {n: sem("moe_" + n + tag) for n in (
                "sel_copied", "psel", "wsel", "xg_ps", "xg_full", "xg_hi", "xg_ready", "silu_ready",
                "h_ready", "hT_ps", "hT_hi", "hT_ready", "ct_ps", "ye_ready", "sc_ps", "sc_added")}
            if sweep == 0:
                m.update(full=full, hi_ready=hi_ready, lo_ready=lo_ready, piece_done=piece_done,
                         first=piece_no(MOE_CHUNK), freed=piece_no(MOE_CHUNK))
            else:
                m.update(full=full_o, lo_ready=lo_ready_o, hi_ready=sem("hi_ready_overflow"),
                         piece_done=sem("piece_done_overflow"), first=0, freed=SPLITS)
            m["sweep"] = sweep
            moe_sems.append(m)

        stream, ada = d["stream"], d["ada"]

        def chunk_loaded(eng, m, local, turn):
            before = (MOE_CHUNK if m["sweep"] == 0 else 0) + local
            eng.wait_ge(m["full"][(MOE_CHUNK + local) % RING], turn * 16 + 16 * (before // RING + 1))

        def expert_piece(local, half):
            return (ring[:, (MOE_CHUNK + local) % RING, half * PIECE:(half + 1) * PIECE],
                    piece_no(MOE_CHUNK + local, half) % SPLITS)

        block = ctx.enter_context(nc.Block())

        @block.sync
        def _(sp):
            sp.dma_start(X[:, :, :], d["x"].rearrange("a (b p) n -> p (a b) n", p=P)).then_inc(x_in, 16)

            def load_chunks(first, count):
                def load(n, turn, s):
                    sp.wait_ge(lo_ready, turn * (2 * RING) + piece_no(n - RING, 2))
                    src = stream[bass.ds(turn * RING + n, 1)].rearrange("a p n -> (a p) n")
                    sp.dma_start(ring[:, n % RING, :], src).then_inc(full[n % RING], 16)
                stream_turns(sp, count, 1, first, load)

            for n in range(RING):
                if n in (0, 2):
                    sp.wait_ge(ada_ahead[2 if n == 0 else -1], 16)
                sp.dma_start(ring[:, n, :], stream[n]).then_inc(full[n], 16)
            load_chunks(RING, FFN1_CHUNK - RING)

            sp.wait_ge(route_ready, 1)
            over = sp.value_load(flag[0:1, 0:1], min_val=0, max_val=1)
            with sp.If(over > 0):
                sp.wait_ge(lo_ready, piece_no(FFN1_CHUNK))
                s0 = MOE_CHUNK % RING
                for n in range(RING):
                    sp.dma_start(ring[:, (s0 + n) % RING, :], stream[MOE_CHUNK + n]).then_inc(full_o[(s0 + n) % RING], 16)
                with sp.Fori(1, EXPERTS * EX_CHUNKS // RING) as turn:
                    for n in range(RING):
                        sp.wait_ge(lo_ready_o, turn * (2 * RING) + 2 * (n - RING + 1))
                        src = stream[bass.ds(turn * RING + (MOE_CHUNK + n), 1)].rearrange("a p n -> (a p) n")
                        sp.dma_start(ring[:, (s0 + n) % RING, :], src).then_inc(full_o[(s0 + n) % RING], 16)
                sp.wait_ge(lo_ready_o, 2 * EX_TOTAL)
            load_chunks(FFN1_CHUNK, N_CHUNKS - FFN1_CHUNK)

            out = d["out"].rearrange("a (b p) n -> p (a b) n", p=P)
            for b in range(NB):
                sp.wait_ge(x_ready, 15 + b)
                sp.dma_start(out[:, b, :], X[:, b, :]).then_inc(out_done, 16)
            sp.wait_ge(out_done, 16 * NB)

        @block.gpsimd
        def _(pool):
            def load_ada(a, turn=0):
                before = a - ADA_RING if a >= ADA_EARLY + ADA_RING else a - ADA_EARLY
                pool.wait_ge(ada_used, turn * ADA_RING + (before + 1))
                src = ada[bass.ds(turn * ADA_RING + a, 1)].rearrange("a p n -> (a p) n")
                pool.dma_start(ada_ring[:, a % ADA_RING, :], src).then_inc(ada_full[a % ADA_RING], 16)

            def load_adas(first, count):
                with pool.Fori(0, count // ADA_RING) as turn:
                    for a in range(first, first + ADA_RING):
                        load_ada(a, turn)

            roots = [0]

            def root(lo, hi):
                roots[0] += 1
                pool.wait_ge(root_in, roots[0])
                pool.tensor_tensor(rstd[:, lo:hi], rstd[:, lo:hi], minus_half[:, lo:hi], ALU.pow).then_inc(root_out, 1)

            def attention_roots():
                root(0, 4)
                for b in range(NB):
                    root(4, 8)

            for a in range(ADA_RING):
                pool.dma_start(ada_ring[:, a, :], ada[a]).then_inc(ada_full[a], 16)
            for i, dst in enumerate(ada_places):
                pool.dma_start(dst, ada[ADA_RING + i]).then_inc(ada_ahead[i], 16)
            pool.memset(minus_half[:, :], -0.5).then_inc(half_ready, 1)
            pool.wait_ge(half_ready, 1)
            load_adas(ADA_EARLY, ADA_RING)
            root(0, 2)
            us = units_of(0)
            for n, u in enumerate(us):
                if n == 0:
                    root(0, 4)
                    for a in range(ADA_EARLY, ADA_EARLY + ADA_IN_B):
                        load_ada(a + ADA_RING)
                a = ADA_EARLY + ADA_IN_B + n
                if a < ADA_MID:
                    load_ada(a + ADA_RING)
                if n >= 1 and us[n - 1].comb is not None:
                    root(4, 8)
            root(0, 2)
            load_adas(ADA_RING + ADA_MID, ADA_CHUNKS - ADA_RING - ADA_MID)
            root(0, 2)
            attention_roots()
            pool.wait_ge(mod_ready, 12)
            pool.dma_start(Z[:, TRI_AT:TRI_AT + 2 * P], d["tri_iota"]).then_inc(late_in, 16)
            pool.dma_start(Z[:, RW_AT:RW_AT + 64], d["router"]).then_inc(late_in, 16)
            pool.dma_start(Z[:, LNM_AT:LNM_AT + 512], d["lnm"]).then_inc(late_in, 16)
            pool.dma_start(Z[:, NA_AT:NA_AT + 4096], d["na"]).then_inc(late_in, 16)
            pool.dma_start(Z[:, DIL_AT:DIL_AT + 4096], d["dil"]).then_inc(late_in, 16)
            root(0, 2)
            pool.dma_start(final_g, d["rows"][4:5, :].broadcast_to([P, D])).then_inc(rows_in, 16)
            pool.dma_start(f1_post_g, d["rows"][5:6, :].broadcast_to([P, D])).then_inc(rows_in, 16)
            pool.wait_ge(x_ready, 8)
            pool.dma_start(gate_mix[:, :], d["rows"][6:7, :].broadcast_to([P, D])).then_inc(rows_in2, 16)
            pool.dma_start(gate_ffn[:, :], d["rows"][7:8, :].broadcast_to([P, D])).then_inc(rows_in2, 16)
            for lo, hi in ((4, 6), (0, 2), (4, 6), (0, 2), (0, 4), (4, 6), (0, 2), (4, 6)):
                root(lo, hi)

        @block.tensor
        def _(pe):
            def mark(s):
                nc.tensor.matmul(ps[0:1, 7, 0:2], zero[:, 0:1], finite[:, 0:2], start=True, stop=True,
                                 skip_group_check=True).then_inc(s, 1)

            def transpose_x(t):
                for j in range(4):
                    for kt in (2 * j, 2 * j + 1):
                        for b in range(NB):
                            m = nc.tensor.transpose(ps[:, j, (kt % 2) * T + b * P:(kt % 2) * T + (b + 1) * P],
                                                    XN[:, b, kt * P:(kt + 1) * P], ident[:, :])
                    m.then_inc(xt_ps, 1)

            def product(out, xh, xl, at, n, last):
                slot, c = at
                wh, wl = WH[:, slot, c:c + 512], WL[:, slot, c:c + 512]
                nc.tensor.matmul(out, xh, wh, start=n, stop=False, skip_group_check=True)
                nc.tensor.matmul(out, xh, wl, start=False, stop=False, skip_group_check=True)
                return nc.tensor.matmul(out, xl, wh, start=False, stop=last, skip_group_check=True)

            def up_piece(chunk, half, turn, banks, pair):
                pe.wait_ge(lo_ready, turn * (2 * RING) + (piece_no(chunk, half) + 1))
                for b in range(NB):
                    for i in range(2):
                        kt = 2 * pair + i
                        xs = slice(b * P, (b + 1) * P)
                        m = product(ps[:, banks[b], :], XTH[:, kt, xs], XTL[:, kt, xs],
                                    (piece_no(chunk, half) % SPLITS, i * 512), kt == 0, kt == KT - 1)
                m.then_inc(piece_done, 1)

            def gemm(g):
                for q in range(GEMM_GROUPS[g]):
                    if q >= 2:
                        pe.wait_ge(gemm_out, 2 * sum(GEMM_GROUPS[:g]) + 2 * (q - 1))
                    banks = [4 + 2 * (q % 2) + b for b in range(NB)]
                    for pair in range(4):
                        up_piece(GEMM_CHUNK[g] + 2 * q + pair // 2, pair % 2, 0, banks, pair)

            def clear_y(banks):
                for j in banks:
                    nc.tensor.matmul(ps[:, j, :], zero[:, :], finite, start=True, stop=False,
                                     skip_group_check=True)

            def ffn(i):
                n0 = FFN_CHUNK[i]
                h0 = FF_STEPS * i
                clear_y(range(4))

                def turn_both():
                    for b in range(NB):
                        for f in range(2):
                            m = nc.tensor.transpose(ps[:, 6 + b, f * P:(f + 1) * P], hbuf[:, b, f * P:(f + 1) * P], ident[:, :])
                    m.then_inc(hT_ps, 1)

                def down_piece(chunk, f, turn, last):
                    pe.wait_ge(lo_ready, turn * (2 * RING) + (piece_no(chunk, f) + 1))
                    for b in range(NB):
                        for half in range(2):
                            m = product(ps[:, 2 * b + half, :], hTH[:, b, f, :], hTL[:, b, f, :],
                                        (piece_no(chunk, f) % SPLITS, half * 512), False, last and f == 1)
                    m.then_inc(piece_done, 1)

                for pair in range(4):
                    up_piece(n0 + pair // 2, pair % 2, 0, (4, 5), pair)

                def step(n, turn, s):
                    k = turn * 2 + (h0 + 1 + s)
                    for pair in range(4):
                        if pair == 0:
                            pe.wait_ge(h_ready, k)
                        up_piece(n + pair // 2, pair % 2, turn, (4, 5), pair)
                        if pair == 0:
                            turn_both()
                    pe.wait_ge(hT_ready, k)
                    for f in range(2):
                        down_piece(n + 2, f, turn, False)

                stream_turns(pe, FF_STEPS - 1, 3, n0 + 2, step)
                pe.wait_ge(h_ready, h0 + FF_STEPS)
                turn_both()
                pe.wait_ge(hT_ready, h0 + FF_STEPS)
                for f in range(2):
                    down_piece(n0 + FF_CHUNKS - 1, f, 0, True)

            def mod_columns(first, count, fills_before, ada_needed):
                pe.wait_ge(ada_used, ada_needed)
                if fills_before:
                    pe.wait_ge(mod_ready, fills_before)
                for i, m6 in enumerate(range(first, first + count)):
                    for j in range(KT):
                        c = i * KT + j
                        m = nc.tensor.matmul(ps[:, 6, c:c + 1], ada_acc[:, m6, j * P:(j + 1) * P], ones[:, 0:1],
                                             start=True, stop=True)
                m.then_inc(mod_ps, 1)

            def mod_rows(m6, fills_before):
                for half in range(2):
                    pe.wait_ge(mod_ready, fills_before + half)
                    nc.tensor.matmul(ps[:, 6, :], ones[:, :], ada_acc[:, m6, half * 512:(half + 1) * 512],
                                     start=True, stop=True).then_inc(mod_ps, 1)

            def fills(g, first, end):
                qk = QK[:, g.gi % 2, :]
                f = g.fill0

                def wanted(i):
                    return first <= i < end

                def begin(f):
                    if f >= 1:
                        pe.wait_ge(filled, f)

                def tiles(srcs):
                    for i, src in enumerate(srcs):
                        for b in range(NB):
                            a = src(b)
                            m = nc.tensor.transpose(ps[0:a.shape[-1], 7, i * T + b * P:i * T + (b + 1) * P], a, ident[:, :])
                    return m

                def pair(col):
                    return [lambda b, c=c: PROJ[:, b, c:c + P] for c in (col, col + P)]

                if g.kind in "AD" or g.kind in "NL":
                    base = {"A": (A_Q, A_K), "D": (D_Q, D_K)}.get(g.kind)
                    if base is None:
                        h0 = (8 if g.kind == "L" else 0) + 4 * g.half
                        base = (h0 * HD, D + h0 * HD)
                    for c in base:
                        begin(f)
                        tiles(pair(c)).then_inc(fill_ps, 1)
                        f += 1
                if g.kind == "C":
                    for c in (C_Q, C_K, C_QI):
                        begin(f)
                        tiles(pair(c)).then_inc(fill_ps, 1)
                        f += 1
                    begin(f)
                    pe.wait_ge(c_ready, g.layer + 1)
                    tiles([lambda b: PROJ[:, b, C_KIREP:C_KIREP + P]]).then_inc(fill_ps, 1)
                if g.kind == "B":
                    if wanted(0):
                        begin(f)
                        pe.wait_ge(latent_in, 32 * (g.layer + 1))
                        pe.wait_ge(b_normed, g.layer + 1)
                        tiles(pair(B_QD)).then_inc(fill_ps, 1)
                    if wanted(1):
                        begin(f + 1)
                        tiles([lambda b: PROJ[:, b, B_KVD:B_KVD + P]]).then_inc(fill_ps, 1)
                    for b in range(NB):
                        if wanted(2 + b):
                            begin(f + 2 + b)
                            for kt in range(2):
                                m = nc.tensor.matmul(ps[:, 7, 0:384], qk[:, kt * T + b * P:kt * T + (b + 1) * P], UQ[:, kt, :],
                                                     start=kt == 0, stop=kt == 1)
                            m.then_inc(fill_ps, 1)
                    for b in range(NB):
                        if wanted(4 + b):
                            begin(f + 4 + b)
                            nc.tensor.matmul(ps[:, 7, :], qk[:, 512 + b * P:512 + (b + 1) * P], UKV,
                                             start=True, stop=True).then_inc(fill_ps, 1)
                    for j in range(2):
                        if wanted(6 + j):
                            begin(f + 6 + j)
                            if j == 0:
                                pe.wait_ge(b_roped, g.layer + 1)
                            tiles([lambda b, h=h: PROJ[:, b, B_UQ + 96 * h:B_UQ + 96 * (h + 1)]
                                   for h in (2 * j, 2 * j + 1)]).then_inc(fill_ps, 1)
                    for j in range(2):
                        if wanted(8 + j):
                            begin(f + 8 + j)
                            tiles([lambda b, h=h: KB[:, b, h, :] for h in (2 * j, 2 * j + 1)]).then_inc(fill_ps, 1)

            def score(u):
                qk = QK[:, u.g.gi % 2, :]
                pe.wait_ge(filled, u.g.fill0 + u.g.n_fills)
                if u.su >= 2:
                    pe.wait_ge(probs, u.su - 1)
                j0 = 2 * (u.su % 2)
                for h in range(4):
                    s = head_slot(h)
                    out = ps[:, j0 + s // 2, (s % 2) * T:(s % 2) * T + u.nk]
                    q0 = u.b * P
                    if u.kind == "I":
                        lhs, rhs = qk[:, (4 + u.part) * T + q0:(4 + u.part) * T + q0 + P], KI4[:, h, 0:u.nk]
                    elif u.kind == "B":
                        lhs, rhs = qk[0:96, h * T + q0:h * T + q0 + P], qk[0:96, D + h * T:D + h * T + u.nk]
                    else:
                        p0, rows = (h % 2) * HD, HD
                        if u.kind == "A":
                            p0, rows = p0 + 32 * u.part, 32
                        tq, tk = h // 2, 2 + h // 2
                        lhs = qk[p0:p0 + rows, tq * T + q0:tq * T + q0 + P]
                        rhs = qk[p0:p0 + rows, tk * T:tk * T + u.nk]
                    m = nc.tensor.matmul(out, lhs, rhs, start=True, stop=True)
                m.then_inc(scores, 1)

            def values(u):
                src = PR[:, (u.su - 1) % 2 if u.kind == "A" else u.su % 2]
                if u.kind == "A":
                    pe.wait_ge(combined, u.comb + 1)
                else:
                    pe.wait_ge(probs, u.su + 1)
                for h in range(4):
                    for kb in range(u.nk // P):
                        m = nc.tensor.transpose(ps[:, 4 + h // 2, (h % 2) * T + kb * P:(h % 2) * T + (kb + 1) * P],
                                                src[:, head_slot(h), kb * P:(kb + 1) * P], ident[:, :])
                m.then_inc(pT_ps, 1)
                pe.wait_ge(pT_ready, u.pu + 1)
                if u.pu >= 1:
                    pe.wait_ge(mixed, u.pu)
                for h in range(4):
                    for kb in range(u.nk // P):
                        if u.kind == "B":
                            c = B_UKV + h * P + HD
                        else:
                            c = {"A": A_V, "C": C_V, "D": D_V, "N": 2 * D, "L": 2 * D + 512}[u.kind] + (4 * u.g.half + h) * HD
                        m = nc.tensor.matmul(ps[:, 6, h * HD:(h + 1) * HD], PT[:, h, kb, :], PROJ[:, kb, c:c + HD],
                                             start=kb == 0, stop=kb == u.nk // P - 1)
                m.then_inc(o_ps, 1)

            def attention(layer):
                us = units_of(layer)
                pe.wait_ge(gemm_out, 2 * sum(GEMM_GROUPS[:2 * layer + 1]))
                fills(us[0].g, 0, us[0].g.n_fills)
                score(us[0])
                for n, u in enumerate(us):
                    part = fill_part(u)
                    if part and last_of_group(u):
                        fills(*part)
                    if n + 1 < len(us):
                        score(us[n + 1])
                    if part and not last_of_group(u):
                        fills(*part)
                    if u.pu is not None:
                        values(u)

            def route():
                pe.wait_ge(late_in, 16 * 5)
                for b in range(NB):
                    for kt in range(KT):
                        m = nc.tensor.matmul(ps[:, 7, b * 8:(b + 1) * 8], XT[:, kt, b * P:(b + 1) * P], router[:, kt, :],
                                             start=kt == 0, stop=kt == KT - 1)
                m.then_inc(route_ps, 1)
                pe.wait_ge(route_sel, 1)
                nc.tensor.matmul(ps[:, 7, 0:8], tri, r_sel[:, 0, :], start=True, stop=True)
                nc.tensor.matmul(ps[:, 7, 8:16], tri, r_sel[:, 1, :], start=True, stop=False)
                nc.tensor.matmul(ps[:, 7, 8:16], ones[:, :], r_sel[:, 0, :], start=False, stop=True)
                nc.tensor.matmul(ps[:, 7, 16:24], ones[:, :], r_sel[:, 0, :], start=True, stop=False)
                nc.tensor.matmul(ps[:, 7, 16:24], ones[:, :], r_sel[:, 1, :], start=False, stop=True).then_inc(rank_ps, 1)

            def experts(m):
                def piece(local, half, turn, e_pieces):
                    pe.wait_ge(m["lo_ready"], turn * (2 * RING) + e_pieces + (m["first"] + 2 * local + half + 1))
                    return expert_piece(local, half)[1]

                def ups(local, par, turn, e_pieces, pairs):
                    for pair in pairs:
                        slot = piece(local + pair // 2, pair % 2, turn, e_pieces)
                        for i in range(2):
                            kt = 2 * pair + i
                            mm = product(ps[:, 4 + par, :], XGH[:, kt, :], XGL[:, kt, :], (slot, i * 512),
                                         kt == 0, kt == KT - 1)
                        mm.then_inc(m["piece_done"], 1)

                def turn_h(par):
                    for f in range(2):
                        mm = nc.tensor.transpose(ps[:, 6 + par, f * P:(f + 1) * P], hbuf[:, par, f * P:(f + 1) * P], ident[:, :])
                    mm.then_inc(m["hT_ps"], 1)

                def downs(local, par, turn, e_pieces, last):
                    for f in range(2):
                        slot = piece(local, f, turn, e_pieces)
                        for half in range(2):
                            mm = product(ps[:, half, :], hTH[:, par, f, :], hTL[:, par, f, :], (slot, half * 512),
                                         False, last and f == 1)
                        mm.then_inc(m["piece_done"], 1)

                def gather(number):
                    pe.wait_ge(m["psel"], number)
                    for j in range(KT):
                        for b in range(NB):
                            mm = nc.tensor.matmul(ps[:, 2 + j // 4, (j % 4) * P:(j % 4 + 1) * P],
                                                  XN[:, b, j * P:(j + 1) * P], PSEL[:, b, :], start=b == 0, stop=b == 1)
                    mm.then_inc(m["xg_ps"], 1)

                def scatter(number):
                    pe.wait_ge(m["ye_ready"], number)
                    for b in range(NB):
                        for half in range(2):
                            mm = nc.tensor.matmul(ps[:, 2 - 2 * b + half, :], CT[:, b, :], YE[:, half * 512:(half + 1) * 512],
                                                  start=True, stop=True)
                        mm.then_inc(m["sc_ps"], 1)

                clear_y(range(2))
                if m["sweep"] == 1:
                    for _ in range(SPLITS):
                        mark(m["piece_done"])
                gather(1)
                with pe.Fori(0, EXPERTS) as e:
                    turn_e = e * (EX_CHUNKS // RING)
                    e_pieces = e * (2 * EX_CHUNKS)
                    k_e = e * EX_STEPS
                    pe.wait_ge(m["xg_ready"], e + 1)
                    ups(0, 0, 0, e_pieces, range(4))
                    scatter(e + 1)
                    ups(2, 1, 0, e_pieces, range(1))
                    pe.wait_ge(m["h_ready"], k_e + 1)
                    turn_h(0)
                    ups(2, 1, 0, e_pieces, range(1, 4))
                    pe.wait_ge(m["sc_added"], e * 2 + 2)
                    clear_y(range(2))
                    pe.wait_ge(m["hT_ready"], k_e + 1)
                    downs(4, 0, 0, e_pieces, False)
                    with pe.Fori(0, (EX_STEPS - 2) // 2) as t:
                        for par in range(2):
                            local = 5 + 3 * par
                            k = t * 2 + k_e + (2 + par)
                            ups(local, par, t, e_pieces, range(1))
                            pe.wait_ge(m["h_ready"], k)
                            turn_h(1 - par)
                            ups(local, par, t, e_pieces, range(1, 4))
                            pe.wait_ge(m["hT_ready"], k)
                            downs(local + 2, 1 - par, t, e_pieces, False)
                    pe.wait_ge(m["h_ready"], k_e + EX_STEPS)
                    turn_h(1)
                    pe.wait_ge(m["wsel"], e + 1)
                    for b in range(NB):
                        mm = nc.tensor.transpose(ps[:, 6, b * P:(b + 1) * P], WSEL[:, b, :], ident[:, :])
                    mm.then_inc(m["ct_ps"], 1)
                    gather(e + 2)
                    pe.wait_ge(m["hT_ready"], k_e + EX_STEPS)
                    downs(EX_CHUNKS - 1, 1, 0, e_pieces, True)
                scatter(EXPERTS + 1)
                pe.wait_ge(m["sc_added"], 2 * EXPERTS + 2)

            pe.wait_ge(zero_ready, 1)
            pe.wait_ge(cols_in, 32)
            for layer in range(LAYERS):
                chunks = (24, ADA_CHUNKS)[layer]
                mod_columns(0, 2, 6 * layer, (ADA_EARLY, ADA_CHUNKS)[layer])
                pe.wait_ge(xn_ready, 2 * NORM_NO[3 * layer])
                transpose_x(3 * layer)
                pe.wait_ge(xt_ready, 4 * (3 * layer + 1))
                gemm(2 * layer)
                pe.wait_ge(gemm_out, 2 * sum(GEMM_GROUPS[:2 * layer + 1]))
                attention(layer)
                pe.wait_ge(mixed, pu_end(layer))
                transpose_x(3 * layer + 1)
                pe.wait_ge(ada_used, chunks)
                mod_rows(2, 6 * layer + 1)
                mod_columns(3, 2, 6 * layer + 3, chunks)
                mod_rows(5, 6 * layer + 4)
                pe.wait_ge(mod_ready, 6 * (layer + 1))
                pe.wait_ge(xt_ready, 4 * (3 * layer + 2))
                gemm(2 * layer + 1)
                pe.wait_ge(xn_ready, 2 * NORM_NO[3 * layer + 2])
                transpose_x(3 * layer + 2)
                pe.wait_ge(xt_ready, 4 * (3 * layer + 3))
                if layer == 0:
                    ffn(0)
                else:
                    route()
                    experts(moe_sems[0])
                    pe.wait_ge(route_ready, 1)
                    over = pe.value_load(flag[0:1, 0:1], min_val=0, max_val=1)
                    with pe.If(over > 0):
                        experts(moe_sems[1])
            pe.wait_ge(xn_ready, 10)
            transpose_x(6)
            pe.wait_ge(xt_ready, 28)
            ffn(1)
            pe.wait_ge(xn_ready, 12)
            transpose_x(7)
            pe.wait_ge(xt_ready, 32)
            gemm(4)
            attention(2)
            pe.wait_ge(xn_ready, 14)
            transpose_x(8)
            pe.wait_ge(xt_ready, 36)
            gemm(5)
            pe.wait_ge(xn_ready, 16)
            transpose_x(9)
            pe.wait_ge(xt_ready, 40)
            ffn(2)

        @block.scalar
        def _(act):
            def loads(pairs, s):
                for dst, src in pairs:
                    act.dma_start(dst, src).then_inc(s, 16)

            loads([(cols[:, :], d["cols"])], cols_in)
            loads([(unit[:, :], d["unit"])], cols_in)
            act.wait_ge(cols_in, 32)
            act.activation(csilu[:, :], cols[:, COL["c"]:COL["c"] + KT], ACT.Silu).then_inc(csilu_ready, 1)
            act.wait_ge(ada_ahead[3], 16)
            loads([(lam_in, d["lam"].broadcast_to([P, 256]).rearrange("p (l n) -> p l n", l=LAYERS)),
                   (gate_mix[:, :], d["rows"][0:1, :].broadcast_to([P, D])),
                   (gate_ffn[:, :], d["rows"][1:2, :].broadcast_to([P, D])),
                   (gdiff[:, :, :].rearrange("p l n -> p (l n)"), d["gdiff"].broadcast_to([P, LAYERS * HD])),
                   (cossin[:, :, :, :].rearrange("p b c n -> p (b c n)"), d["cossin"]),
                   (alibi[:, :], d["alibi"]), (cmask[:, :], d["cmask"]), (band[:, :], d["band"][0])], const_in)

            def squares(t):
                if t == 0:
                    act.wait_ge(x_in, 16)
                elif t == 8:
                    act.wait_ge(mixed, pu_end(LAYERS))
                if t == 8:
                    for b in range(NB):
                        for half in range(2):
                            cs = slice(half * 512, (half + 1) * 512)
                            act.activation(YB[:, b, cs], XN[:, b, cs], ACT.Square,
                                           accum_out=ss[:, 2 * b + half:2 * b + half + 1]).then_inc(sq_ready, 1)
                else:
                    for b in range(NB):
                        if t > 0:
                            act.wait_ge(x_ready, 2 * X_READY[t] - 1 + b)
                        act.activation(XN[:, b, :], X[:, b, :], ACT.Square,
                                       accum_out=ss[:, b:b + 1]).then_inc(sq_ready, 1)

            def split_hi(chunk, half, turn=0):
                if half == 0:
                    act.wait_ge(full[chunk % RING], turn * 16 + 16 * (chunk // RING + 1))
                p = piece_no(chunk, half)
                if p >= SPLITS:
                    act.wait_ge(piece_done, turn * (2 * RING) + (p - SPLITS + 1))
                act.activation(WH[:, p % SPLITS, :], ring[:, chunk % RING, half * PIECE:(half + 1) * PIECE],
                               ACT.Copy).then_inc(hi_ready, 1)

            def ahead_hi(first):
                for half in range(SPLITS):
                    split_hi(first + half // 2, half % 2)

            def xt_split_hi(t):
                for j in range(4):
                    act.wait_ge(xt_full, 4 * SPLIT_NO[t] + j + 1)
                    act.activation(XTH[:, 2 * j:2 * j + 2, :], XT[:, 2 * j:2 * j + 2, :], ACT.Copy).then_inc(xt_hi, 1)

            def gemm_copy(g):
                dst = PROJ if g % 2 == 0 else YB

                def copy_out(q):
                    act.wait_ge(piece_done, piece_no(GEMM_CHUNK[g] + 2 * q + 1, 2))
                    for b in range(NB):
                        act.activation(dst[:, b, q * 512:(q + 1) * 512], ps[:, 4 + 2 * (q % 2) + b, :],
                                       ACT.Copy).then_inc(gemm_out, 1)

                for q in range(GEMM_GROUPS[g]):
                    for i in range(4):
                        if q > 0 or i >= SPLITS:
                            split_hi(GEMM_CHUNK[g] + 2 * q + i // 2, i % 2)
                        if q > 0 and i == 3:
                            copy_out(q - 1)
                copy_out(GEMM_GROUPS[g] - 1)

            def ffn(i):
                h0 = FF_STEPS * i
                n0 = FFN_CHUNK[i]

                def silu_both(n, turn):
                    act.wait_ge(piece_done, turn * (2 * RING) + piece_no(n + 1, 2))
                    act.activation(sgt[:, :, :], ps[:, 4:6, 0:FW], ACT.Silu).then_inc(silu_ready, 1)

                def hT_high(k):
                    act.wait_ge(hT_ps, k)
                    act.activation(hTH[:, :, :, :].rearrange("p b f n -> p b (f n)"), ps[:, 6:8, 0:2 * P],
                                   ACT.Copy).then_inc(hT_hi, 1)

                def step(n, turn, k):
                    split_hi(n, 0, turn)
                    silu_both(n - 2 if isinstance(k, int) and k == h0 + 1 else n - 3, turn)
                    split_hi(n, 1, turn)
                    for half in range(2):
                        split_hi(n + 1, half, turn)
                    hT_high(k)
                    for half in range(2):
                        split_hi(n + 2, half, turn)

                for s in range(2):
                    step(n0 + 2 + 3 * s, 0, h0 + 1 + s)
                stream_turns(act, FF_STEPS - 3, 3, n0 + 8, lambda n, turn, s: step(n, turn, turn * 2 + (h0 + 3 + s)))
                silu_both(n0 + FF_CHUNKS - 4, 0)
                for half in range(2):
                    split_hi(n0 + FF_CHUNKS - 1, half)
                hT_high(h0 + FF_STEPS)
                act.wait_ge(piece_done, piece_no(n0 + FF_CHUNKS - 1, 2))
                for b in range(NB):
                    act.activation(YB[:, b, :], ps[:, 2 * b:2 * b + 2, :].rearrange("p j n -> p (j n)"), ACT.Copy).then_inc(y_out, 1)

            def result_squares(src, number, s, count):
                for b in range(NB):
                    act.wait_ge(s, count - 1 + b)
                    act.activation(XN[:, b, :], src[:, b, :], ACT.Square,
                                   accum_out=ss[:, 4 + b:5 + b]).then_inc(res_sq, 1)

            def copy_fills(g, first, end):
                qk = QK[:, g.gi % 2, :]
                f = g.fill0

                def fill(f, dst, src, scale=1.0, last=True):
                    if not first <= f - g.fill0 < end:
                        return
                    act.wait_ge(fill_ps, f + 1)
                    ins = act.activation(dst, src, ACT.Copy, scale=scale)
                    if last:
                        ins.then_inc(filled, 1)

                if g.kind in "ADNL":
                    for i in range(2):
                        fill(f + i, qk[:, i * 512:(i + 1) * 512], ps[:, 7, :])
                if g.kind == "C":
                    for i in range(3):
                        fill(f + i, qk[:, i * 512:(i + 1) * 512], ps[:, 7, :])
                    for h in range(4):
                        fill(f + 3, KI4[32 * h:32 * (h + 1), h, :], ps[32 * h:32 * (h + 1), 7, 0:T], last=h == 3)
                if g.kind == "B":
                    for i, (c, w) in enumerate(((B_QD, 256), (B_KVD, 128)) if first == 0 else ()):
                        for b in range(NB):
                            if 2 * i + b > 0:
                                act.wait_ge(b_sq, 4 * g.layer + 2 * i + b)
                            act.activation(junk[:, 0:w], PROJ[:, b, c:c + w], ACT.Square,
                                           accum_out=ss[:, 2 * i + b:2 * i + b + 1]).then_inc(b_sq, 1)
                    for kt in range(2):
                        at = COL["q_g"] + 2 * g.layer + kt
                        fill(f, qk[:, kt * T:(kt + 1) * T], ps[:, 7, kt * T:(kt + 1) * T], cols[:, at:at + 1], kt == 1)
                    at = COL["kv_g"] + g.layer
                    fill(f + 1, qk[:, 512:768], ps[:, 7, 0:T], cols[:, at:at + 1])
                    for b in range(NB):
                        fill(f + 2 + b, PROJ[:, b, B_UQ:B_UQ + 384], ps[:, 7, 0:384])
                    for b in range(NB):
                        fill(f + 4 + b, PROJ[:, b, B_UKV:B_UKV + 512], ps[:, 7, :])
                    for i in range(4):
                        fill(f + 6 + i, qk[0:96, i * 512:(i + 1) * 512], ps[0:96, 7, :])

            def probabilities(u):
                par = u.su % 2
                if u.su >= 2:
                    name, number = release(UNITS[u.su - 2])
                    act.wait_ge({"idx": idx_added, "comb": combined, "pT": pT_ps}[name], number)
                src = ps[:, 2 * par:2 * par + 2, :].rearrange("p j (s k) -> p (j s) k", s=2)
                if u.kind == "I":
                    act.wait_ge(scores, u.su + 1)
                    act.activation(PR[:, par, :, 0:u.nk], src[:, :, 0:u.nk], ACT.Relu).then_inc(probs, 1)
                    return
                act.wait_ge(biased, u.bi + 1)
                for h in range(4):
                    s = head_slot(h)
                    ins = act.activation(PR[:, par, s, 0:u.nk], src[:, s, 0:u.nk], ACT.Exp, bias=nmax[:, par, s:s + 1],
                                         accum_out=den[:, par, h:h + 1])
                ins.then_inc(probs, 1)

            def copy_pT(u):
                act.wait_ge(pT_ps, u.pu + 1)
                src = ps[:, 4:6, :].rearrange("p j (h k) -> p (j h) k", h=2)
                act.activation(PT.rearrange("p h b q -> p h (b q)")[:, :, 0:u.nk], src[:, :, 0:u.nk],
                               ACT.Copy).then_inc(pT_ready, 1)

            def attention(layer):
                us = units_of(layer)
                copy_fills(us[0].g, 0, us[0].g.n_fills)
                probabilities(us[0])
                for n, u in enumerate(us):
                    if fill_part(u):
                        copy_fills(*fill_part(u))
                    if n + 1 < len(us):
                        probabilities(us[n + 1])
                    if u.pu is not None:
                        copy_pT(u)

            def route():
                act.wait_ge(route_max, 1)
                for b in range(NB):
                    act.activation(r_exp[:, b, :], r_logit[:, b, 0:8], ACT.Exp, bias=r_nv1[:, b:b + 1])
                    ins = act.activation(r_e2[:, b:b + 1], r_top[:, b, 1:2], ACT.Exp, bias=r_nv1[:, b:b + 1])
                ins.then_inc(route_exp, 1)

            def experts(m):
                def hi(local, half, turn, e_pieces, e_turns):
                    raw, slot = expert_piece(local, half)
                    if half == 0:
                        chunk_loaded(act, m, local, turn + e_turns)
                    act.wait_ge(m["piece_done"], turn * (2 * RING) + e_pieces + (m["freed"] + 2 * local + half - SPLITS + 1))
                    act.activation(WH[:, slot, :], raw, ACT.Copy).then_inc(m["hi_ready"], 1)

                def silu(last, par, turn, e_pieces):
                    act.wait_ge(m["piece_done"], turn * (2 * RING) + e_pieces + (m["freed"] + 2 * last + 2))
                    act.activation(sgt[:, par, :], ps[:, 4 + par, 0:FW], ACT.Silu).then_inc(m["silu_ready"], 1)

                def hT_high(par, k):
                    act.wait_ge(m["hT_ps"], k)
                    act.activation(hTH[:, par].rearrange("p f n -> p (f n)"), ps[:, 6 + par, 0:2 * P],
                                   ACT.Copy).then_inc(m["hT_hi"], 1)

                def gathered(number):
                    act.wait_ge(m["xg_ps"], number)
                    for j in range(KT):
                        ins = act.activation(XG[:, j, :], ps[:, 2 + j // 4, (j % 4) * P:(j % 4 + 1) * P], ACT.Identity,
                                             scale=xscale[:, j:j + 1], bias=modc[:, 16 + j:17 + j])
                    ins.then_inc(m["xg_full"], 1)
                    act.wait_ge(m["xg_full"], number)
                    act.activation(XGH, XG, ACT.Copy).then_inc(m["xg_hi"], 1)

                def copy_ye():
                    act.activation(YE, ps[:, 0:2, :].rearrange("p j n -> p (j n)"), ACT.Copy).then_inc(m["ye_ready"], 1)

                gathered(1)
                with act.Fori(0, EXPERTS) as e:
                    e_turns = e * (EX_CHUNKS // RING)
                    e_pieces = e * (2 * EX_CHUNKS)
                    k_e = e * EX_STEPS
                    for pair in range(4):
                        if pair == 3:
                            act.wait_ge(m["piece_done"], e_pieces + m["freed"])
                            copy_ye()
                        hi(pair // 2, pair % 2, 0, e_pieces, e_turns)
                    for pair in range(4):
                        hi(2 + pair // 2, pair % 2, 0, e_pieces, e_turns)
                        if pair == 0:
                            silu(1, 0, 0, e_pieces)
                    hT_high(0, k_e + 1)
                    for half in range(2):
                        hi(4, half, 0, e_pieces, e_turns)
                    with act.Fori(0, (EX_STEPS - 2) // 2) as t:
                        for par in range(2):
                            local = 5 + 3 * par
                            for pair in range(4):
                                hi(local + pair // 2, pair % 2, t, e_pieces, e_turns)
                                if pair == 0:
                                    silu(local - 2, 1 - par, t, e_pieces)
                            hT_high(1 - par, t * 2 + k_e + (2 + par))
                            for half in range(2):
                                hi(local + 2, half, t, e_pieces, e_turns)
                    for half in range(2):
                        hi(EX_CHUNKS - 1, half, 0, e_pieces, e_turns)
                        if half == 0:
                            silu(EX_CHUNKS - 3, 1, 0, e_pieces)
                    hT_high(1, k_e + EX_STEPS)
                    act.wait_ge(m["ct_ps"], e + 1)
                    act.activation(CT.rearrange("p b s -> p (b s)"), ps[:, 6, 0:T], ACT.Copy)
                    gathered(e + 2)
                act.wait_ge(m["piece_done"], m["freed"] + 2 * EX_TOTAL)
                copy_ye()

            for layer in range(LAYERS):
                if layer == 1:
                    ahead_hi(GEMM_CHUNK[2])
                squares(3 * layer)
                if layer == 1:
                    loads([(gate_ffn[:, :], d["rows"][3:4, :].broadcast_to([P, D]))], gates_in)
                else:
                    act.wait_ge(ada_used, ADA_EARLY)
                    ahead_hi(GEMM_CHUNK[0])
                xt_split_hi(3 * layer)
                gemm_copy(2 * layer)
                act.wait_ge(gemm_out, 2 * sum(GEMM_GROUPS[:2 * layer + 1]))
                if layer == 0:
                    act.wait_ge(lam_exp_in, 1)
                    act.activation(lamc[:, 0:4], lamc[:, 4:8], ACT.Exp).then_inc(lam_exp_out, 1)
                loads([(UKV, d["ukv"][layer]), (UQ.rearrange("p k n -> p (k n)"), d["uq"][layer])], latent_in)
                attention(layer)
                act.wait_ge(mixed, pu_end(layer))
                if layer + 1 < LAYERS:
                    loads([(band[:, :], d["band"][layer + 1])], layer_in)
                ahead_hi(GEMM_CHUNK[2 * layer + 1])
                xt_split_hi(3 * layer + 1)
                gemm_copy(2 * layer + 1)
                if layer == 0:
                    ahead_hi(FFN_CHUNK[0])
                squares(3 * layer + 2)
                if layer == 0:
                    loads([(gate_mix[:, :], d["rows"][2:3, :].broadcast_to([P, D]))], gates_in)
                    xt_split_hi(2)
                    ffn(0)
                else:
                    route()
                    experts(moe_sems[0])
                    act.wait_ge(route_ready, 1)
                    over = act.value_load(flag[0:1, 0:1], min_val=0, max_val=1)
                    with act.If(over > 0):
                        experts(moe_sems[1])
            result_squares(X, 0, x_ready, 8)
            ahead_hi(FFN_CHUNK[1])
            squares(6)
            xt_split_hi(6)
            ffn(1)
            result_squares(YB, 1, y_out, 4)
            ahead_hi(GEMM_CHUNK[4])
            squares(7)
            xt_split_hi(7)
            gemm_copy(4)
            attention(2)
            squares(8)
            ahead_hi(GEMM_CHUNK[5])
            xt_split_hi(8)
            gemm_copy(5)
            result_squares(YB, 2, gemm_out, 2 * sum(GEMM_GROUPS))
            ahead_hi(FFN_CHUNK[2])
            squares(9)
            xt_split_hi(9)
            ffn(2)
            result_squares(YB, 3, y_out, 6)

        @block.vector
        def _(dve):
            linked = [0]

            def link(ins):
                linked[0] += 1
                ins.then_inc(dve_chain, 1)
                dve.wait_ge(dve_chain, linked[0])

            def ada_step(a, turn=0, m6=None):
                q = a % 4
                acc = ada_acc[:, (a % 24) // 4, :] if m6 is None else ada_acc[:, bass.ds(m6, 1), :].rearrange("p a n -> p (a n)")
                if m6 is None and ADA_RING <= a < ADA_EARLY:
                    dve.wait_ge(ada_ahead[a - ADA_RING], 16)
                    w = ada_places[a - ADA_RING]
                else:
                    loads = (a if a < ADA_RING else a - len(ADA_AHEAD)) // ADA_RING + 1
                    dve.wait_ge(ada_full[a % ADA_RING], turn * (16 * 4 // ADA_RING) + 16 * loads)
                    w = ada_ring[:, a % ADA_RING, :]
                if q == 0:
                    nc.vector.tensor_scalar(acc, w[:, 0:D], csilu[:, 0:1], None, ALU.mult).then_inc(ada_half, 1)
                else:
                    dve.wait_ge(ada_used, turn * 4 + a)
                    nc.vector.scalar_tensor_tensor(acc, w[:, 0:D], csilu[:, 2 * q:2 * q + 1], acc, ALU.mult,
                                                   ALU.add).then_inc(ada_half, 1)
                dve.wait_ge(ada_half, turn * 4 + (a + 1))
                nc.vector.scalar_tensor_tensor(acc, w[:, D:2 * D], csilu[:, 2 * q + 1:2 * q + 2], acc, ALU.mult,
                                               ALU.add).then_inc(ada_used, 1)

            def mod_columns_add(first, layer, number):
                dve.wait_ge(mod_ps, number)
                at = COL["ada_b"] + 48 * layer + 8 * first
                to = 0 if first == 0 else 16
                link(nc.vector.tensor_tensor(modc[:, to:to + 16], ps[:, 6, 0:16], cols[:, at:at + 16], ALU.add))
                g = COL["mix_g" if first == 0 else "ffn_g"] + 8 * layer
                return to, g

            def mod_columns(first, layer, number):
                to, g = mod_columns_add(first, layer, number)
                nc.vector.tensor_copy(ps[0:1, 6, 0:1], modc[0:1, 0:1]).then_inc(mod_ready, 1)

            def set_xscale(first, layer):
                to = 0 if first == 0 else 16
                g = COL["mix_g" if first == 0 else "ffn_g"] + 8 * layer
                link(nc.vector.scalar_tensor_tensor(xscale[:, :], modc[:, to + 8:to + 16], 1.0, cols[:, g:g + 8],
                                                    ALU.add, ALU.mult))

            def mod_rows(gate, bias, number):
                for half in range(2):
                    dve.wait_ge(mod_ps, number + half)
                    cs = slice(half * 512, (half + 1) * 512)
                    nc.vector.tensor_tensor(gate[:, cs], ps[:, 6, :], bias[:, cs], ALU.add).then_inc(mod_ready, 1)

            roots = [0]

            def inverse_root(*parts):
                for out, sums, width in parts:
                    ins = nc.vector.tensor_scalar(out, sums, 1.0 / width, EPS, ALU.mult, ALU.add)
                roots[0] += 1
                ins.then_inc(root_in, 1)
                dve.wait_ge(root_out, roots[0])

            def normalise(t):
                dve.wait_ge(sq_ready, SQUARES[t])
                if t == 8:
                    inverse_root((rstd[:, 0:4], ss[:, 0:4], 512))
                    for b in range(NB):
                        for half in range(2):
                            cs = slice(half * 512, (half + 1) * 512)
                            ins = nc.vector.tensor_scalar(XN[:, b, cs], XN[:, b, cs],
                                                          rstd[:, 2 * b + half:2 * b + half + 1], None, ALU.mult)
                        ins.then_inc(xn_ready, 1)
                else:
                    inverse_root((rstd[:, 0:2], ss[:, 0:2], D))
                    for b in range(NB):
                        nc.vector.tensor_scalar(XN[:, b, :], X[:, b, :], rstd[:, b:b + 1], None,
                                                ALU.mult).then_inc(xn_ready, 1)

            def copy_xt(t):
                gain = {6: "f1_g", 7: "mp_g", 8: "out_g", 9: "f2_g"}.get(t)
                for j in range(4):
                    dve.wait_ge(xt_ps, 4 * t + j + 1)
                    if t in (1, 4):
                        nc.vector.tensor_copy(XT[:, 2 * j:2 * j + 2, :].rearrange("p k n -> p (k n)"), ps[:, j, :]).then_inc(xt_full, 1)
                        continue
                    for kt in (2 * j, 2 * j + 1):
                        src = ps[:, j, (kt % 2) * T:(kt % 2 + 1) * T]
                        if gain:
                            at = COL[gain] + kt
                            ins = nc.vector.tensor_scalar(XT[:, kt, :], src, cols[:, at:at + 1], None, ALU.mult)
                        else:
                            sh = (0 if t % 3 == 0 else 16) + kt
                            ins = nc.vector.tensor_scalar(XT[:, kt, :], src, xscale[:, kt:kt + 1], modc[:, sh:sh + 1],
                                                          ALU.mult, ALU.add)
                    ins.then_inc(xt_ready if t == 5 else xt_full, 1)
                if t == 5:
                    return
                for j in range(4):
                    dve.wait_ge(xt_hi, 4 * SPLIT_NO[t] + j + 1)
                    ks = slice(2 * j, 2 * j + 2)
                    nc.vector.tensor_tensor(XTL[:, ks, :], XT[:, ks, :], XTH[:, ks, :].bitcast(F32),
                                            ALU.subtract).then_inc(xt_ready, 1)

            def split_lo(chunk, half, turn=0):
                p = piece_no(chunk, half)
                dve.wait_ge(hi_ready, turn * (2 * RING) + (p + 1))
                nc.vector.tensor_tensor(WL[:, p % SPLITS, :], ring[:, chunk % RING, half * PIECE:(half + 1) * PIECE],
                                        WH[:, p % SPLITS, :].bitcast(F32), ALU.subtract).then_inc(lo_ready, 1)

            def ahead_lo(chunk):
                for half in range(2):
                    split_lo(chunk, half)

            def gemm_lo(g):
                for p in range(SPLITS, 4 * GEMM_GROUPS[g]):
                    split_lo(GEMM_CHUNK[g] + p // 2, p % 2)

            def add_gated(gate, s, count):
                for b in range(NB):
                    dve.wait_ge(s, count - 1 + b)
                    link(nc.vector.tensor_tensor(YB[:, b, :], YB[:, b, :], gate[:, :], ALU.mult))
                    nc.vector.tensor_tensor(X[:, b, :], X[:, b, :], YB[:, b, :], ALU.add).then_inc(x_ready, 1)

            def add_normed(row, number, factor):
                dve.wait_ge(res_sq, 2 * number)
                inverse_root((rstd[:, 4:6], ss[:, 4:6], D))
                for b in range(NB):
                    link(nc.vector.scalar_tensor_tensor(YB[:, b, :], YB[:, b, :], rstd[:, 4 + b:5 + b], row,
                                                        ALU.mult, ALU.mult))
                    nc.vector.scalar_tensor_tensor(X[:, b, :], YB[:, b, :], factor, X[:, b, :], ALU.mult,
                                                   ALU.add).then_inc(x_ready, 1)

            def ffn(i):
                h0, n0 = FF_STEPS * i, FFN_CHUNK[i]

                def h_both(k):
                    dve.wait_ge(silu_ready, k)
                    nc.vector.tensor_tensor(hbuf[:, :, :], sgt[:, :, :], ps[:, 4:6, FW:2 * FW], ALU.mult).then_inc(h_ready, 1)

                def hT_low(k):
                    dve.wait_ge(hT_hi, k)
                    nc.vector.tensor_tensor(hTL[:, :, :, :].rearrange("p b f n -> p b (f n)"), ps[:, 6:8, 0:2 * P],
                                            hTH[:, :, :, :].rearrange("p b f n -> p b (f n)").bitcast(F32),
                                            ALU.subtract).then_inc(hT_ready, 1)

                if i == 0:
                    ada_step(26)
                    ada_step(27)

                def step(n, turn, s):
                    k = turn * 2 + (h0 + 1 + s)
                    split_lo(n, 0, turn)
                    h_both(k)
                    split_lo(n, 1, turn)
                    if i == 0:
                        ada_step(28 + 2 * s, turn, turn + 1)
                    for half in range(2):
                        split_lo(n + 1, half, turn)
                    hT_low(k)
                    for half in range(2):
                        split_lo(n + 2, half, turn)
                        if i == 0 and half == 0:
                            ada_step(29 + 2 * s, turn, turn + 1)

                stream_turns(dve, FF_STEPS - 1, 3, n0 + 2, step)
                h_both(h0 + FF_STEPS)
                for half in range(2):
                    split_lo(n0 + FF_CHUNKS - 1, half)
                hT_low(h0 + FF_STEPS)

            def bias_table(u):
                at = 0 if u.b == 0 else 512
                if u.kind in "AC":
                    return alibi[:, at:at + 4 * u.nk].rearrange("p (s k) -> p s k", s=4)
                if u.kind == "D":
                    return band[:, at:at + 4 * u.nk].rearrange("p (s k) -> p s k", s=4)
                if u.kind == "B":
                    at = 0 if u.b == 0 else 128
                    return cmask[:, at:at + u.nk].unsqueeze(1).broadcast_to([P, 4, u.nk])
                return (na_bias if u.kind == "N" else dil_bias)[:, u.b, u.g.half]

            def bias(u):
                par = u.su % 2
                dve.wait_ge(scores, u.su + 1)
                if u.kind == "D" and u.layer == 1 and u.b == 0:
                    dve.wait_ge(layer_in, 16)
                src = ps[:, 2 * par:2 * par + 2, :].rearrange("p j (s k) -> p (j s) k", s=2)[:, :, 0:u.nk]
                scale = {"A": 32 ** -0.5, "B": 96 ** -0.5}.get(u.kind, HD ** -0.5)
                link(nc.vector.scalar_tensor_tensor(src, src, scale, bias_table(u), ALU.mult, ALU.add))
                if u.kind == "C":
                    link(nc.vector.tensor_tensor(src, src, SEL[u.b].unsqueeze(1).broadcast_to([P, 4, u.nk]), ALU.add))
                nc.vector.tensor_reduce(nmax[:, par, :], src, AX_X, ALU.max, negate=True).then_inc(biased, 1)

            def index_add(u):
                par, b, nk = u.su % 2, u.b, u.nk
                work = [PROJ[:, i, C_WORK:C_WORK + nk] for i in range(2)]
                dve.wait_ge(probs, u.su + 1)
                for h in range(4):
                    src = PR[:, par, head_slot(h), 0:nk]
                    at = 0 if b == 0 else 128
                    prev = cmask[:, at:at + nk] if u.part == 0 and h == 0 else work[0]
                    ins = nc.vector.scalar_tensor_tensor(work[0], src, w16[:, b, 4 * u.part + h:4 * u.part + h + 1], prev,
                                                         ALU.mult, ALU.add)
                    if h < 3:
                        link(ins)
                ins.then_inc(idx_added, 1)
                if u.part == 0:
                    dve.wait_ge(idx_added, u.idx + 1)
                    return
                dve.wait_ge(idx_added, u.idx + 1)
                for r in range(N_SEL // 8):
                    link(nc.vector.max(top8[:, :], work[r % 2]))
                    link(nc.vector.match_replace(work[1 - r % 2], top8[:, :], work[r % 2], TAKEN))
                link(nc.vector.tensor_scalar(SEL[b], work[0], TAKEN / 1.5, MASK, ALU.is_gt, ALU.mult))

            def finish(u):
                par = u.su % 2
                if u.kind == "I":
                    index_add(u)
                    return
                dve.wait_ge(probs, u.su + 1)
                done = [v.pu for v in UNITS[:max(u.su - 1, 0)] if v.pu is not None]
                if done:
                    dve.wait_ge(mixed, done[-1] + 1)
                link(nc.vector.reciprocal(rden[:, par, :], den[:, par, :]))
                if u.comb is None:
                    return
                link(nc.vector.tensor_scalar(rden[:, par, :], rden[:, par, :], lamc[:, 4 + u.layer:5 + u.layer], None, ALU.mult))
                for h in range(4):
                    s = head_slot(h)
                    p0 = PR[:, 1 - par, s, 0:u.nk]
                    ins = nc.vector.tensor_scalar(p0, p0, rden[:, 1 - par, h:h + 1], None, ALU.mult)
                link(ins)
                for h in range(4):
                    s = head_slot(h)
                    p0, p1 = PR[:, 1 - par, s, 0:u.nk], PR[:, par, s, 0:u.nk]
                    ins = nc.vector.scalar_tensor_tensor(p0, p1, rden[:, par, h:h + 1], p0, ALU.mult, ALU.add)
                ins.then_inc(combined, 1)

            def store(u):
                dve.wait_ge(o_ps, u.pu + 1)
                c = {"A": 0, "B": 256, "C": 512, "D": 768, "N": 0, "L": 512}[u.kind] + 256 * u.g.half
                dst = XN[:, u.b, c:c + 256].rearrange("p (h e) -> p h e", h=4)
                src = ps[:, 6, 0:256].rearrange("p (h e) -> p h e", h=4)
                if u.kind != "A":
                    nc.vector.tensor_tensor(dst, src, rden[:, u.su % 2, :].unsqueeze(2).broadcast_to([P, 4, HD]),
                                            ALU.mult).then_inc(mixed, 1)
                    return
                sq = FS[:, 1024:1280].rearrange("p (h e) -> p h e", h=4)
                link(nc.vector.tensor_copy(dst, src))
                link(nc.vector.tensor_tensor(sq, dst, dst, ALU.mult))
                link(nc.vector.tensor_reduce(rstd[:, 4:8], sq, AX_X, ALU.add))
                inverse_root((rstd[:, 4:8], rstd[:, 4:8], HD))
                link(nc.vector.tensor_tensor(dst, dst, rstd[:, 4:8].unsqueeze(2).broadcast_to([P, 4, HD]), ALU.mult))
                nc.vector.tensor_tensor(dst, dst, gdiff[:, u.layer, :].unsqueeze(1).broadcast_to([P, 4, HD]),
                                        ALU.mult).then_inc(mixed, 1)

            def rope(x, b):
                n = x.shape[1]
                cos = cossin[:, b, 0, :].unsqueeze(1).broadcast_to([P, n, 16])
                sin = cossin[:, b, 1, :].unsqueeze(1).broadcast_to([P, n, 16])
                x1, x2 = x[:, :, 0:16], x[:, :, 16:32]
                nc.vector.tensor_tensor(TR[:, 0, 0:n], x1, cos, ALU.mult)
                nc.vector.tensor_tensor(TR[:, 1, 0:n], x2, sin, ALU.mult)
                nc.vector.tensor_tensor(TR[:, 2, 0:n], x1, sin, ALU.mult)
                link(nc.vector.tensor_tensor(TR[:, 3, 0:n], x2, cos, ALU.mult))
                nc.vector.tensor_tensor(x1, TR[:, 0, 0:n], TR[:, 1, 0:n], ALU.subtract)
                link(nc.vector.tensor_tensor(x2, TR[:, 2, 0:n], TR[:, 3, 0:n], ALU.add))

            def prepare_rope(g):
                dve.wait_ge(filled, g.fill0 + 6)
                for b in range(NB):
                    q = PROJ[:, b, B_UQ:B_UQ + 384].rearrange("p (h n) -> p h n", h=4)
                    rope(q[:, :, 64:96], b)
                    rope(PROJ[:, b, B_KR:B_KR + 32].unsqueeze(1), b)
                    kv = PROJ[:, b, B_UKV:B_UKV + 512].rearrange("p (h n) -> p h n", h=4)
                    nc.vector.tensor_copy(KB[:, b, :, 0:64], kv[:, :, 0:64])
                    ins = nc.vector.tensor_copy(KB[:, b, :, 64:96],
                                                PROJ[:, b, B_KR:B_KR + 32].unsqueeze(1).broadcast_to([P, 4, 32]))
                ins.then_inc(b_roped, 1)

            def prepare(g):
                if g.kind == "B":
                    dve.wait_ge(b_sq, 4 * (g.layer + 1))
                    inverse_root((rstd[:, 0:2], ss[:, 0:2], 256), (rstd[:, 2:4], ss[:, 2:4], 128))
                    for i, (c, w) in enumerate(((B_QD, 256), (B_KVD, 128))):
                        for b in range(NB):
                            ins = nc.vector.tensor_scalar(PROJ[:, b, c:c + w], PROJ[:, b, c:c + w],
                                                          rstd[:, 2 * i + b:2 * i + b + 1], None, ALU.mult)
                    ins.then_inc(b_normed, 1)
                    if g.layer == 0:
                        for a in range(ADA_EARLY, ADA_EARLY + ADA_IN_B):
                            ada_step(a)
                if g.kind == "C":
                    dve.wait_ge(fill_ps, g.fill0)
                    nc.vector.memset(KI4, 0.0)
                    for b in range(NB):
                        nc.vector.tensor_scalar(w16[:, b, :], PROJ[:, b, C_WI:C_WI + 8], (8 * 32) ** -0.5, None, ALU.mult)
                        ins = nc.vector.tensor_copy(PROJ[:, b, C_KIREP:C_KIREP + P].rearrange("p (h n) -> p h n", h=4),
                                                    PROJ[:, b, C_KI:C_KI + 32].unsqueeze(1).broadcast_to([P, 4, 32]))
                    ins.then_inc(c_ready, 1)

            def attention(layer):
                us = units_of(layer)
                dve.wait_ge(gemm_out, 2 * sum(GEMM_GROUPS[:2 * layer + 1]))
                bias(us[0])
                for n, u in enumerate(us):
                    if u.first_of_group and u.g.gi + 1 < len(GROUPS) and GROUPS[u.g.gi + 1].layer == layer:
                        prepare(GROUPS[u.g.gi + 1])
                    if fill_part(u) and fill_part(u)[0].kind == "B" and fill_part(u)[1] == 6:
                        prepare_rope(GROUPS[u.g.gi + 1])
                    if n + 1 < len(us) and us[n + 1].kind != "I":
                        bias(us[n + 1])
                    finish(u)
                    if layer == 0 and ADA_EARLY + ADA_IN_B + n < ADA_MID:
                        ada_step(ADA_EARLY + ADA_IN_B + n)
                    if n >= 1 and us[n - 1].pu is not None:
                        store(us[n - 1])
                store(us[-1])

            def route():
                dve.wait_ge(late_in, 16 * 5)
                nc.vector.memset(r_logit, -3.0e38)
                nc.vector.memset(r_rank[:, :, 8:9], -1000.0)
                link(nc.vector.memset(r_take, -3.0e38))
                dve.wait_ge(route_ps, 1)
                link(nc.vector.tensor_copy(r_logit[:, :, 0:8], ps[:, 7, 0:16].rearrange("p (b n) -> p b n", b=NB)))
                for b in range(NB):
                    ins = nc.vector.max(r_top[:, b, :], r_logit[:, b, 0:8])
                link(ins)
                nc.vector.tensor_scalar(r_nv1, r_top[:, :, 0:1].rearrange("p b a -> p (b a)"), -1.0, None, ALU.mult).then_inc(route_max, 1)
                link(nc.vector.tensor_copy(r_take[:, :, 0:2], r_top[:, :, 0:2]))
                for b in range(NB):
                    ins = nc.vector.match_replace(r_marked[:, b, :], r_take[:, b, :], r_logit[:, b, :], 3.0e38)
                link(ins)
                nc.vector.tensor_scalar(r_sel, r_marked[:, :, 0:8], 1.0e38, None, ALU.is_ge).then_inc(route_sel, 1)
                dve.wait_ge(route_exp, 1)
                link(nc.vector.tensor_scalar(r_den, r_e2, 1.0, None, ALU.add))
                link(nc.vector.reciprocal(r_den, r_den))
                dve.wait_ge(route_sel, 1)
                link(nc.vector.tensor_tensor(r_comb, r_exp, r_sel, ALU.mult))
                link(nc.vector.tensor_tensor(r_comb, r_comb, r_den.unsqueeze(2).broadcast_to([P, NB, 8]), ALU.mult))
                dve.wait_ge(rank_ps, 1)
                link(nc.vector.scalar_tensor_tensor(r_rank[:, :, 0:8], ps[:, 7, 0:16].rearrange("p (b n) -> p b n", b=NB), 1000.0,
                                                    r_sel, ALU.add, ALU.mult))
                link(nc.vector.tensor_scalar(r_rank[:, :, 0:8], r_rank[:, :, 0:8], -1000.0, None, ALU.add))
                link(nc.vector.tensor_reduce(r_cnt[0:1, :], ps[0:1, 7, 16:24], AX_X, ALU.max))
                link(nc.vector.memset(YB, 0.0))
                nc.vector.tensor_scalar(flag[:, :], r_cnt[0:1, :], float(P), None, ALU.is_gt).then_inc(route_ready, 1)

            def experts(m):
                def lo(local, half, turn, e_pieces):
                    raw, slot = expert_piece(local, half)
                    dve.wait_ge(m["hi_ready"], turn * (2 * RING) + e_pieces + (m["first"] + 2 * local + half + 1))
                    nc.vector.tensor_tensor(WL[:, slot, :], raw, WH[:, slot, :].bitcast(F32),
                                            ALU.subtract).then_inc(m["lo_ready"], 1)

                def h_product(par, k):
                    dve.wait_ge(m["silu_ready"], k)
                    nc.vector.tensor_tensor(hbuf[:, par, :], sgt[:, par, :], ps[:, 4 + par, FW:2 * FW],
                                            ALU.mult).then_inc(m["h_ready"], 1)

                def hT_low(par, k):
                    dve.wait_ge(m["hT_hi"], k)
                    nc.vector.tensor_tensor(hTL[:, par].rearrange("p f n -> p (f n)"), ps[:, 6 + par, 0:2 * P],
                                            hTH[:, par].rearrange("p f n -> p (f n)").bitcast(F32),
                                            ALU.subtract).then_inc(m["hT_ready"], 1)

                def gathered_lo(number):
                    dve.wait_ge(m["xg_hi"], number)
                    nc.vector.tensor_tensor(XGL, XG, XGH.bitcast(F32), ALU.subtract).then_inc(m["xg_ready"], 1)

                def take_rank(column):
                    return nc.vector.tensor_scalar(r_rk, r_rank[:, :, column].rearrange("p b a -> p (b a)"),
                                                   -float(P) * m["sweep"], None, ALU.add)

                def select():
                    for b in range(NB):
                        ins = nc.vector.tensor_scalar(PSEL[:, b, :], iota, r_rk[:, b:b + 1], None, ALU.is_equal)
                    ins.then_inc(m["psel"], 1)

                def add_scattered(number):
                    for b in range(NB):
                        dve.wait_ge(m["sc_ps"], number + b)
                        nc.vector.tensor_tensor(YB[:, b, :], YB[:, b, :],
                                                ps[:, 2 - 2 * b:4 - 2 * b, :].rearrange("p j n -> p (j n)"),
                                                ALU.add).then_inc(m["sc_added"], 1)

                nc.vector.memset(CT, 0.0)
                take_rank(slice(0, 1)).then_inc(m["sel_copied"], 1)
                dve.wait_ge(m["sel_copied"], 1)
                select()
                gathered_lo(1)
                with dve.Fori(0, EXPERTS) as e:
                    e_pieces = e * (2 * EX_CHUNKS)
                    k_e = e * EX_STEPS
                    for pair in range(4):
                        lo(pair // 2, pair % 2, 0, e_pieces)
                    for pair in range(4):
                        lo(2 + pair // 2, pair % 2, 0, e_pieces)
                        if pair == 0:
                            h_product(0, k_e + 1)
                        if pair == 1:
                            add_scattered(e * 2 + 1)
                    hT_low(0, k_e + 1)
                    for half in range(2):
                        lo(4, half, 0, e_pieces)
                    dve.wait_ge(m["psel"], e + 1)
                    take_rank(bass.ds(e + 1, 1))
                    nc.vector.tensor_copy(r_cb, r_comb[:, :, bass.ds(e, 1)].rearrange("p b a -> p (b a)")).then_inc(m["sel_copied"], 1)
                    dve.wait_ge(m["sel_copied"], e + 2)
                    for b in range(NB):
                        ins = nc.vector.tensor_scalar(WSEL[:, b, :], PSEL[:, b, :], r_cb[:, b:b + 1], None, ALU.mult)
                    ins.then_inc(m["wsel"], 1)
                    dve.wait_ge(m["wsel"], e + 1)
                    select()
                    with dve.Fori(0, (EX_STEPS - 2) // 2) as t:
                        for par in range(2):
                            local = 5 + 3 * par
                            k = t * 2 + k_e + (2 + par)
                            for pair in range(4):
                                lo(local + pair // 2, pair % 2, t, e_pieces)
                                if pair == 0:
                                    h_product(1 - par, k)
                            hT_low(1 - par, k)
                            for half in range(2):
                                lo(local + 2, half, t, e_pieces)
                    for half in range(2):
                        lo(EX_CHUNKS - 1, half, 0, e_pieces)
                        if half == 0:
                            h_product(1, k_e + EX_STEPS)
                    hT_low(1, k_e + EX_STEPS)
                    gathered_lo(e + 2)
                add_scattered(2 * EXPERTS + 1)

            def lambdas():
                dve.wait_ge(const_in, 16 * N_CONST)
                v = lam_in.rearrange("p l (i a n) -> p l i a n", i=2, a=2)
                for l in range(LAYERS):
                    for i in range(2):
                        link(nc.vector.tensor_tensor(lam_pr[:, l, 32 * i:32 * (i + 1)], v[:, l, i, 0, :], v[:, l, i, 1, :], ALU.mult))
                nc.vector.tensor_reduce(lamc[:, 4:8], lam_pr[:, :, :].rearrange("p l (i n) -> p (l i) n", i=2), AX_X,
                                        ALU.add).then_inc(lam_exp_in, 1)
                dve.wait_ge(lam_exp_out, 1)
                for l in range(LAYERS):
                    lam_init = 0.8 - 0.6 * math.exp(-0.3 * l)
                    link(nc.vector.tensor_tensor(lamc[:, 4 + l:5 + l], lamc[:, 2 * l + 1:2 * l + 2], lamc[:, 2 * l:2 * l + 1],
                                                 ALU.subtract))
                    link(nc.vector.tensor_scalar(lamc[:, 4 + l:5 + l], lamc[:, 4 + l:5 + l], -lam_init, None, ALU.add))
                    link(nc.vector.tensor_scalar(gdiff[:, l, :], gdiff[:, l, :], 1.0 - lam_init, None, ALU.mult))

            nc.vector.memset(zero[:, :], 0.0).then_inc(zero_ready, 1)
            dve.wait_ge(csilu_ready, 1)
            for a in range(ADA_EARLY):
                ada_step(a)
            for layer in range(LAYERS):
                ahead_lo(GEMM_CHUNK[2 * layer])
                mod_columns(0, layer, 1 + 6 * layer)
                set_xscale(0, layer)
                normalise(3 * layer)
                copy_xt(3 * layer)
                ahead_lo(GEMM_CHUNK[2 * layer] + 1)
                gemm_lo(2 * layer)
                if layer == 0:
                    lambdas()
                attention(layer)
                if layer == 1:
                    dve.wait_ge(gates_in, 32)
                ahead_lo(GEMM_CHUNK[2 * layer + 1])
                copy_xt(3 * layer + 1)
                mod_rows(gate_mix, gate_mix, 6 * layer + 2)
                mod_columns(3, layer, 6 * layer + 4)
                mod_rows(gate_ffn, gate_ffn, 6 * layer + 5)
                ahead_lo(GEMM_CHUNK[2 * layer + 1] + 1)
                gemm_lo(2 * layer + 1)
                add_gated(gate_mix, gemm_out, 2 * sum(GEMM_GROUPS[:2 * layer + 2]))
                set_xscale(3, layer)
                if layer == 0:
                    ahead_lo(FFN_CHUNK[0])
                normalise(3 * layer + 2)
                copy_xt(3 * layer + 2)
                if layer == 0:
                    ahead_lo(FFN_CHUNK[0] + 1)
                    ffn(0)
                    add_gated(gate_ffn, y_out, 2)
                else:
                    route()
                    experts(moe_sems[0])
                    dve.wait_ge(route_ready, 1)
                    over = dve.value_load(flag[0:1, 0:1], min_val=0, max_val=1)
                    with dve.If(over > 0):
                        experts(moe_sems[1])
                        dve.wait_ge(moe_sems[1]["sc_added"], 2 * EXPERTS + 2)
                    add_gated(gate_ffn, moe_sems[0]["sc_added"], 2 * EXPERTS + 2)
            dve.wait_ge(res_sq, 2)
            dve.wait_ge(rows_in, 32)
            inverse_root((rstd[:, 4:6], ss[:, 4:6], D))
            for b in range(NB):
                nc.vector.scalar_tensor_tensor(X[:, b, :], X[:, b, :], rstd[:, 4 + b:5 + b], final_g, ALU.mult,
                                               ALU.mult).then_inc(x_ready, 1)
            ahead_lo(FFN_CHUNK[1])
            normalise(6)
            copy_xt(6)
            ahead_lo(FFN_CHUNK[1] + 1)
            for b in range(NB):
                for g in range(2):
                    link(nc.vector.tensor_tensor(dil_bias[:, b, g], dil_bias[:, b, g],
                                                 lnm[:, b, :].unsqueeze(1).broadcast_to([P, 4, T]), ALU.add))
            ffn(1)
            add_normed(f1_post_g, 2, 0.5)
            ahead_lo(GEMM_CHUNK[4])
            normalise(7)
            copy_xt(7)
            ahead_lo(GEMM_CHUNK[4] + 1)
            gemm_lo(4)
            attention(2)
            normalise(8)
            ahead_lo(GEMM_CHUNK[5])
            copy_xt(8)
            ahead_lo(GEMM_CHUNK[5] + 1)
            gemm_lo(5)
            dve.wait_ge(rows_in2, 32)
            add_normed(gate_mix[:, :], 3, 1.0)
            ahead_lo(FFN_CHUNK[2])
            normalise(9)
            copy_xt(9)
            ahead_lo(FFN_CHUNK[2] + 1)
            ffn(2)
            add_normed(gate_ffn[:, :], 4, 0.5)



def product_chunks(w, groups):
    w = np.pad(w, ((0, 0), (0, groups * 512 - w.shape[1])))
    return w.reshape(2, 4, P, groups, 512).transpose(3, 0, 2, 1, 4).reshape(2 * groups, P, CHW)


def ffn_chunks(w1, w3, w2):
    steps = w1.shape[1] // FW
    up = np.stack([w1.reshape(2, 4, P, steps, FW), w3.reshape(2, 4, P, steps, FW)], axis=4)
    up = up.transpose(3, 0, 2, 1, 4, 5).reshape(steps, 2, P, CHW)
    down = w2.reshape(steps, 2, P, D).transpose(0, 2, 1, 3).reshape(steps, 1, P, CHW)
    out = np.empty((3 * steps, P, CHW), np.float32)
    out[0:2] = up[0]
    mid = out[2:-1].reshape(steps - 1, 3, P, CHW)
    mid[:, 0:2] = up[1:]
    mid[:, 2:3] = down[:-1]
    out[-1] = down[-1, 0]
    return out


def columns(v):
    return v.reshape(-1, P).T


def slotted(table):
    order = [h for s in range(4) for h in range(4) if head_slot(h) == s]
    t = table.reshape(-1, 4, NB, P, T)[:, order]
    return t.transpose(3, 2, 0, 1, 4)


def causal_pack(t):
    return np.concatenate([t[:, 0, 0, :, 0:P].reshape(P, -1), t[:, 1, 0].reshape(P, -1)], axis=1)


def arrays_of(i):
    i = {k: np.asarray(v) for k, v in i.items()}
    q, k = np.arange(T)[:, None], np.arange(T)[None, :]
    allowed = k // 64 <= q // 64
    slopes = (2.0 ** (-8.0 * np.arange(1, 5) / 4)).astype(np.float32)
    alibi = np.where(allowed, -slopes[:, None, None] * np.abs(q - k).astype(np.float32), np.float32(MASK)).astype(np.float32)
    cmask = np.where(allowed, np.float32(0), np.float32(MASK)).astype(np.float32)
    cm = cmask.reshape(NB, P, T)
    rel = np.clip(q - k, -128, 128) + 128
    band = np.stack([causal_pack(slotted(np.where(allowed, i["band_rel_bias"][l][:, rel], np.float32(MASK)))) for l in range(LAYERS)])
    qr, qc, kr, kc = q // 64, q % 64, k // 64, k % 64
    start = np.clip(qc - 8, 0, 48)
    near = (kc >= start) & (kc < start + 16)
    na = np.where(near, i["na_rel_bias_2"][0][:, kr - qr + 7, np.clip(kc - qc + 15, 0, 30)], np.float32(MASK))
    off = k - q
    member = [np.abs(off) <= 64, off % 4 == 0, off % 16 == 0]
    times = sum(m.astype(np.int64) for m in member)
    dist = np.abs(off)
    large = 8 + (np.log(np.maximum(dist, 1).astype(np.float32) / 8) / math.log(1024 / 8) * 8).astype(np.int32)
    bucket = np.where(off > 0, 16, 0) + np.where(dist < 8, dist, np.minimum(large, 15))
    dil = np.where(times > 0, i["t5_rel_bias_2"][:, bucket], np.float32(MASK))
    lnm = np.log(np.maximum(times, 1)).astype(np.float32).reshape(NB, P, T).transpose(1, 0, 2).reshape(P, NB * T)
    inv = np.float32(10000.0) ** (-np.arange(0, 32, 2, dtype=np.float32) / np.float32(32))
    ang = np.arange(T, dtype=np.float32)[:, None] * inv[None, :]
    cossin = np.stack([np.cos(ang), np.sin(ang)], axis=1).reshape(NB, P, 2, 16).transpose(1, 0, 2, 3).reshape(P, 64)
    ada_b = i["ada_b"].reshape(LAYERS, 6, D)
    stream = np.concatenate([
        product_chunks(i["w_in"][0], 6), product_chunks(i["w_out"][0], 2),
        ffn_chunks(i["ffn_w1"][0], i["ffn_w3"][0], i["ffn_w2"][0]),
        product_chunks(i["w_in"][1], 6), product_chunks(i["w_out"][1], 2),
        *[ffn_chunks(i["moe_w1"][0, e], i["moe_w3"][0, e], i["moe_w2"][0, e]) for e in range(EXPERTS)],
        ffn_chunks(i["ffn1_w_gate_2"][0], i["ffn1_w_up_2"][0], i["ffn1_w_down_2"][0]),
        product_chunks(i["w_qkv_2"][0], 6), product_chunks(i["w_out_2"][0], 2),
        ffn_chunks(i["ffn2_w_gate_2"][0], i["ffn2_w_up_2"][0], i["ffn2_w_down_2"][0])])
    ada = i["ada_w"].reshape(LAYERS, 4, 2, P, 6, D).transpose(0, 4, 1, 3, 2, 5).reshape(ADA_CHUNKS, P, CHW)
    cols = np.concatenate([columns(v) for v in (
        i["mix_norm_g"], i["ffn_norm_g"], i["ffn1_pre_g_2"], i["mix_pre_g_2"], i["ffn2_pre_g_2"],
        np.concatenate([i["na_out_g_2"][0], i["dil_out_g_2"][0]]), ada_b, i["mla_q_norm_g"], i["mla_kv_norm_g"], i["c"])], axis=1)
    rows = np.stack([ada_b[0, 2], ada_b[0, 5], ada_b[1, 2], ada_b[1, 5], i["final_norm_g"], i["ffn1_post_g_2"][0],
                     i["mix_post_g_2"][0], i["ffn2_post_g_2"][0]])
    tri = (np.arange(P)[:, None] < np.arange(P)[None, :]).astype(np.float32)
    iota = np.broadcast_to(np.arange(P, dtype=np.float32), (P, P))
    out = dict(
        x=i["x"], stream=stream, ada=ada, cols=cols, rows=rows,
        lam=i["diff_lambda"].reshape(1, 256), gdiff=i["diff_norm_g"].reshape(1, 128),
        unit=np.concatenate([np.eye(P), np.ones((P, P))], axis=1), cossin=cossin,
        alibi=causal_pack(slotted(alibi)), cmask=np.concatenate([cm[0, :, 0:P], cm[1]], axis=1), band=band,
        uq=i["mla_w_uq"].reshape(LAYERS, 2, P, 384).transpose(0, 2, 1, 3).reshape(LAYERS, P, 768), ukv=i["mla_w_ukv"],
        na=slotted(na).reshape(P, -1), dil=slotted(dil).reshape(P, -1), lnm=lnm,
        tri_iota=np.concatenate([tri, iota], axis=1),
        router=i["moe_router"][0].reshape(KT, P, 8).transpose(1, 0, 2).reshape(P, 64))
    return {n: np.ascontiguousarray(a, dtype=np.float32) for n, a in out.items()}


def kernel(**inputs):
    import concourse.bacc as bacc
    from concourse.bass_utils import run_bass_kernel_spmd

    nc = bacc.Bacc("TRN2", target_bir_lowering=False, num_devices=1)
    arrays = {f"in_{n}": a for n, a in arrays_of(inputs).items()}
    aps = {n[3:]: nc.dram_tensor(n, a.shape, F32, kind="ExternalInput").ap() for n, a in arrays.items()}
    aps["out"] = nc.dram_tensor("out", (1, T, D), F32, kind="ExternalOutput").ap()
    program(nc, aps)
    r = run_bass_kernel_spmd(nc, [arrays], core_ids=[0])
    return r.results[0]["out"]
```
